# Optimizing a Trainium2 kernel written in Bass

```python
import math
import jax, jax.numpy as jnp
from jax import lax
import numpy as np

D_MODEL = 2048
BATCH = 1
SEQ = 256
DEPTH = 2

PLE_DIM = 256
D_A = D_MODEL // 2
A_GROUPS = 8
CONV_A_WIDTH = 31
D_B = D_MODEL // 2
RG_HEADS = 8
RG_HEAD_DIM = D_B // RG_HEADS
CONV_B_WIDTH = 4
RG_C = 8.0
SB_HEADS = 16
SB_HEAD_DIM = D_MODEL // SB_HEADS
BLOCK_Q = 128
D_FF = 4 * D_MODEL
N_EVEN = (DEPTH + 1) // 2
N_ODD = DEPTH // 2
EPS = 1e-6
D_IN_REC = 2 * D_A + 2 * D_B

kernel_name = "hybrid_conformer_rglru_stickbreaking_trunk"

def rms_norm(x, g):
    xf = x.astype(jnp.float32)
    y = xf * lax.rsqrt(jnp.mean(xf * xf, axis=-1, keepdims=True) + EPS)
    return (y * g.astype(jnp.float32)).astype(x.dtype)

def layer_norm(x, g, b):
    xf = x.astype(jnp.float32)
    mu = jnp.mean(xf, axis=-1, keepdims=True)
    var = jnp.mean(jnp.square(xf - mu), axis=-1, keepdims=True)
    y = (xf - mu) * lax.rsqrt(var + EPS)
    return (y * g.astype(jnp.float32) + b.astype(jnp.float32)).astype(x.dtype)

def causal_depthwise_conv(x, w, b):
    k_width = w.shape[0]
    out = lax.conv_general_dilated(
        x, w[:, None, :].astype(x.dtype), window_strides=(1,), padding=[(k_width - 1, 0)],
        dimension_numbers=("NWC", "WIO", "NWC"), feature_group_count=x.shape[-1])
    return out + b

def rg_lru(x, w_a, b_a, w_x, b_x, lam):
    bsz, seq, ch = x.shape
    xh = x.reshape(bsz, seq, RG_HEADS, RG_HEAD_DIM)
    r = jax.nn.sigmoid(jnp.einsum("bshi,hij->bshj", xh, w_a).reshape(bsz, seq, ch) + b_a)
    i = jax.nn.sigmoid(jnp.einsum("bshi,hij->bshj", xh, w_x).reshape(bsz, seq, ch) + b_x)
    log_a = -RG_C * r.astype(jnp.float32) * jax.nn.softplus(-lam.astype(jnp.float32))
    a = jnp.exp(log_a)
    mult = jnp.sqrt(-jnp.expm1(2.0 * log_a))
    u = mult * (i * x).astype(jnp.float32)

    def combine(c1, c2):
        a1, u1 = c1
        a2, u2 = c2
        return a1 * a2, a2 * u1 + u2

    _, h = lax.associative_scan(combine, (a, u), axis=1)
    return h.astype(x.dtype)

def conv_recurrent_mixer(hn, w_in, conv_a_w, conv_a_b, ln_a_g, ln_a_b,
                         conv_b_w, conv_b_b, w_rg_a, b_rg_a, w_rg_x, b_rg_x, rg_lambda, w_out):
    u = hn @ w_in
    a_val, a_gate, xr, gr = jnp.split(u, [D_A, 2 * D_A, 2 * D_A + D_B], axis=-1)
    ya = a_val * jax.nn.sigmoid(a_gate)
    ya = causal_depthwise_conv(ya, conv_a_w, conv_a_b)
    ya = jax.nn.silu(layer_norm(ya, ln_a_g, ln_a_b))
    xr = causal_depthwise_conv(xr, conv_b_w, conv_b_b)
    yb = rg_lru(xr, w_rg_a, b_rg_a, w_rg_x, b_rg_x, rg_lambda) * jax.nn.gelu(gr)
    return jnp.concatenate([ya, yb], axis=-1) @ w_out

def stick_breaking_attention(q, k, v):
    bsz, nh, seq, dh = q.shape
    n_blocks = seq // BLOCK_Q
    scale = 1.0 / math.sqrt(dh)
    q_blocks = q.reshape(bsz, nh, n_blocks, BLOCK_Q, dh).transpose(2, 0, 1, 3, 4)
    key_pos = jnp.arange(seq)

    def one_block(args):
        q_blk, blk_idx = args
        z = jnp.einsum("bhqd,bhkd->bhqk", q_blk, k,
                       preferred_element_type=jnp.float32) * scale
        q_pos = blk_idx * BLOCK_Q + jnp.arange(BLOCK_Q)
        mask = key_pos[None, :] < q_pos[:, None]
        log_one_minus = jnp.where(mask, -jax.nn.softplus(z), 0.0)
        key_axis = log_one_minus.ndim - 1
        tail = lax.cumsum(log_one_minus, axis=key_axis, reverse=True) - log_one_minus
        log_w = jax.nn.log_sigmoid(z) + tail
        w = jnp.where(mask, jnp.exp(log_w), 0.0)
        return jnp.einsum("bhqk,bhkd->bhqd", w.astype(v.dtype), v)

    out = lax.map(one_block, (q_blocks, jnp.arange(n_blocks)))
    return out.transpose(1, 2, 0, 3, 4).reshape(bsz, nh, seq, dh)

def stick_breaking_mixer(hn, w_qkv, w_o):
    bsz, seq, _ = hn.shape
    qkv = hn @ w_qkv
    q, k, v = jnp.split(qkv, 3, axis=-1)
    to_heads = lambda t: t.reshape(bsz, seq, SB_HEADS, SB_HEAD_DIM).transpose(0, 2, 1, 3)
    o = stick_breaking_attention(to_heads(q), to_heads(k), to_heads(v))
    o = o.transpose(0, 2, 1, 3).reshape(bsz, seq, D_MODEL)
    return o @ w_o

def squared_relu_mlp(hn, w_up, w_down):
    return jnp.square(jax.nn.relu(hn @ w_up)) @ w_down

def setup_inputs(seed: int = 0) -> dict:
    key = jax.random.key(seed)
    ks = jax.random.split(key, 32)
    f32 = jnp.float32
    nrm = lambda k, shape, fan_in: jax.random.normal(k, shape, f32) * (fan_in ** -0.5)
    gain = lambda k, shape: 1.0 + 0.05 * jax.random.normal(k, shape, f32)
    small = lambda k, shape: 0.02 * jax.random.normal(k, shape, f32)
    a_c = jax.random.uniform(ks[16], (N_EVEN, D_B), f32, 0.9, 0.999)
    a0 = a_c ** (1.0 / RG_C)
    rg_lambda = jnp.log(a0) - jnp.log1p(-a0)
    return {
        "x": jax.random.normal(ks[0], (BATCH, SEQ, D_MODEL), f32),
        "p": jax.random.normal(ks[1], (DEPTH, BATCH, SEQ, PLE_DIM), f32),
        "norm_mix_g": gain(ks[2], (DEPTH, D_MODEL)),
        "norm_mlp_g": gain(ks[3], (DEPTH, D_MODEL)),
        "norm_ple_g": gain(ks[4], (DEPTH, D_MODEL)),
        "norm_f_g": gain(ks[5], (D_MODEL,)),
        "w_in_rec": nrm(ks[6], (N_EVEN, D_MODEL, D_IN_REC), D_MODEL),
        "conv_a_w": nrm(ks[7], (N_EVEN, CONV_A_WIDTH, D_A), CONV_A_WIDTH),
        "conv_a_b": small(ks[8], (N_EVEN, D_A)),
        "ln_a_g": gain(ks[9], (N_EVEN, D_A)),
        "ln_a_b": small(ks[10], (N_EVEN, D_A)),
        "conv_b_w": nrm(ks[11], (N_EVEN, CONV_B_WIDTH, D_B), CONV_B_WIDTH),
        "conv_b_b": small(ks[12], (N_EVEN, D_B)),
        "w_rg_a": nrm(ks[13], (N_EVEN, RG_HEADS, RG_HEAD_DIM, RG_HEAD_DIM), RG_HEAD_DIM),
        "b_rg_a": small(ks[14], (N_EVEN, D_B)),
        "w_rg_x": nrm(ks[15], (N_EVEN, RG_HEADS, RG_HEAD_DIM, RG_HEAD_DIM), RG_HEAD_DIM),
        "b_rg_x": small(ks[17], (N_EVEN, D_B)),
        "rg_lambda": rg_lambda,
        "w_out_rec": nrm(ks[18], (N_EVEN, D_A + D_B, D_MODEL), D_A + D_B),
        "w_qkv": nrm(ks[19], (N_ODD, D_MODEL, 3 * D_MODEL), D_MODEL),
        "w_o_attn": nrm(ks[20], (N_ODD, D_MODEL, D_MODEL), D_MODEL),
        "w_mlp_up": nrm(ks[21], (DEPTH, D_MODEL, D_FF), D_MODEL),
        "w_mlp_down": nrm(ks[22], (DEPTH, D_FF, D_MODEL), D_FF),
        "w_ple_proj": nrm(ks[23], (DEPTH, PLE_DIM, D_MODEL), PLE_DIM),
        "w_ple_gate": nrm(ks[24], (DEPTH, D_MODEL, D_MODEL), D_MODEL),
    }

def reference(x, p, norm_mix_g, norm_mlp_g, norm_ple_g, norm_f_g, w_in_rec, conv_a_w, conv_a_b,
              ln_a_g, ln_a_b, conv_b_w, conv_b_b, w_rg_a, b_rg_a, w_rg_x, b_rg_x, rg_lambda,
              w_out_rec, w_qkv, w_o_attn, w_mlp_up, w_mlp_down, w_ple_proj, w_ple_gate):
    h = x
    for i in range(DEPTH):
        j = i // 2
        hn = rms_norm(h, norm_mix_g[i])
        if i % 2 == 0:
            mix = conv_recurrent_mixer(hn, w_in_rec[j], conv_a_w[j], conv_a_b[j], ln_a_g[j], ln_a_b[j],
                                       conv_b_w[j], conv_b_b[j], w_rg_a[j], b_rg_a[j], w_rg_x[j],
                                       b_rg_x[j], rg_lambda[j], w_out_rec[j])
        else:
            mix = stick_breaking_mixer(hn, w_qkv[j], w_o_attn[j])
        h = h + mix
        h = h + squared_relu_mlp(rms_norm(h, norm_mlp_g[i]), w_mlp_up[i], w_mlp_down[i])
        gate = jax.nn.sigmoid(rms_norm(h, norm_ple_g[i]) @ w_ple_gate[i])
        h = h + (p[i] @ w_ple_proj[i]) * gate
    return rms_norm(h, norm_f_g)


_drawn_inputs = setup_inputs


def setup_inputs(seed=0):
    import zlib

    import numpy as np

    out = dict(_drawn_inputs(seed))
    spreads = {}
    factors = {'norm_ple_g': 7.326, 'conv_a_b': 3.157, 'ln_a_b': 6.832, 'b_rg_a': 52.824, 'b_rg_x': 29.04}
    for name, (base, spread) in spreads.items():
        noise = np.random.default_rng([zlib.crc32(name.encode()), seed]).standard_normal(out[name].shape)
        drawn = base * np.exp(spread * noise) if base else spread * noise
        out[name] = __import__('jax').numpy.asarray(drawn.astype(out[name].dtype))
    for name, factor in factors.items():
        out[name] = (out[name] * factor).astype(out[name].dtype)
    return out
```

```python
from contextlib import ExitStack

import concourse.bass as bass
from concourse import mybir

P = 128
D = 2048
T = 256
FF = 4 * D
PLE = 256
DA = D // 2
DB = D // 2
CA = 31
CB = 4
DH = 128
NT = D // P
NG = D // T
CHUNK = 1024
NRAW = 4
NSPL = 8
EPS = 1e-6
PAD_A = CA - 1
PAD_B = CB - 1

ALU = mybir.AluOpType
ACT = mybir.ActivationFunctionType
F32 = mybir.dt.float32
F32R = mybir.dt.float32r
AX_X = mybir.AxisListType.X

G_GLU, C_GLU = 0, 0
G_REC, C_REC = 8, 32
C_RG = 64
G_PLE0, C_PLE0 = 16, 66
G_OUT0, C_OUT0 = 24, 71
G_MLP0, C_MLP0 = 32, 103
G_GATE0, C_GATE0 = 96, 359
G_QKV, C_QKV = 104, 391
G_PLE1, C_PLE1 = 128, 487
G_OUT1, C_OUT1 = 136, 492
G_MLP1, C_MLP1 = 144, 524
G_GATE1, C_GATE1 = 208, 780
CHUNKS = 812

GAIN = 0
CONV_A_W = GAIN + 7 * NT
CONV_A_B = CONV_A_W + 8 * CA
LN_G = CONV_A_B + 8
LN_B = LN_G + 8
CONV_B_W = LN_B + 8
CONV_B_B = CONV_B_W + 8 * CB
RG_BA = CONV_B_B + 8
RG_BX = RG_BA + 8
LAMBDA = RG_BX + 8
NPAR = LAMBDA + 8


def trunk(nc, xT, pT, par, w_in, w_rg_a, w_rg_x, w_out, w_qkv, w_o, w_up, w_down, w_proj, w_gate, outT):
    with ExitStack() as ctx:
        def sb(name, shape, dt=F32):
            return ctx.enter_context(nc.sbuf_tensor(name, shape, dt))

        def sem(name):
            return ctx.enter_context(nc.semaphore(name))

        raw = sb("raw", [P, NRAW, 4, 256])
        spl = sb("spl", [P, NSPL, 4, 2, 256], F32R)
        h = sb("h", [P, NT, T])
        cross = sb("cross", [P, 2, T])
        tv = sb("tv", [P, 2, T])
        nacc = sb("nacc", [P, T])
        rB = sb("rB", [P, T])
        rC = sb("rC", [P, 2])
        params = sb("params", [P, NPAR])
        lamc = sb("lamc", [P, 8])
        nlamc = sb("nlamc", [P, 8])
        small = sb("small", [P, 4, 8])
        onesD = sb("onesD", [P, P])
        onesA = sb("onesA", [P, P])
        epsb = sb("epsb", [P, 1])
        ngtri = sb("ngtri", [P, P], F32R)
        ngone = sb("ngone", [P, P], F32R)
        mask = sb("mask", [P, P])
        with nc.sbuf_tensor("rg", [P, 8, 2, T], F32) as rg, nc.sbuf_tensor("dec", [P, 8, T], F32) as dec, \
                nc.sbuf_tensor("mlt", [P, 8, T], F32) as mlt:
            pass
        XA = sb("XA", [P, NT, 2, T], F32R)
        with nc.sbuf_tensor("glu", [P, 8, PAD_A + T], F32) as glu, \
                nc.sbuf_tensor("xrp", [P, 2, PAD_B + T], F32) as xrp:
            pass
        XB = sb("XB", [P, NT, 2, T], F32R)
        with nc.sbuf_tensor("qk0", [P, 2, 2, 2, T], F32R) as qk0, nc.sbuf_tensor("v0", [P, 2, 2, T], F32R) as v0, \
                nc.sbuf_tensor("te", [P, 2, 384], F32) as te:
            pass
        pp = sb("pp", [P, NT, T])
        with nc.sbuf_tensor("y", [P, 8, T], F32) as y:
            pass
        qk1 = sb("qk1", [P, 2, 2, 2, T], F32R)
        v1 = sb("v1", [P, 2, 2, T], F32R)
        tl = sb("tl", [P, 2, 384])
        ws = sb("ws", [P, 2, 2, 384], F32R)
        qk, vv = (qk0, qk1), (v0, v1)

        ps = ctx.enter_context(nc.psum_tensor("ps", [P, 4, 512], F32))
        Z = ctx.enter_context(nc.psum_tensor("Z", [P, 2, 512], F32))
        O = ctx.enter_context(nc.psum_tensor("O", [P, 2, 512], F32))

        raw_landed = [sem(f"raw_landed{i}") for i in range(NRAW)]
        hi_ready = sem("hi_ready")
        lo_ready = sem("lo_ready")
        chunk_used = sem("chunk_used")
        par_landed = sem("par_landed")
        x_landed = [sem(f"x_landed{i}") for i in range(4)]
        consts_ready = sem("consts_ready")
        cross_copied = sem("cross_copied")
        sum_ready = sem("sum_ready")
        res_ready = sem("res_ready")
        sq_ready = sem("sq_ready")
        res_hi = sem("res_hi")
        sq_folded = sem("sq_folded")
        res_tiles = sem("res_tiles")
        nacc_clear = sem("nacc_clear")
        stat_ready = sem("stat_ready")
        root_ready = sem("root_ready")
        rstd_ready = sem("rstd_ready")
        up_relu = sem("up_relu")
        up_sq = sem("up_sq")
        up_hi = sem("up_hi")
        up_tiles = sem("up_tiles")
        gate_scaled = sem("gate_scaled")
        gate_sig = sem("gate_sig")
        gate_mul = sem("gate_mul")
        glu_scaled = sem("glu_scaled")
        glu_sig = sem("glu_sig")
        glu_val = sem("glu_val")
        glu_ready = sem("glu_ready")
        conv_step = sem("conv_step")
        xr_step = sem("xr_step")
        xr_hi = sem("xr_hi")
        xr_tiles = sem("xr_tiles")
        gr_scaled = sem("gr_scaled")
        gr_ready = sem("gr_ready")
        rg_done = sem("rg_done")
        rg_cross = sem("rg_cross")
        rg_sum = sem("rg_sum")
        rg_act = sem("rg_act")
        rg_vec = sem("rg_vec")
        ln_part = sem("ln_part")
        ln_stat = sem("ln_stat")
        ln_act = sem("ln_act")
        ln_vec = sem("ln_vec")
        qk_scaled = sem("qk_scaled")
        qk_hi = sem("qk_hi")
        qk_split = sem("qk_split")
        z_ready = sem("z_ready")
        z_abs = sem("z_abs")
        z_exp = sem("z_exp")
        z_log = sem("z_log")
        soft_raw = sem("soft_raw")
        soft_ready = sem("soft_ready")
        soft_hi = sem("soft_hi")
        soft_split = sem("soft_split")
        logw_ready = sem("logw_ready")
        logw_cut = sem("logw_cut")
        w_exp = sem("w_exp")
        w_ready = sem("w_ready")
        w_hi = sem("w_hi")
        w_split = sem("w_split")
        o_ready = sem("o_ready")
        o_hi = sem("o_hi")
        att_tiles = sem("att_tiles")
        out_scaled = sem("out_scaled")
        out_ready = sem("out_ready")
        stored = sem("stored")
        ple_done = sem("ple_done")
        yb_tiles = sem("yb_tiles")
        ya_tiles = sem("ya_tiles")
        lam_abs = sem("lam_abs")
        lam_exp = sem("lam_exp")
        lam_chain = sem("lam_chain")

        def counts(base, turns):
            return base > 0 or not isinstance(turns, int)

        def bcast(ap, n):
            return ap.unsqueeze(1).broadcast_to([P, n, ap.shape[-1]])

        def par_col(c):
            return params[:, bass.ds(c, 1)]

        def gain(n, t):
            return par_col(t + (GAIN + n * NT))

        block = ctx.enter_context(nc.Block())

        @block.sync
        def _(sp):
            def load(m, it, src):
                if counts(m - NRAW + 1, it):
                    sp.wait_ge(lo_ready, it * 8 + (m - NRAW + 1))
                sp.dma_start(raw[:, m % NRAW, :, :], src).then_inc(raw_landed[m % NRAW], 16)

            def load_group(m, it, w, col, rows=(0, 4, 8, 12), row0=0):
                for j, r in enumerate(rows):
                    src = w[bass.ds(row0 + r * P, 4 * P), bass.ds(col, 256)]
                    load(m + j, it, src.rearrange("(t p) n -> p t n", p=P))

            def load_ple(m, layer):
                load(m, 0, pT.rearrange("l (t p) n -> p (l t) n", p=P))
                for j in range(4):
                    src = w_proj[layer, :, 512 * j:512 * j + 512]
                    load(m + 1 + j, 0, src.rearrange("(t p) n -> p t n", p=P))

            def mlp(layer, m):
                with sp.Fori(0, 4) as f:
                    with sp.Fori(0, 4) as i:
                        for s in range(2):
                            load_group(m + 4 * s, f * 8 + i, w_up[layer], f * D + i * 512 + 256 * s)
                    with sp.Fori(0, 4) as i:
                        for s in range(2):
                            load_group(m + 32 + 4 * s, f * 8 + i, w_down[layer], i * 512 + 256 * s, row0=f * D)

            def square(m, w, rows=(0, 4, 8, 12), first=0):
                with sp.Fori(first, first + 4) as i:
                    for s in range(2):
                        load_group(m + 4 * s - 8 * first, i, w, i * 512 + (256 * s - 512 * first), rows)

            sp.dma_start(params[:, :], par).then_inc(par_landed, 16)
            sp.dma_start(h[:, 0:4, :], xT[0:4 * P, :].rearrange("(t p) n -> p t n", p=P)).then_inc(x_landed[0], 16)
            for j in range(4):
                load(j, 0, w_in[0, j * 4 * P:(j + 1) * 4 * P, 0:256].rearrange("(t p) n -> p t n", p=P))
                if j < 3:
                    k = j + 1
                    sp.dma_start(h[:, 4 * k:4 * k + 4, :], xT[4 * k * P:(4 * k + 4) * P, :].rearrange(
                        "(t p) n -> p t n", p=P)).then_inc(x_landed[k], 16)
            load_group(4, 0, w_in[0], DA)
            with sp.Fori(1, 4) as i:
                load_group(C_GLU, i, w_in[0], i * 256)
                load_group(C_GLU + 4, i, w_in[0], i * 256 + DA)
            with sp.Fori(0, 4) as i:
                load_group(C_REC, i, w_in[0], i * 256 + 2 * DA)
                load_group(C_REC + 4, i, w_in[0], i * 256 + 2 * DA + DB)
            for j, w in enumerate((w_rg_a, w_rg_x)):
                m = C_RG + j
                sp.wait_ge(lo_ready, m - NRAW + 1)
                dst = raw[:, m % NRAW, :, :].rearrange("p a (b n) -> p (a b) n", b=2)
                sp.dma_start(dst, w[0].rearrange("h i j -> i h j")).then_inc(raw_landed[m % NRAW], 16)
            load_ple(C_PLE0, 0)
            square(C_OUT0, w_out[0], (8, 12, 0, 4), first=1)
            mlp(0, C_MLP0)
            square(C_GATE0, w_gate[0])
            with sp.Fori(0, 4) as i:
                for s in range(2):
                    for part in range(3):
                        load_group(C_QKV + 12 * s + 4 * part, i * 3, w_qkv[0], i * 512 + (part * D + 256 * s))
            load_ple(C_PLE1, 1)
            square(C_OUT1, w_o[0])
            mlp(1, C_MLP1)
            square(C_GATE1, w_gate[1])
            for q in range(4):
                sp.wait_ge(out_ready, q + 1)
                sp.dma_start(outT[4 * q * P:(4 * q + 4) * P, :].rearrange("(t p) n -> p t n", p=P),
                             h[:, 4 * q:4 * q + 4, :]).then_inc(stored, 16)
            sp.wait_ge(stored, 64)

        @block.gpsimd
        def _(pool):
            pool.memset(onesD[:, :], 1.0 / D)
            pool.memset(onesA[:, :], 1.0 / DA)
            pool.memset(epsb[:, :], EPS)
            pool.memset(glu[:, :, 0:PAD_A], 0.0)
            pool.memset(xrp[:, :, 0:PAD_B], 0.0)
            pool.memset(tl[:, 0, 0:P], -1.0)
            pool.memset(tl[:, 1, 0:P], 1.0).then_inc(consts_ready, 1)
            pool.wait_ge(consts_ready, 1)
            pool.affine_select(out=tl[:, 0, P:2 * P], in_=tl[:, 0, 0:P], compare_op=ALU.is_ge, fill=0.0, base=0,
                               pattern=[[-1, P]], channel_multiplier=1)
            pool.affine_select(out=mask[:, :], in_=tl[:, 1, 0:P], compare_op=ALU.is_gt, fill=0.0, base=0,
                               pattern=[[1, P]], channel_multiplier=-1).then_inc(consts_ready, 1)

        @block.tensor
        def _(pe):
            def gemm(g, gi, m, it, x, tiles=None, order=(0, 4, 8, 12), tokens_out=False):
                b = 2 * (g % 2)
                if counts(g - 1, gi):
                    pe.wait_ge(sum_ready, gi + (g - 1))
                for j in range(4):
                    if tiles is not None:
                        pe.wait_ge(*tiles[j])
                    pe.wait_ge(lo_ready, it * 8 + (m + j + 1))
                    w = spl[:, (m + j) % NSPL, :, :, :]
                    for q in range(4):
                        kt = order[j] + q
                        first, last = j == 0 and q == 0, j == 3 and q == 3
                        for o in range(2):
                            c = slice(o * P, (o + 1) * P)
                            if tokens_out:
                                pe.matmul(ps[:, b + o, :], x[:, kt, 0, c], w[:, q, :, :], start=first, stop=False)
                                mm = pe.matmul(ps[:, b + o, 0:256], x[:, kt, 1, c], w[:, q, 0, :],
                                               start=False, stop=last)
                            else:
                                pe.matmul(ps[:, b + o, :], w[:, q, 0, c], x[:, kt, :, :], start=first, stop=False)
                                mm = pe.matmul(ps[:, b + o, 0:256], w[:, q, 1, c], x[:, kt, 0, :],
                                               start=False, stop=last)
                    mm.then_inc(chunk_used, 1)

            def stats(n, columns=False):
                pe.wait_ge(sq_folded, 16 * (n + 1))
                if n > 0:
                    pe.wait_ge(rstd_ready, n)
                mm = pe.matmul(Z[:, 0, 0:256], onesD[:, :], nacc[:, :], start=True, stop=True)
                if columns:
                    for t in range(2):
                        mm = pe.matmul(Z[:, 0, 256 + t:257 + t], nacc[:, t * P:(t + 1) * P], onesD[:, 0:1],
                                       start=False, stop=True, skip_group_check=True)
                mm.then_inc(stat_ready, 1)

            def after_res(f):
                return [(res_tiles, f + 2 * j + 2) for j in range(4)]

            def ple(g, m, layer, units):
                for u in units:
                    c, b = m + 1 + u // 2, 2 * (u % 2)
                    pe.wait_ge(sum_ready, g + u - 1)
                    pe.wait_ge(lo_ready, c + 1)
                    for k in range(2):
                        x = spl[:, m % NSPL, 2 * layer + k, :, :]
                        for o in range(2):
                            w = spl[:, c % NSPL, 2 * k + u % 2, :, o * P:(o + 1) * P]
                            pe.matmul(ps[:, b + o, :], w[:, 0, :], x, start=(k == 0), stop=False)
                            mm = pe.matmul(ps[:, b + o, 0:256], w[:, 1, :], x[:, 0, :], start=False, stop=(k == 1))
                    if u < 7:
                        mm.then_inc(ple_done, 1)
                    else:
                        mm.then_inc(chunk_used, 5)

            def scores(pr, i, s):
                pe.wait_ge(qk_split, i * 6 + (3 * pr + 2))
                if counts(pr, i):
                    pe.wait_ge(logw_cut, i * 2 + pr)
                q, k = qk[s][:, 0, :, :, :], qk[s][:, 1, :, :, :]
                for e in range(2):
                    for kt, cols, qs in ((0, slice(0, 256), slice(0, 256)), (1, slice(256, 384), slice(P, 256))):
                        kc = slice(kt * P, (kt + 1) * P)
                        for n, (kh, qh) in enumerate(((0, 0), (0, 1), (1, 0))):
                            mm = pe.matmul(Z[:, e, cols], k[:, e, kh, kc], q[:, e, qh, qs],
                                           start=(n == 0 and kt == 0), stop=False, skip_group_check=True)
                mm.then_inc(z_ready, 1)

            def suffix_sums(pr, i):
                pe.wait_ge(soft_split, i * 2 + (pr + 1))
                for e in range(2):
                    for hl in range(2):
                        pe.matmul(Z[:, e, 0:384], ngtri[:, :], ws[:, e, hl, 0:384],
                                  start=False, stop=False, skip_group_check=True)
                        mm = pe.matmul(Z[:, e, P:256], ngone[:, :], ws[:, e, hl, 256:384],
                                       start=False, stop=(hl == 1), skip_group_check=True)
                mm.then_inc(logw_ready, 1)

            def values(pr, i, s):
                v = vv[s]
                pe.wait_ge(qk_split, i * 6 + (3 * pr + 3))
                pe.wait_ge(w_split, i * 2 + (pr + 1))
                if counts(pr, i):
                    pe.wait_ge(att_tiles, i * 2 + pr)
                for e in range(2):
                    hc = slice(e * P, (e + 1) * P)
                    for kt, cols, wc in ((0, slice(0, 256), slice(0, 256)), (1, slice(P, 256), slice(256, 384))):
                        for n, (vh, wh) in enumerate(((0, 0), (0, 1), (1, 0))):
                            mm = pe.matmul(O[:, e, cols], v[:, kt, vh, hc], ws[:, e, wh, wc],
                                           start=(n == 0 and kt == 0), stop=(n == 2 and kt == 1),
                                           skip_group_check=True)
                mm.then_inc(o_ready, 1)

            def first_pair(g, m, x, f_in, norm):
                gemm(g, 0, m, 0, x, after_res(f_in))
                stats(norm)
                gemm(g + 1, 0, m + 4, 0, x)

            def mlp(g, m, x, hid, f_in, norm, u):
                first_pair(g, m, x, f_in, norm)
                with pe.Fori(1, 4) as i:
                    for s in range(2):
                        gemm(g + s, i * 2, m + 4 * s, i, x)
                with pe.Fori(0, 4) as i:
                    for s in range(2):
                        gemm(g + 8 + s, i * 2, m + 32 + 4 * s, i, hid,
                             [(up_tiles, u + 2 * j + 2) for j in range(4)])
                with pe.Fori(1, 4) as f:
                    with pe.Fori(0, 4) as i:
                        for s in range(2):
                            gemm(g + s, f * 16 + i * 2, m + 4 * s, f * 8 + i, x)
                    with pe.Fori(0, 4) as i:
                        for s in range(2):
                            gemm(g + 8 + s, f * 16 + i * 2, m + 32 + 4 * s, f * 8 + i, hid,
                                 [(up_tiles, f * 8 + (u + 2 * j + 2)) for j in range(4)])

            def square(g, m, x, tiles, order=(0, 4, 8, 12)):
                with pe.Fori(0, 4) as i:
                    for s in range(2):
                        gemm(g + s, i * 2, m + 4 * s, i, x, tiles, order)

            def after_norm(g, m, x, f_in, norm):
                first_pair(g, m, x, f_in, norm)
                with pe.Fori(1, 4) as i:
                    for s in range(2):
                        gemm(g + s, i * 2, m + 4 * s, i, x)

            pe.wait_ge(consts_ready, 1)
            after_norm(G_GLU, C_GLU, XA, 0, 0)
            with pe.Fori(0, 4) as i:
                for s in range(2):
                    gemm(G_REC + s, i * 2, C_REC + 4 * s, i, XA)
            pe.wait_ge(lo_ready, C_RG + 2)
            pe.wait_ge(xr_tiles, 4)
            for t in range(8):
                B = (Z, O)[t % 2]
                if t >= 2:
                    pe.wait_ge(rg_sum, t - 1)
                for a in range(2):
                    w = spl[:, (C_RG + a) % NSPL, t // 2, :, (t % 2) * P:(t % 2 + 1) * P]
                    pe.matmul(B[:, a, :], w[:, 0, :], XB[:, 8 + t, :, :], start=True, stop=False)
                    mm = pe.matmul(B[:, a, 0:256], w[:, 1, :], XB[:, 8 + t, 0, :], start=False, stop=True)
                if t < 7:
                    mm.then_inc(rg_done, 1)
                else:
                    mm.then_inc(chunk_used, 2)
            ple(G_PLE0, C_PLE0, 0, range(8))
            for n in range(2):
                pe.wait_ge(ln_part, n + 1)
                pe.matmul(Z[:, 0, 0:256], onesA[:, :], nacc[:, :], start=True, stop=True).then_inc(ln_stat, 1)
            square(G_OUT0, C_OUT0, XB, [(yb_tiles, 1), (yb_tiles, 1), (ya_tiles, 1), (ya_tiles, 1)], (8, 12, 0, 4))
            mlp(G_MLP0, C_MLP0, XA, XB, 8, 1, 0)
            after_norm(G_GATE0, C_GATE0, XA, 16, 2)

            def pair(s, i, first):
                g, m = G_QKV + 3 * s, C_QKV + 12 * s
                gemm(g, i * 6, m, i * 3, XB, after_res(24) if first else None)
                if first:
                    stats(3, columns=True)
                else:
                    suffix_sums(s - 1, i)
                gemm(g + 1, i * 6, m + 4, i * 3, XB)
                if not first:
                    values(s - 1, i, (s - 1) % 2)
                gemm(g + 2, i * 6, m + 8, i * 3, XB, tokens_out=True)
                scores(s, i, s)

            pair(0, 0, True)
            pair(1, 0, False)
            with pe.Fori(1, 4) as i:
                pair(0, i, False)
                pair(1, i, False)
            ple(G_PLE1, C_PLE1, 1, range(4))
            suffix_sums(7, 0)
            ple(G_PLE1, C_PLE1, 1, range(4, 8))
            values(7, 0, 1)
            square(G_OUT1, C_OUT1, XA, [(att_tiles, 2 * j + 2) for j in range(4)])
            mlp(G_MLP1, C_MLP1, XB, XA, 32, 4, 32)
            after_norm(G_GATE1, C_GATE1, XB, 40, 5)
            stats(6)

        @block.scalar
        def _(act):
            def copy(out, in_, scale=1.0):
                return act.activation(out, in_, ACT.Copy, scale=scale)

            def split(m, it=0):
                if m < CHUNKS:
                    act.wait_ge(raw_landed[m % NRAW], it * (16 * 8 // NRAW) + 16 * (m // NRAW + 1))
                    if counts(m - NSPL + 1, it):
                        act.wait_ge(chunk_used, it * 8 + (m - NSPL + 1))
                    copy(spl[:, m % NSPL, :, 0, :], raw[:, m % NRAW, :, :]).then_inc(hi_ready, 1)

            def period(m, it, k=4):
                for q in range(k):
                    split(m + NSPL + q, it)

            def take_cross(g, gi, ready):
                if counts(g, gi):
                    act.wait_ge(sum_ready, gi + g)
                act.wait_ge(*ready)
                b = 2 * (g % 2)
                copy(cross[:, :, :], ps[:, b:b + 2, 256:512]).then_inc(cross_copied, 1)

            def group_done(m, it):
                return chunk_used, it * 8 + (m + 4)

            def norm(n, columns=False):
                act.wait_ge(stat_ready, n + 1)
                r = act.activation(rB[:, :], Z[:, 0, 0:256], ACT.Sqrt, bias=epsb[:, :])
                if columns:
                    r = act.activation(rC[:, :], Z[:, 0, 256:258], ACT.Sqrt, bias=epsb[:, :])
                r.then_inc(root_ready, 1)

            def squares(t0):
                act.activation(tv[:, :, :], h[:, bass.ds(t0, 2), :], ACT.Square).then_inc(sq_ready, 1)

            def res_his(t0, n, X):
                for j in range(2):
                    r = act.activation(X[:, bass.ds(t0 + j, 1), 0, :], h[:, bass.ds(t0 + j, 1), :], ACT.Identity,
                                       scale=gain(n, t0 + j))
                r.then_inc(res_hi, 1)

            def residual(hidx, t0, n, X):
                act.wait_ge(res_ready, hidx + 1)
                squares(t0)
                if X is not None:
                    res_his(t0, n, X)
                else:
                    act.wait_ge(sq_ready, hidx - 39)
                    for j in range(2):
                        hj = h[:, bass.ds(t0 + j, 1), :]
                        r = act.activation(hj, hj, ACT.Identity, scale=gain(n, t0 + j))
                    r.then_inc(out_scaled, 1)

            def up(g, gi, m, it, u, t0, hid, norm_n=None):
                period(m, it)
                take_cross(g, gi, group_done(m, it))
                if norm_n is not None:
                    norm(norm_n)
                act.wait_ge(up_relu, u + 1)
                act.activation(tv[:, :, :], tv[:, :, :], ACT.Square).then_inc(up_sq, 1)
                act.wait_ge(up_sq, u + 1)
                copy(hid[:, bass.ds(t0, 2), 0, :], tv[:, :, :]).then_inc(up_hi, 1)

            def down(g, gi, m, it):
                period(m, it)
                take_cross(g, gi, group_done(m, it))

            def gate(g, gi, m, it, k, hidx, t0, n, X, norm_n=None):
                period(m, it)
                take_cross(g, gi, group_done(m, it))
                if norm_n is not None:
                    norm(norm_n)
                act.wait_ge(gate_scaled, k + 1)
                act.activation(tv[:, :, :], tv[:, :, :], ACT.Sigmoid).then_inc(gate_sig, 1)
                residual(hidx, t0, n, X)

            def out_groups(g, m, hidx, n, X):
                with act.Fori(0, 4) as i:
                    for s in range(2):
                        period(m + 4 * s, i)
                        take_cross(g + s, i * 2, group_done(m + 4 * s, i))
                        residual(i * 2 + (hidx + s), i * 4 + 2 * s, n, X)

            def mlp(g, m, u, hidx, norm_in, hid, n, X):
                for s in range(2):
                    up(g + s, 0, m + 4 * s, 0, u + s, 2 * s, hid, norm_in if s == 0 else None)
                with act.Fori(1, 4) as i:
                    for s in range(2):
                        up(g + s, i * 2, m + 4 * s, i, i * 2 + (u + s), i * 4 + 2 * s, hid)
                with act.Fori(0, 4) as i:
                    for s in range(2):
                        down(g + 8 + s, i * 2, m + 32 + 4 * s, i)
                with act.Fori(1, 3) as f:
                    with act.Fori(0, 4) as i:
                        for s in range(2):
                            up(g + s, f * 16 + i * 2, m + 4 * s, f * 8 + i, f * 8 + i * 2 + (u + s),
                               i * 4 + 2 * s, hid)
                    with act.Fori(0, 4) as i:
                        for s in range(2):
                            down(g + 8 + s, f * 16 + i * 2, m + 32 + 4 * s, f * 8 + i)
                g, m, u, hidx = g + 48, m + 192, u + 24, hidx + 24
                with act.Fori(0, 4) as i:
                    for s in range(2):
                        up(g + s, i * 2, m + 4 * s, i, i * 2 + (u + s), i * 4 + 2 * s, hid)
                out_groups(g + 8, m + 32, hidx, n, X)

            def gates(g, m, k, hidx, norm_in, n, X):
                for s in range(2):
                    gate(g + s, 0, m + 4 * s, 0, k + s, hidx + s, 2 * s, n, X, norm_in if s == 0 else None)
                with act.Fori(1, 3) as i:
                    for s in range(2):
                        gate(g + s, i * 2, m + 4 * s, i, i * 2 + (k + s), i * 2 + (hidx + s), i * 4 + 2 * s, n, X)
                for s in range(2):
                    gate(g + 6 + s, 0, m + 24 + 4 * s, 0, k + 6 + s, hidx + 6 + s, 12 + 2 * s, n, X)

            act.wait_ge(par_landed, 16)
            act.activation(small[:, 0, :], params[:, LAMBDA:LAMBDA + 8], ACT.Abs).then_inc(lam_abs, 1)
            act.wait_ge(lam_abs, 1)
            act.activation(small[:, 1, :], small[:, 0, :], ACT.Exp, scale=-1.0).then_inc(lam_exp, 1)
            for f in range(8):
                act.wait_ge(x_landed[f // 2], 16)
                if f >= 1:
                    act.wait_ge(sq_folded, 2 * f)
                squares(2 * f)
                res_his(2 * f, 0, XA)
                split(f)

            def glu_pair(c, first):
                period(C_GLU, c)
                take_cross(G_GLU, c * 2, group_done(C_GLU, c))
                if first:
                    norm(0)
                period(C_GLU + 4, c)
                take_cross(G_GLU + 1, c * 2, group_done(C_GLU + 4, c))
                act.wait_ge(glu_scaled, c + 1)
                act.activation(tv[:, :, :], tv[:, :, :], ACT.Sigmoid).then_inc(glu_sig, 1)

            glu_pair(0, True)
            with act.Fori(1, 4) as c:
                glu_pair(c, False)
            with act.Fori(0, 4) as c:
                period(C_REC, c)
                take_cross(G_REC, c * 2, group_done(C_REC, c))
                act.wait_ge(xr_step, c * 9 + 9)
                copy(XB[:, bass.ds(c * 2 + 8, 2), 0, :], pp[:, bass.ds(c * 2, 2), :]).then_inc(xr_hi, 1)
                period(C_REC + 4, c)
                take_cross(G_REC + 1, c * 2, group_done(C_REC + 4, c))
                act.wait_ge(gr_scaled, c + 1)
                act.activation(pp[:, bass.ds(c * 2 + 8, 2), :], tv[:, :, :], ACT.Gelu_apprx_tanh).then_inc(gr_ready, 1)
            for t in range(8):
                B = (Z, O)[t % 2]
                if t < 7:
                    act.wait_ge(rg_done, t + 1)
                else:
                    act.wait_ge(chunk_used, C_RG + 2)
                if t == 0:
                    act.wait_ge(sum_ready, G_PLE0)
                else:
                    act.wait_ge(rg_sum, t)
                copy(cross[:, :, :], B[:, :, 256:512]).then_inc(rg_cross, 1)
            period(C_RG, 0, 2)
            act.wait_ge(rg_sum, 8)
            for a, bias in ((0, RG_BA), (1, RG_BX)):
                for t in range(8):
                    r = act.activation(rg[:, t, a, :], rg[:, t, a, :], ACT.Sigmoid, bias=par_col(bias + t))
            r.then_inc(rg_act, 1)
            act.wait_ge(rg_act, 1)
            act.wait_ge(lam_chain, LAM_STEPS)
            for t in range(8):
                act.activation(dec[:, t, :], rg[:, t, 0, :], ACT.Exp, scale=nlamc[:, t:t + 1])
            for t in range(8):
                r = act.activation(mlt[:, t, :], rg[:, t, 0, :], ACT.Tanh, scale=lamc[:, t:t + 1])
            r.then_inc(rg_act, 1)
            act.wait_ge(rg_vec, 2)
            act.activation(mlt[:, :, :], mlt[:, :, :], ACT.Sqrt).then_inc(rg_act, 1)
            act.wait_ge(rg_vec, 6)
            copy(XB[:, 8:16, 0, :], rg[:, :, 0, :]).then_inc(rg_act, 1)

            def ple_cross(g, m, layer, units):
                for u in units:
                    take_cross(g + u, 0, (ple_done, 7 * layer + u + 1) if u < 7 else (chunk_used, m + 5))

            ple_cross(G_PLE0, C_PLE0, 0, range(8))
            period(C_PLE0, 0, 5)
            act.wait_ge(ln_vec, 1)
            act.activation(dec[:, :, :], y[:, :, :], ACT.Square).then_inc(ln_act, 1)
            act.wait_ge(ln_stat, 2)
            act.activation(tv[:, 0, :], Z[:, 0, 0:256], ACT.Sqrt, bias=epsb[:, :]).then_inc(ln_act, 1)
            act.wait_ge(ln_vec, 3)
            for t in range(8):
                r = act.activation(y[:, t, :], y[:, t, :], ACT.Silu, scale=par_col(LN_G + t), bias=par_col(LN_B + t))
            r.then_inc(ln_act, 1)
            act.wait_ge(ln_act, 3)
            copy(XB[:, 0:8, 0, :], y[:, :, :]).then_inc(ln_act, 1)

            out_groups(G_OUT0, C_OUT0, 0, 1, XA)
            mlp(G_MLP0, C_MLP0, 0, 8, 1, XB, 2, XA)
            gates(G_GATE0, C_GATE0, 0, 40, 2, 3, XB)

            def soft_exp(pr, i):
                act.wait_ge(z_ready, i * 2 + (pr + 1))
                act.activation(te[:, :, :], Z[:, :, 0:384], ACT.Abs).then_inc(z_abs, 1)
                act.wait_ge(z_abs, i * 2 + (pr + 1))
                act.activation(te[:, :, :], te[:, :, :], ACT.Exp, scale=-1.0).then_inc(z_exp, 1)
                act.wait_ge(z_exp, i * 2 + (pr + 1))
                act.activation(te[:, :, :], te[:, :, :], ACT.Ln, bias=1.0).then_inc(z_log, 1)

            def soft_round(pr, i):
                act.wait_ge(soft_ready, i * 2 + (pr + 1))
                copy(ws[:, :, 0, :], tl[:, :, :]).then_inc(soft_hi, 1)

            def weights_exp(pr, i):
                act.wait_ge(logw_cut, i * 2 + (pr + 1))
                act.activation(tl[:, :, :], te[:, :, :], ACT.Exp).then_inc(w_exp, 1)

            def weights_round(pr, i):
                act.wait_ge(w_ready, i * 2 + (pr + 1))
                copy(ws[:, :, 0, :], tl[:, :, :]).then_inc(w_hi, 1)

            def out_round(pr, i):
                act.wait_ge(o_ready, i * 2 + (pr + 1))
                copy(XA[:, bass.ds(i * 4 + 2 * pr, 2), 0, :], O[:, :, 0:256]).then_inc(o_hi, 1)

            def qkv(part, s, i, first=False):
                g, m = G_QKV + 3 * s + part, C_QKV + 12 * s + 4 * part
                steps = ((soft_exp, soft_round), (weights_exp, weights_round), (out_round,))[part]
                for q in range(4):
                    if q < len(steps) and not first:
                        steps[q](s - 1, i)
                    split(m + NSPL + q, i * 3)
                take_cross(g, i * 6, group_done(m, i * 3))
                if first and part == 0:
                    norm(3, columns=True)
                act.wait_ge(qk_scaled, i * 6 + (3 * s + part + 1))
                out = vv[s][:, :, 0, :] if part == 2 else qk[s][:, part, :, 0, :]
                copy(out, tv[:, :, :]).then_inc(qk_hi, 1)

            for s in range(2):
                for part in range(3):
                    qkv(part, s, 0, first=(s == 0))
            with act.Fori(1, 4) as i:
                for s in range(2):
                    for part in range(3):
                        qkv(part, s, i)
            soft_exp(7, 0)
            ple_cross(G_PLE1, C_PLE1, 1, range(2))
            soft_round(7, 0)
            ple_cross(G_PLE1, C_PLE1, 1, range(2, 4))
            weights_exp(7, 0)
            ple_cross(G_PLE1, C_PLE1, 1, range(4, 6))
            weights_round(7, 0)
            ple_cross(G_PLE1, C_PLE1, 1, range(6, 8))
            period(C_PLE1, 0, 5)
            out_round(7, 0)

            out_groups(G_OUT1, C_OUT1, 48, 4, XB)
            mlp(G_MLP1, C_MLP1, 32, 56, 4, XA, 5, XB)
            gates(G_GATE1, C_GATE1, 8, 88, 5, 6, None)
            norm(6)

        @block.vector
        def _(dve):
            def split(m, it=0):
                if m < CHUNKS:
                    dve.wait_ge(hi_ready, it * 8 + (m + 1))
                    s = spl[:, m % NSPL, :, :, :]
                    dve.tensor_tensor(s[:, :, 1, :], raw[:, m % NRAW, :, :], s[:, :, 0, :].bitcast(F32),
                                      ALU.subtract).then_inc(lo_ready, 1)

            def period(m, it, k=4):
                for q in range(k):
                    split(m + NSPL + q, it)

            def lo_of(X, t0, n, v):
                return dve.tensor_tensor(X[:, bass.ds(t0, n), 1, :], v, X[:, bass.ds(t0, n), 0, :].bitcast(F32),
                                         ALU.subtract)

            def take_sum(g, gi, out=None):
                b = 2 * (g % 2)
                dve.wait_ge(cross_copied, gi + (g + 1))
                dve.tensor_tensor(tv[:, :, :] if out is None else out, cross[:, :, :], ps[:, b:b + 2, 0:256],
                                  ALU.add).then_inc(sum_ready, 1)

            def scaled(g, gi, out, done):
                dve.wait_ge(sum_ready, gi + (g + 1))
                dve.tensor_tensor(out, tv[:, :, :], bcast(rB[:, :], 2), ALU.mult).then_inc(done, 1)

            def norm(n, columns=False):
                dve.wait_ge(root_ready, n + 1)
                r = dve.reciprocal(rB[:, :], rB[:, :])
                if columns:
                    r = dve.reciprocal(rC[:, :], rC[:, :])
                r.then_inc(rstd_ready, 1)
                dve.wait_ge(rstd_ready, n + 1)

            def clear(n):
                if n >= 1:
                    dve.wait_ge(stat_ready, n)
                dve.memset(nacc[:, :], 0.0).then_inc(nacc_clear, 1)
                dve.wait_ge(nacc_clear, n + 1)

            def fold(f):
                dve.wait_ge(sq_ready, f + 1)
                dve.tensor_tensor(tv[:, 0, :], tv[:, 0, :], tv[:, 1, :], ALU.add).then_inc(sq_folded, 1)
                dve.wait_ge(sq_folded, f * 2 + 1)
                dve.tensor_tensor(nacc[:, :], nacc[:, :], tv[:, 0, :], ALU.add).then_inc(sq_folded, 1)
                dve.wait_ge(sq_folded, f * 2 + 2)

            def res_los(f, t0, n, X):
                dve.wait_ge(res_hi, f + 1)
                for j in range(2):
                    r = dve.scalar_tensor_tensor(
                        out=X[:, bass.ds(t0 + j, 1), 1, :], in0=h[:, bass.ds(t0 + j, 1), :], scalar=gain(n, t0 + j),
                        in1=X[:, bass.ds(t0 + j, 1), 0, :].bitcast(F32), op0=ALU.mult, op1=ALU.subtract)
                r.then_inc(res_tiles, 1)

            def add_h(hidx, t0, early):
                if not early:
                    dve.wait_ge(res_ready, hidx - 7)
                ht = h[:, bass.ds(t0, 2), :]
                dve.tensor_tensor(ht, ht, tv[:, :, :], ALU.add).then_inc(res_ready, 1)
                dve.wait_ge(res_ready, hidx + 1)

            def residual(f, t0, n, X):
                fold(f)
                if X is not None:
                    res_los(f, t0, n, X)

            def up(g, gi, m, it, u, t0, hid, norm_n=None):
                period(m, it)
                take_sum(g, gi)
                if norm_n is not None:
                    norm(norm_n)
                dve.wait_ge(sum_ready, gi + (g + 1))
                dve.scalar_tensor_tensor(out=tv[:, :, :], in0=tv[:, :, :], scalar=0.0, in1=bcast(rB[:, :], 2),
                                         op0=ALU.max, op1=ALU.mult).then_inc(up_relu, 1)
                dve.wait_ge(up_hi, u + 1)
                lo_of(hid, t0, 2, tv[:, :, :]).then_inc(up_tiles, 1)
                dve.wait_ge(up_tiles, u + 1)

            def down(g, gi, m, it, hidx, t0, early=False):
                period(m, it)
                take_sum(g, gi)
                dve.wait_ge(sum_ready, gi + (g + 1))
                add_h(hidx, t0, early)

            def gate(g, gi, m, it, k, f, hidx, t0, n, X, norm_n=None):
                period(m, it)
                take_sum(g, gi)
                if norm_n is not None:
                    norm(norm_n)
                    clear(n)
                scaled(g, gi, tv[:, :, :], gate_scaled)
                dve.wait_ge(gate_sig, k + 1)
                dve.tensor_tensor(tv[:, :, :], tv[:, :, :], pp[:, bass.ds(t0, 2), :], ALU.mult).then_inc(gate_mul, 1)
                dve.wait_ge(gate_mul, k + 1)
                add_h(hidx, t0, False)
                residual(f, t0, n, X)

            def out_groups(g, m, hidx, f, n, X, early=False):
                clear(n)
                with dve.Fori(0, 4) as i:
                    for s in range(2):
                        down(g + s, i * 2, m + 4 * s, i, i * 2 + (hidx + s), i * 4 + 2 * s, early)
                        residual(i * 2 + (f + s), i * 4 + 2 * s, n, X)

            def mlp(g, m, u, hidx, norm_in, hid, f_out, n, X):
                for s in range(2):
                    up(g + s, 0, m + 4 * s, 0, u + s, 2 * s, hid, norm_in if s == 0 else None)
                with dve.Fori(1, 4) as i:
                    for s in range(2):
                        up(g + s, i * 2, m + 4 * s, i, i * 2 + (u + s), i * 4 + 2 * s, hid)
                with dve.Fori(0, 4) as i:
                    for s in range(2):
                        down(g + 8 + s, i * 2, m + 32 + 4 * s, i, i * 2 + (hidx + s), i * 4 + 2 * s)
                with dve.Fori(1, 3) as f:
                    with dve.Fori(0, 4) as i:
                        for s in range(2):
                            up(g + s, f * 16 + i * 2, m + 4 * s, f * 8 + i, f * 8 + i * 2 + (u + s),
                               i * 4 + 2 * s, hid)
                    with dve.Fori(0, 4) as i:
                        for s in range(2):
                            down(g + 8 + s, f * 16 + i * 2, m + 32 + 4 * s, f * 8 + i,
                                 f * 8 + i * 2 + (hidx + s), i * 4 + 2 * s)
                g, m, u, hidx = g + 48, m + 192, u + 24, hidx + 24
                with dve.Fori(0, 4) as i:
                    for s in range(2):
                        up(g + s, i * 2, m + 4 * s, i, i * 2 + (u + s), i * 4 + 2 * s, hid)
                out_groups(g + 8, m + 32, hidx, f_out, n, X)

            def gates(g, m, k, f, hidx, norm_in, n, X):
                for s in range(2):
                    gate(g + s, 0, m + 4 * s, 0, k + s, f + s, hidx + s, 2 * s, n, X, norm_in if s == 0 else None)
                with dve.Fori(1, 3) as i:
                    for s in range(2):
                        gate(g + s, i * 2, m + 4 * s, i, i * 2 + (k + s), i * 2 + (f + s), i * 2 + (hidx + s),
                             i * 4 + 2 * s, n, X)
                for s in range(2):
                    gate(g + 6 + s, 0, m + 24 + 4 * s, 0, k + 6 + s, f + 6 + s, hidx + 6 + s, 12 + 2 * s, n, X)

            lam = params[:, LAMBDA:LAMBDA + 8]
            poly, e_, s2, s1 = (small[:, j, :] for j in range(4))
            steps = [0]

            def link(ins):
                steps[0] += 1
                ins.then_inc(lam_chain, 1)
                dve.wait_ge(lam_chain, steps[0])

            dve.wait_ge(par_landed, 16)
            dve.wait_ge(consts_ready, 2)
            dve.tensor_copy(ngtri[:, :], tl[:, 0, P:2 * P])
            dve.tensor_copy(ngone[:, :], tl[:, 0, 0:P])
            clear(0)
            for f in range(8):
                fold(f)
                res_los(f, 2 * f, 0, XA)
                split(f)
            dve.wait_ge(lam_exp, 1)
            link(dve.tensor_scalar(s2, e_, 2.0, None, ALU.add))
            link(dve.reciprocal(s2, s2))
            link(dve.tensor_tensor(s1, e_, s2, ALU.mult))
            link(dve.tensor_tensor(s2, s1, s1, ALU.mult))
            link(dve.tensor_scalar(poly, s2, 1.0 / 17, None, ALU.mult))
            for k in (15, 13, 11, 9, 7, 5, 3):
                link(dve.scalar_tensor_tensor(out=poly, in0=poly, scalar=1.0 / k, in1=s2, op0=ALU.add, op1=ALU.mult))
            link(dve.scalar_tensor_tensor(out=poly, in0=poly, scalar=1.0, in1=s1, op0=ALU.add, op1=ALU.mult))
            link(dve.tensor_scalar(s2, lam, 0.0, -1.0, ALU.min, ALU.mult))
            link(dve.scalar_tensor_tensor(out=s1, in0=poly, scalar=2.0, in1=s2, op0=ALU.mult, op1=ALU.add))
            link(dve.tensor_scalar(lamc[:, :], s1, 8.0, None, ALU.mult))
            link(dve.tensor_scalar(nlamc[:, :], s1, -8.0, None, ALU.mult))
            assert steps[0] == LAM_STEPS

            def conv(pair, base, taps, n0, n1):
                for n in range(n0, n1):
                    k, j = taps[n // 2], n % 2
                    t = pair * 2 + j
                    if n == 0:
                        dve.wait_ge(glu_ready, pair + 1)
                    if k > 0:
                        dve.wait_ge(conv_step, base if n < 2 else base + (n - 1))
                    x, w = glu[:, bass.ds(t, 1), k:k + T], par_col(t * CA + (CONV_A_W + k))
                    yt = y[:, bass.ds(t, 1), :]
                    if k == 0:
                        r = dve.tensor_scalar(yt, x, w, par_col(t + CONV_A_B), ALU.mult, ALU.add)
                    else:
                        r = dve.scalar_tensor_tensor(out=yt, in0=x, scalar=w, in1=yt, op0=ALU.mult, op1=ALU.add)
                    r.then_inc(conv_step, 1)

            EARLY, LATE = tuple(range(16)), tuple(range(16, CA))

            def glu_pair(c, first):
                for q in range(4):
                    if not first:
                        conv(c - 1, c * 32 - 32, EARLY, 4 * q, 4 * q + 4)
                    split(C_GLU + NSPL + q, c)
                take_sum(G_GLU, c * 2)
                if first:
                    norm(0)
                scaled(G_GLU, c * 2, glu[:, bass.ds(c * 2, 2), PAD_A:], glu_val)
                dve.wait_ge(glu_val, c + 1)
                for q in range(4):
                    if not first:
                        conv(c - 1, c * 32 - 32, EARLY, 16 + 4 * q, 20 + 4 * q)
                    split(C_GLU + 4 + NSPL + q, c)
                take_sum(G_GLU + 1, c * 2)
                scaled(G_GLU + 1, c * 2, tv[:, :, :], glu_scaled)
                dve.wait_ge(glu_sig, c + 1)
                gl = glu[:, bass.ds(c * 2, 2), PAD_A:]
                dve.tensor_tensor(gl, gl, tv[:, :, :], ALU.mult).then_inc(glu_ready, 1)
                dve.wait_ge(glu_ready, c + 1)

            glu_pair(0, True)
            with dve.Fori(1, 4) as c:
                glu_pair(c, False)
            conv(3, 96, EARLY, 0, 32)

            def short_conv(c):
                for n in range(2 * CB):
                    k, j = n // 2, n % 2
                    dve.wait_ge(xr_step, c * 9 + (1 if n < 2 else n))
                    t = c * 2 + j
                    x, w = xrp[:, j, k:k + T].unsqueeze(1), par_col(t * CB + (CONV_B_W + k))
                    o = pp[:, bass.ds(t, 1), :]
                    if k == 0:
                        r = dve.tensor_scalar(o, x, w, par_col(t + CONV_B_B), ALU.mult, ALU.add)
                    else:
                        r = dve.scalar_tensor_tensor(out=o, in0=x, scalar=w, in1=o, op0=ALU.mult, op1=ALU.add)
                    r.then_inc(xr_step, 1)

            def rec_pair(c, first):
                for q in range(4):
                    conv(c, c * 30 + 128, LATE, 4 * q, 4 * q + 4)
                    split(C_REC + NSPL + q, c)
                if not first:
                    dve.wait_ge(gr_ready, c)
                take_sum(G_REC, c * 2)
                scaled(G_REC, c * 2, xrp[:, :, PAD_B:], xr_step)
                short_conv(c)
                dve.wait_ge(xr_hi, c + 1)
                lo_of(XB, c * 2 + 8, 2, pp[:, bass.ds(c * 2, 2), :]).then_inc(xr_tiles, 1)
                for q in range(4):
                    conv(c, c * 30 + 128, LATE, 16 + 4 * q, min(20 + 4 * q, 30))
                    split(C_REC + 4 + NSPL + q, c)
                take_sum(G_REC + 1, c * 2)
                scaled(G_REC + 1, c * 2, tv[:, :, :], gr_scaled)

            rec_pair(0, True)
            with dve.Fori(1, 4) as c:
                rec_pair(c, False)

            for t in range(8):
                B = (Z, O)[t % 2]
                dve.wait_ge(rg_cross, t + 1)
                dve.tensor_tensor(rg[:, t, :, :], cross[:, :, :], B[:, :, 0:256], ALU.add).then_inc(rg_sum, 1)
            period(C_RG, 0, 2)
            dve.wait_ge(conv_step, 8 * CA)
            dve.tensor_reduce(nacc[:, :], y[:, :, :].rearrange("p t n -> p n t"), AX_X, ALU.add).then_inc(ln_part, 1)
            r_, i_ = rg[:, :, 0, :], rg[:, :, 1, :]
            dve.wait_ge(rg_act, 2)
            dve.tensor_tensor(r_, dec[:, :, :], dec[:, :, :], ALU.mult).then_inc(rg_vec, 1)
            dve.wait_ge(rg_vec, 1)
            dve.scalar_tensor_tensor(out=mlt[:, :, :], in0=r_, scalar=1.0, in1=mlt[:, :, :],
                                     op0=ALU.add, op1=ALU.mult).then_inc(rg_vec, 1)
            dve.tensor_tensor(i_, i_, pp[:, 0:8, :], ALU.mult).then_inc(rg_vec, 1)
            dve.wait_ge(rg_vec, 3)
            dve.wait_ge(rg_act, 3)
            dve.tensor_tensor(i_, i_, mlt[:, :, :], ALU.mult).then_inc(rg_vec, 1)
            dve.wait_ge(rg_vec, 4)
            for t in range(8):
                r = dve.tensor_tensor_scan(rg[:, t, 0, :], dec[:, t, :], rg[:, t, 1, :], 0.0, ALU.mult, ALU.add)
            r.then_inc(rg_vec, 1)
            dve.wait_ge(rg_vec, 5)
            dve.wait_ge(gr_ready, 4)
            dve.tensor_tensor(r_, r_, pp[:, 8:16, :], ALU.mult).then_inc(rg_vec, 1)
            dve.wait_ge(rg_act, 4)
            lo_of(XB, 8, 8, r_).then_inc(yb_tiles, 1)

            def ple_sums(g, units):
                for u in units:
                    take_sum(g + u, 0, pp[:, 2 * u:2 * u + 2, :])

            ple_sums(G_PLE0, range(8))
            period(C_PLE0, 0, 5)
            dve.wait_ge(ln_stat, 1)
            dve.tensor_tensor(y[:, :, :], y[:, :, :], bcast(Z[:, 0, 0:256], 8), ALU.subtract).then_inc(ln_vec, 1)
            dve.wait_ge(ln_act, 1)
            dve.tensor_reduce(nacc[:, :], dec[:, :, :].rearrange("p t n -> p n t"), AX_X, ALU.add).then_inc(ln_part, 1)
            dve.wait_ge(ln_act, 2)
            dve.reciprocal(tv[:, 0, :], tv[:, 0, :]).then_inc(ln_vec, 1)
            dve.wait_ge(ln_vec, 2)
            dve.tensor_tensor(y[:, :, :], y[:, :, :], bcast(tv[:, 0, :], 8), ALU.mult).then_inc(ln_vec, 1)
            dve.wait_ge(ln_act, 4)
            lo_of(XB, 0, 8, y[:, :, :]).then_inc(ya_tiles, 1)

            out_groups(G_OUT0, C_OUT0, 0, 8, 1, XA, early=True)
            mlp(G_MLP0, C_MLP0, 0, 8, 1, XB, 16, 2, XA)
            gates(G_GATE0, C_GATE0, 0, 24, 40, 2, 3, XB)

            z = Z[:, :, 0:384]

            def keep_earlier_keys(done):
                d = tl[:, :, :].rearrange("p e (b n) -> p e b n", n=P)[:, :, 0:3:2, :]
                dve.tensor_tensor(d, d, mask[:, :].unsqueeze(1).unsqueeze(1).broadcast_to([P, 2, 2, P]),
                                  ALU.mult).then_inc(done, 1)

            def soft_sum(pr, i):
                dve.wait_ge(z_log, i * 2 + (pr + 1))
                dve.scalar_tensor_tensor(out=tl[:, :, :], in0=z, scalar=0.0, in1=te[:, :, :],
                                         op0=ALU.max, op1=ALU.add).then_inc(soft_raw, 1)
                dve.wait_ge(soft_raw, i * 2 + (pr + 1))
                keep_earlier_keys(soft_ready)

            def soft_rest(pr, i):
                dve.wait_ge(soft_hi, i * 2 + (pr + 1))
                dve.tensor_tensor(ws[:, :, 1, :], tl[:, :, :], ws[:, :, 0, :].bitcast(F32),
                                  ALU.subtract).then_inc(soft_split, 1)

            def weights_cut(pr, i):
                dve.wait_ge(logw_ready, i * 2 + (pr + 1))
                dve.tensor_scalar(te[:, :, :], z, 0.0, None, ALU.min).then_inc(logw_cut, 1)

            def weights_mask(pr, i):
                dve.wait_ge(w_exp, i * 2 + (pr + 1))
                keep_earlier_keys(w_ready)

            def weights_rest(pr, i):
                dve.wait_ge(w_hi, i * 2 + (pr + 1))
                dve.tensor_tensor(ws[:, :, 1, :], tl[:, :, :], ws[:, :, 0, :].bitcast(F32),
                                  ALU.subtract).then_inc(w_split, 1)

            def out_rest(pr, i):
                dve.wait_ge(o_hi, i * 2 + (pr + 1))
                lo_of(XA, i * 4 + 2 * pr, 2, O[:, :, 0:256]).then_inc(att_tiles, 1)

            def qkv(part, s, i, first=False):
                g, m = G_QKV + 3 * s + part, C_QKV + 12 * s + 4 * part
                steps = ((soft_sum, soft_rest), (weights_cut, weights_mask, weights_rest), (out_rest,))[part]
                for q in range(4):
                    if q < len(steps) and not first:
                        steps[q](s - 1, i)
                    split(m + NSPL + q, i * 3)
                take_sum(g, i * 6)
                if first and part == 0:
                    norm(3, columns=True)
                dve.wait_ge(sum_ready, i * 6 + (g + 1))
                if part == 0:
                    dve.scalar_tensor_tensor(out=tv[:, :, :], in0=tv[:, :, :], scalar=float(DH) ** -0.5,
                                             in1=bcast(rB[:, :], 2), op0=ALU.mult, op1=ALU.mult).then_inc(qk_scaled, 1)
                elif part == 1:
                    dve.tensor_tensor(tv[:, :, :], tv[:, :, :], bcast(rB[:, :], 2), ALU.mult).then_inc(qk_scaled, 1)
                else:
                    for t in range(2):
                        r = dve.tensor_scalar(tv[:, t, :], tv[:, t, :], rC[:, t:t + 1], None, ALU.mult)
                    r.then_inc(qk_scaled, 1)
                dve.wait_ge(qk_hi, i * 6 + (3 * s + part + 1))
                X = vv[s] if part == 2 else qk[s][:, part, :, :, :]
                lo_of(X, 0, 2, tv[:, :, :]).then_inc(qk_split, 1)
                dve.wait_ge(qk_split, i * 6 + (3 * s + part + 1))

            for s in range(2):
                for part in range(3):
                    qkv(part, s, 0, first=(s == 0))
            with dve.Fori(1, 4) as i:
                for s in range(2):
                    for part in range(3):
                        qkv(part, s, i)
            ple_sums(G_PLE1, range(2))
            soft_sum(7, 0)
            soft_rest(7, 0)
            ple_sums(G_PLE1, range(2, 4))
            weights_cut(7, 0)
            ple_sums(G_PLE1, range(4, 6))
            weights_mask(7, 0)
            weights_rest(7, 0)
            ple_sums(G_PLE1, range(6, 8))
            period(C_PLE1, 0, 5)
            out_rest(7, 0)

            out_groups(G_OUT1, C_OUT1, 48, 32, 4, XB)
            mlp(G_MLP1, C_MLP1, 32, 56, 4, XA, 40, 5, XB)
            gates(G_GATE1, C_GATE1, 8, 48, 88, 5, 6, None)
            norm(6)
            dve.wait_ge(out_scaled, 8)
            for q in range(4):
                hq = h[:, 4 * q:4 * q + 4, :]
                dve.tensor_tensor(hq, hq, bcast(rB[:, :], 4), ALU.mult).then_inc(out_ready, 1)


LAM_STEPS = 17


def _columns(a, n):
    import numpy as np
    return np.asarray(a).reshape(-1, n, P).transpose(2, 0, 1).reshape(P, -1)


def kernel(x, p, norm_mix_g, norm_mlp_g, norm_ple_g, norm_f_g, w_in_rec, conv_a_w, conv_a_b, ln_a_g, ln_a_b,
           conv_b_w, conv_b_b, w_rg_a, b_rg_a, w_rg_x, b_rg_x, rg_lambda, w_out_rec, w_qkv, w_o_attn,
           w_mlp_up, w_mlp_down, w_ple_proj, w_ple_gate):
    import numpy as np
    import concourse.bacc as bacc
    from concourse.bass_utils import run_bass_kernel_spmd

    norms = [norm_mix_g[0], norm_mlp_g[0], norm_ple_g[0], norm_mix_g[1], norm_mlp_g[1], norm_ple_g[1], norm_f_g]
    taps_a = np.asarray(conv_a_w)[0].reshape(CA, 8, P).transpose(2, 1, 0).reshape(P, 8 * CA)
    taps_b = np.asarray(conv_b_w)[0].reshape(CB, 8, P).transpose(2, 1, 0).reshape(P, 8 * CB)
    par = np.concatenate([_columns(g, NT) for g in norms] + [taps_a] + [_columns(v, 8) for v in (conv_a_b, ln_a_g, ln_a_b)]
                         + [taps_b] + [_columns(v, 8) for v in (conv_b_b, b_rg_a, b_rg_x, rg_lambda)], axis=1)
    ins = {
        "xT": np.asarray(x)[0].T, "pT": np.asarray(p)[:, 0].transpose(0, 2, 1), "par": par,
        "w_in": w_in_rec, "w_rg_a": w_rg_a, "w_rg_x": w_rg_x, "w_out": w_out_rec, "w_qkv": w_qkv, "w_o": w_o_attn,
        "w_up": w_mlp_up, "w_down": w_mlp_down, "w_proj": w_ple_proj, "w_gate": w_ple_gate,
    }
    ins = {k: np.ascontiguousarray(v) for k, v in ins.items()}
    nc = bacc.Bacc("TRN2", target_bir_lowering=False, num_devices=1)
    aps = {k: nc.dram_tensor(f"in_{k}", v.shape, mybir.dt.from_np(v.dtype), kind="ExternalInput").ap()
           for k, v in ins.items()}
    out = nc.dram_tensor("outT", (D, T), F32, kind="ExternalOutput").ap()
    trunk(nc, outT=out, **aps)
    r = run_bass_kernel_spmd(nc, [{f"in_{k}": v for k, v in ins.items()}], core_ids=[0])
    return np.ascontiguousarray(r.results[0]["outT"].T)[None]
```

```python
from contextlib import ExitStack

import concourse.bass as bass
from concourse import mybir

P = 128
D = 2048
T = 256
FF = 4 * D
PLE = 256
DA = D // 2
DB = D // 2
CA = 31
CB = 4
DH = 128
NT = D // P
NG = D // T
CHUNK = 1024
NRAW = 4
NSPL = 8
EPS = 1e-6
PAD_A = CA - 1
PAD_B = CB - 1
XRP = PAD_B + T + 1

ALU = mybir.AluOpType
ACT = mybir.ActivationFunctionType
F32 = mybir.dt.float32
F32R = mybir.dt.float32r
AX_X = mybir.AxisListType.X

G_REC, C_REC = 0, 2
C_RG = 8
G_GLU, C_GLU = 8, 34
G_OUTB, C_OUTB = 16, 66
G_PLE0, C_PLE0 = 24, 82
G_OUTA, C_OUTA = 32, 87
G_MLP0, C_MLP0 = 40, 103
G_GATE0, C_GATE0 = 104, 359
G_QKV, C_QKV = 112, 391
G_PLE1, C_PLE1 = 136, 487
G_OUT1, C_OUT1 = 144, 492
G_MLP1, C_MLP1 = 152, 524
G_GATE1, C_GATE1 = 216, 780
CHUNKS = 812
H_OUTB, H_OUTA, H_MLP0, H_GATE0, H_OUT1, H_MLP1, H_GATE1 = 0, 8, 16, 48, 56, 64, 96
NDG = 14
CA_PE = 24
CSTEPS = 39
LAM_STEPS = 17

GAIN = 0
CONV_A_W = GAIN + 7 * NT
CONV_A_B = CONV_A_W + 8 * CA
LN_G = CONV_A_B + 8
LN_B = LN_G + 8
CONV_B_W = LN_B + 8
CONV_B_B = CONV_B_W + 8 * CB
RG_BA = CONV_B_B + 8
RG_BX = RG_BA + 8
LAMBDA = RG_BX + 8
NPAR = LAMBDA + 8


def trunk(nc, xT, pT, par, w_in, w_rg_a, w_rg_x, w_out, w_qkv, w_o, w_up, w_down, w_proj, w_gate, outT):
    with ExitStack() as ctx:
        def sb(name, shape, dt=F32):
            return ctx.enter_context(nc.sbuf_tensor(name, shape, dt))

        def sem(name):
            return ctx.enter_context(nc.semaphore(name))

        raw = sb("raw", [P, NRAW, 4, 256])
        spl = sb("spl", [P, NSPL, 4, 2, 256], F32R)
        h = sb("h", [P, NT, T])
        cross = sb("cross", [P, 2, T])
        tv = sb("tv", [P, 2, T])
        nacc = sb("nacc", [P, T])
        rB = sb("rB", [P, T])
        rC = sb("rC", [P, 2])
        params = sb("params", [P, NPAR])
        lamc = sb("lamc", [P, 8])
        nlamc = sb("nlamc", [P, 8])
        small = sb("small", [P, 4, 8])
        onesD = sb("onesD", [P, P])
        onesA = sb("onesA", [P, P])
        epsb = sb("epsb", [P, 1])
        ngtri = sb("ngtri", [P, P], F32R)
        ngone = sb("ngone", [P, P], F32R)
        mask = sb("mask", [P, P])
        XA = sb("XA", [P, NT, 2, T], F32R)
        with nc.sbuf_tensor("glu", [P, 8, PAD_A + T], F32) as glu, \
                nc.sbuf_tensor("xrp", [P, 2, XRP], F32) as xrp, \
                nc.sbuf_tensor("rest", [P, 8 * 2 * T - 8 * (PAD_A + T) - 2 * XRP], F32), \
                nc.sbuf_tensor("rg", [P, 8, 2, T], F32) as rg:
            pass
        XB = sb("XB", [P, NT, 2, T], F32R)
        with nc.sbuf_tensor("qk0", [P, 2, 2, 2, T], F32R) as qk0, nc.sbuf_tensor("v0", [P, 2, 2, T], F32R) as v0, \
                nc.sbuf_tensor("te", [P, 2, 384], F32) as te:
            pass
        pp = sb("pp", [P, NT, T])
        with nc.sbuf_tensor("wrg", [P, 2, 4, 2, 256], F32R) as wrg:
            pass
        with nc.sbuf_tensor("mlt", [P, 8, T], F32) as mlt, nc.sbuf_tensor("dec", [P, 8, T], F32) as dec:
            pass
        with nc.sbuf_tensor("y", [P, 8, T], F32) as y, nc.sbuf_tensor("y2", [P, T], F32) as y2, \
                nc.sbuf_tensor("dg", [P, NDG, P], F32) as dg, nc.sbuf_tensor("ident", [P, P], F32) as ident:
            pass
        qk1 = sb("qk1", [P, 2, 2, 2, T], F32R)
        v1 = sb("v1", [P, 2, 2, T], F32R)
        tl = sb("tl", [P, 2, 384])
        ws = sb("ws", [P, 2, 2, 384], F32R)
        qk, vv = (qk0, qk1), (v0, v1)

        ps = ctx.enter_context(nc.psum_tensor("ps", [P, 4, 512], F32))
        Z = ctx.enter_context(nc.psum_tensor("Z", [P, 2, 512], F32))
        O = ctx.enter_context(nc.psum_tensor("O", [P, 2, 512], F32))

        raw_landed = [sem(f"raw_landed{i}") for i in range(NRAW)]
        hi_ready = sem("hi_ready")
        lo_ready = sem("lo_ready")
        chunk_used = sem("chunk_used")
        par_landed = sem("par_landed")
        x_landed = [sem(f"x_landed{i}") for i in range(4)]
        consts_ready = sem("consts_ready")
        cross_copied = sem("cross_copied")
        sum_ready = sem("sum_ready")
        res_ready = sem("res_ready")
        sq_ready = sem("sq_ready")
        res_hi = sem("res_hi")
        sq_folded = sem("sq_folded")
        res_tiles = sem("res_tiles")
        nacc_clear = sem("nacc_clear")
        stat_ready = sem("stat_ready")
        root_ready = sem("root_ready")
        rstd_ready = sem("rstd_ready")
        up_relu = sem("up_relu")
        up_sq = sem("up_sq")
        up_hi = sem("up_hi")
        up_tiles = sem("up_tiles")
        gate_scaled = sem("gate_scaled")
        gate_sig = sem("gate_sig")
        gate_mul = sem("gate_mul")
        glu_scaled = sem("glu_scaled")
        glu_sig = sem("glu_sig")
        glu_val = sem("glu_val")
        glu_ready = sem("glu_ready")
        conv_step = sem("conv_step")
        dg_ready = sem("dg_ready")
        dg_used = sem("dg_used")
        conv_taken = sem("conv_taken")
        xr_step = sem("xr_step")
        xr_hi = sem("xr_hi")
        xr_tiles = sem("xr_tiles")
        gr_scaled = sem("gr_scaled")
        gr_ready = sem("gr_ready")
        rg_done = sem("rg_done")
        rg_cross = sem("rg_cross")
        rg_sum = sem("rg_sum")
        rg_act = sem("rg_act")
        rg_vec = sem("rg_vec")
        ln_part = sem("ln_part")
        ln_stat = sem("ln_stat")
        ln_act = sem("ln_act")
        ln_vec = sem("ln_vec")
        qk_scaled = sem("qk_scaled")
        qk_hi = sem("qk_hi")
        qk_split = sem("qk_split")
        z_ready = sem("z_ready")
        z_abs = sem("z_abs")
        z_exp = sem("z_exp")
        z_log = sem("z_log")
        soft_raw = sem("soft_raw")
        soft_ready = sem("soft_ready")
        soft_hi = sem("soft_hi")
        soft_split = sem("soft_split")
        logw_ready = sem("logw_ready")
        logw_cut = sem("logw_cut")
        w_exp = sem("w_exp")
        w_ready = sem("w_ready")
        w_hi = sem("w_hi")
        w_split = sem("w_split")
        o_ready = sem("o_ready")
        o_hi = sem("o_hi")
        att_tiles = sem("att_tiles")
        out_scaled = sem("out_scaled")
        out_ready = sem("out_ready")
        stored = sem("stored")
        ple_done = sem("ple_done")
        yb_tiles = sem("yb_tiles")
        ya_tiles = sem("ya_tiles")
        lam_abs = sem("lam_abs")
        lam_exp = sem("lam_exp")
        lam_chain = sem("lam_chain")

        def counts(base, turns):
            return base > 0 or not isinstance(turns, int)

        def bcast(ap, n):
            return ap.unsqueeze(1).broadcast_to([P, n, ap.shape[-1]])

        def par_col(c):
            return params[:, bass.ds(c, 1)]

        def gain(n, t):
            return par_col(t + (GAIN + n * NT))

        block = ctx.enter_context(nc.Block())

        @block.sync
        def _(sp):
            def load(m, it, src):
                if counts(m - NRAW + 1, it):
                    sp.wait_ge(lo_ready, it * 8 + (m - NRAW + 1))
                sp.dma_start(raw[:, m % NRAW, :, :], src).then_inc(raw_landed[m % NRAW], 16)

            def load_group(m, it, w, col, row0=0, rows=(0, 4, 8, 12)):
                for j, r in enumerate(rows):
                    src = w[bass.ds(row0 + r * P, 4 * P), bass.ds(col, 256)]
                    load(m + j, it, src.rearrange("(t p) n -> p t n", p=P))

            def load_ple(m, layer):
                load(m, 0, pT.rearrange("l (t p) n -> p (l t) n", p=P))
                for j in range(4):
                    src = w_proj[layer, :, 512 * j:512 * j + 512]
                    load(m + 1 + j, 0, src.rearrange("(t p) n -> p t n", p=P))

            def mlp(layer, m):
                with sp.Fori(0, 4) as f:
                    with sp.Fori(0, 4) as i:
                        for s in range(2):
                            load_group(m + 4 * s, f * 8 + i, w_up[layer], f * D + i * 512 + 256 * s)
                    with sp.Fori(0, 4) as i:
                        for s in range(2):
                            load_group(m + 32 + 4 * s, f * 8 + i, w_down[layer], i * 512 + 256 * s, row0=f * D)

            def square(m, w):
                with sp.Fori(0, 4) as i:
                    for s in range(2):
                        load_group(m + 4 * s, i, w, i * 512 + 256 * s)

            def half_square(m, w, row0):
                with sp.Fori(0, 2) as i:
                    for s in range(4):
                        load_group(m + 2 * s, i, w, i * 1024 + 256 * s, row0, (0, 4))

            for k in range(4):
                sp.dma_start(h[:, 4 * k:4 * k + 4, :], xT[4 * k * P:(4 * k + 4) * P, :].rearrange(
                    "(t p) n -> p t n", p=P)).then_inc(x_landed[k], 16)
                if k == 0:
                    sp.dma_start(params[:, :], par).then_inc(par_landed, 16)
                src = w_in[0, k * 4 * P:(k + 1) * 4 * P, 2 * DA:2 * DA + 256]
                load(k, 0, src.rearrange("(t p) n -> p t n", p=P))
            load_group(4, 0, w_in[0], 2 * DA + DB)
            for j, w in enumerate((w_rg_a, w_rg_x)):
                m = C_RG + j
                sp.wait_ge(lo_ready, m - NRAW + 1)
                dst = raw[:, m % NRAW, :, :].rearrange("p a (b n) -> p (a b) n", b=2)
                sp.dma_start(dst, w[0].rearrange("h i j -> i h j")).then_inc(raw_landed[m % NRAW], 16)
            with sp.Fori(1, 4) as i:
                load_group(C_REC, i, w_in[0], i * 256 + 2 * DA)
                load_group(C_REC + 4, i, w_in[0], i * 256 + 2 * DA + DB)
            with sp.Fori(0, 4) as i:
                load_group(C_GLU, i, w_in[0], i * 256)
                load_group(C_GLU + 4, i, w_in[0], i * 256 + DA)
            half_square(C_OUTB, w_out[0], DA)
            load_ple(C_PLE0, 0)
            half_square(C_OUTA, w_out[0], 0)
            mlp(0, C_MLP0)
            square(C_GATE0, w_gate[0])
            with sp.Fori(0, 4) as i:
                for s in range(2):
                    for part in range(3):
                        load_group(C_QKV + 12 * s + 4 * part, i * 3, w_qkv[0], i * 512 + (part * D + 256 * s))
            load_ple(C_PLE1, 1)
            square(C_OUT1, w_o[0])
            mlp(1, C_MLP1)
            square(C_GATE1, w_gate[1])
            for q in range(4):
                sp.wait_ge(out_ready, q + 1)
                sp.dma_start(outT[4 * q * P:(4 * q + 4) * P, :].rearrange("(t p) n -> p t n", p=P),
                             h[:, 4 * q:4 * q + 4, :]).then_inc(stored, 16)
            sp.wait_ge(stored, 64)

        @block.gpsimd
        def _(pool):
            pool.memset(onesD[:, :], 1.0 / D)
            pool.memset(onesA[:, :], 1.0 / DA)
            pool.memset(epsb[:, :], EPS)
            pool.memset(y2[:, 0:P], 1.0)
            pool.memset(glu[:, :, 0:PAD_A], 0.0)
            pool.memset(xrp[:, :, 0:PAD_B], 0.0)
            pool.memset(tl[:, 0, 0:P], -1.0)
            pool.memset(tl[:, 1, 0:P], 1.0).then_inc(consts_ready, 1)
            pool.wait_ge(consts_ready, 1)
            pool.affine_select(out=tl[:, 0, P:2 * P], in_=tl[:, 0, 0:P], compare_op=ALU.is_ge, fill=0.0, base=0,
                               pattern=[[-1, P]], channel_multiplier=1)
            pool.affine_select(out=ident[:, :], in_=y2[:, 0:P], compare_op=ALU.is_equal, fill=0.0, base=0,
                               pattern=[[-1, P]], channel_multiplier=1)
            pool.affine_select(out=mask[:, :], in_=tl[:, 1, 0:P], compare_op=ALU.is_gt, fill=0.0, base=0,
                               pattern=[[1, P]], channel_multiplier=-1).then_inc(consts_ready, 1)

        @block.tensor
        def _(pe):
            def gemm(g, gi, m, it, x, tiles=None, rows=(0, 4, 8, 12), tokens_out=False, mid=None, releases=1):
                b = 2 * (g % 2)
                if counts(g - 1, gi):
                    pe.wait_ge(sum_ready, gi + (g - 1))
                n_ = len(rows)
                for j in range(n_):
                    if mid is not None and j == n_ // 2:
                        mid()
                    if tiles is not None:
                        pe.wait_ge(*tiles[j])
                    pe.wait_ge(lo_ready, it * 8 + (m + j + 1))
                    w = spl[:, (m + j) % NSPL, :, :, :]
                    for q in range(4):
                        kt = rows[j] + q
                        first, last = j == 0 and q == 0, j == n_ - 1 and q == 3
                        for o in range(2):
                            c = slice(o * P, (o + 1) * P)
                            if tokens_out:
                                pe.matmul(ps[:, b + o, :], x[:, kt, 0, c], w[:, q, :, :], start=first, stop=False)
                                mm = pe.matmul(ps[:, b + o, 0:256], x[:, kt, 1, c], w[:, q, 0, :],
                                               start=False, stop=last)
                            else:
                                pe.matmul(ps[:, b + o, :], w[:, q, 0, c], x[:, kt, :, :], start=first, stop=False)
                                mm = pe.matmul(ps[:, b + o, 0:256], w[:, q, 1, c], x[:, kt, 0, :],
                                               start=False, stop=last)
                    mm.then_inc(chunk_used, releases if j == n_ - 1 else 1)

            def stats(n, columns=False):
                pe.wait_ge(sq_folded, 16 * (n + 1))
                if n > 0:
                    pe.wait_ge(rstd_ready, n)
                mm = pe.matmul(Z[:, 0, 0:256], onesD[:, :], nacc[:, :], start=True, stop=True)
                if columns:
                    for t in range(2):
                        mm = pe.matmul(Z[:, 0, 256 + t:257 + t], nacc[:, t * P:(t + 1) * P], onesD[:, 0:1],
                                       start=False, stop=True, skip_group_check=True)
                mm.then_inc(stat_ready, 1)

            def after_res(f):
                return [(res_tiles, f + 2 * j + 2) for j in range(4)]

            def ple(g, m, layer, units):
                for u in units:
                    c, b = m + 1 + u // 2, 2 * (u % 2)
                    pe.wait_ge(sum_ready, g + u - 1)
                    pe.wait_ge(lo_ready, c + 1)
                    for k in range(2):
                        x = spl[:, m % NSPL, 2 * layer + k, :, :]
                        for o in range(2):
                            w = spl[:, c % NSPL, 2 * k + u % 2, :, o * P:(o + 1) * P]
                            pe.matmul(ps[:, b + o, :], w[:, 0, :], x, start=(k == 0), stop=False)
                            mm = pe.matmul(ps[:, b + o, 0:256], w[:, 1, :], x[:, 0, :], start=False, stop=(k == 1))
                    if u < 7:
                        mm.then_inc(ple_done, 1)
                    else:
                        mm.then_inc(chunk_used, 5)

            def scores(pr, i, s):
                pe.wait_ge(qk_split, i * 6 + (3 * pr + 2))
                if counts(pr, i):
                    pe.wait_ge(logw_cut, i * 2 + pr)
                q, k = qk[s][:, 0, :, :, :], qk[s][:, 1, :, :, :]
                for e in range(2):
                    for kt, cols, qs in ((0, slice(0, 256), slice(0, 256)), (1, slice(256, 384), slice(P, 256))):
                        kc = slice(kt * P, (kt + 1) * P)
                        for n, (kh, qh) in enumerate(((0, 0), (0, 1), (1, 0))):
                            mm = pe.matmul(Z[:, e, cols], k[:, e, kh, kc], q[:, e, qh, qs],
                                           start=(n == 0 and kt == 0), stop=False, skip_group_check=True)
                mm.then_inc(z_ready, 1)

            def suffix_sums(pr, i):
                pe.wait_ge(soft_split, i * 2 + (pr + 1))
                for e in range(2):
                    for hl in range(2):
                        pe.matmul(Z[:, e, 0:384], ngtri[:, :], ws[:, e, hl, 0:384],
                                  start=False, stop=False, skip_group_check=True)
                        mm = pe.matmul(Z[:, e, P:256], ngone[:, :], ws[:, e, hl, 256:384],
                                       start=False, stop=(hl == 1), skip_group_check=True)
                mm.then_inc(logw_ready, 1)

            def values(pr, i, s):
                v = vv[s]
                pe.wait_ge(qk_split, i * 6 + (3 * pr + 3))
                pe.wait_ge(w_split, i * 2 + (pr + 1))
                if counts(pr, i):
                    pe.wait_ge(att_tiles, i * 2 + pr)
                for e in range(2):
                    hc = slice(e * P, (e + 1) * P)
                    for kt, cols, wc in ((0, slice(0, 256), slice(0, 256)), (1, slice(P, 256), slice(256, 384))):
                        for n, (vh, wh) in enumerate(((0, 0), (0, 1), (1, 0))):
                            mm = pe.matmul(O[:, e, cols], v[:, kt, vh, hc], ws[:, e, wh, wc],
                                           start=(n == 0 and kt == 0), stop=(n == 2 and kt == 1),
                                           skip_group_check=True)
                mm.then_inc(o_ready, 1)

            def first_pair(g, m, x, f_in, norm):
                gemm(g, 0, m, 0, x, after_res(f_in))
                stats(norm)
                gemm(g + 1, 0, m + 4, 0, x)

            def mlp(g, m, x, hid, f_in, norm, u):
                first_pair(g, m, x, f_in, norm)
                with pe.Fori(1, 4) as i:
                    for s in range(2):
                        gemm(g + s, i * 2, m + 4 * s, i, x)
                with pe.Fori(0, 4) as i:
                    for s in range(2):
                        gemm(g + 8 + s, i * 2, m + 32 + 4 * s, i, hid,
                             [(up_tiles, u + 2 * j + 2) for j in range(4)])
                with pe.Fori(1, 4) as f:
                    with pe.Fori(0, 4) as i:
                        for s in range(2):
                            gemm(g + s, f * 16 + i * 2, m + 4 * s, f * 8 + i, x)
                    with pe.Fori(0, 4) as i:
                        for s in range(2):
                            gemm(g + 8 + s, f * 16 + i * 2, m + 32 + 4 * s, f * 8 + i, hid,
                                 [(up_tiles, f * 8 + (u + 2 * j + 2)) for j in range(4)])

            def square(g, m, x, tiles):
                with pe.Fori(0, 4) as i:
                    for s in range(2):
                        gemm(g + s, i * 2, m + 4 * s, i, x, tiles)

            def after_norm(g, m, x, f_in, norm):
                first_pair(g, m, x, f_in, norm)
                with pe.Fori(1, 4) as i:
                    for s in range(2):
                        gemm(g + s, i * 2, m + 4 * s, i, x)

            pe.wait_ge(consts_ready, 1)
            gemm(G_REC, 0, 0, 0, XA, after_res(0))
            gemm(G_REC + 1, 0, 4, 0, XA, mid=lambda: stats(0), releases=3)

            def rg_head(pair, j):
                B = (Z, O)[j]
                if j == 0:
                    pe.wait_ge(xr_tiles, pair + 1)
                if pair > 0:
                    pe.wait_ge(rg_sum, 2 * pair + j - 1)
                for a in range(2):
                    x, w = XB[:, 8 + 2 * pair + j, :, :], wrg[:, a, pair, :, j * P:(j + 1) * P]
                    pe.matmul(B[:, a, :], w[:, 0, :], x, start=True, stop=False)
                    mm = pe.matmul(B[:, a, 0:256], w[:, 1, :], x[:, 0, :], start=False, stop=True)
                mm.then_inc(rg_done, 1)

            pe.wait_ge(lo_ready, C_RG + 2)
            for i in range(1, 4):
                for s in range(2):
                    gemm(G_REC + 2 * i + s, 0, C_REC + 8 * i + 4 * s, 0, XA)
                    rg_head(i - 1, s)
            rg_head(3, 0)
            rg_head(3, 1)

            def conv(pair, count, tap, n):
                if tap == 0:
                    pe.wait_ge(glu_ready, pair + 1)
                for k in range(tap, tap + n):
                    pe.wait_ge(dg_ready, count + (k + 1))
                    pe.matmul(O[:, 0, 0:256], dg[:, k % NDG, :], glu[:, bass.ds(pair * 2 + 1, 1), k:k + T],
                              start=(k == 0), stop=(k == CA_PE - 1), skip_group_check=True).then_inc(dg_used, 1)

            gemm(G_GLU, 0, C_GLU, 0, XA)
            pe.wait_ge(rg_sum, 8)
            gemm(G_GLU + 1, 0, C_GLU + 4, 0, XA)
            with pe.Fori(1, 4) as c:
                for s in range(2):
                    def taps(tap):
                        conv(c - 1, c * CA_PE - CA_PE, tap, 8)

                    gemm(G_GLU + s, c * 2, C_GLU + 4 * s, c, XA, mid=None if s == 0 else lambda: taps(8))
                    taps(16 * s)
            def ln_mean(n):
                pe.wait_ge(ln_part, n)
                pe.matmul(Z[:, 0, 0:256], onesA[:, :], nacc[:, :], start=True, stop=True).then_inc(ln_stat, 1)

            for s in range(NG):
                gemm(G_OUTB + s, 0, C_OUTB + 2 * s, 0, XB, [(yb_tiles, 1)] * 2, (8, 12))
                if s < 4:
                    conv(3, 3 * CA_PE, 6 * s, 6)
                if s == 4:
                    ln_mean(1)
                if s == 6:
                    ln_mean(2)
            ple(G_PLE0, C_PLE0, 0, range(8))
            with pe.Fori(0, 2) as i:
                for s in range(4):
                    gemm(G_OUTA + s, i * 4, C_OUTA + 2 * s, i, XB, [(ya_tiles, 1), (ya_tiles, 2)], (0, 4))
            mlp(G_MLP0, C_MLP0, XA, XB, 8, 1, 0)
            after_norm(G_GATE0, C_GATE0, XA, 16, 2)

            def pair(s, i, first):
                g, m = G_QKV + 3 * s, C_QKV + 12 * s
                gemm(g, i * 6, m, i * 3, XB, after_res(24) if first else None)
                if first:
                    stats(3, columns=True)
                gemm(g + 1, i * 6, m + 4, i * 3, XB, mid=None if first else lambda: suffix_sums(s - 1, i))
                gemm(g + 2, i * 6, m + 8, i * 3, XB, tokens_out=True,
                     mid=None if first else lambda: values(s - 1, i, (s - 1) % 2))
                scores(s, i, s)

            pair(0, 0, True)
            pair(1, 0, False)
            with pe.Fori(1, 4) as i:
                pair(0, i, False)
                pair(1, i, False)
            ple(G_PLE1, C_PLE1, 1, range(4))
            suffix_sums(7, 0)
            ple(G_PLE1, C_PLE1, 1, range(4, 8))
            values(7, 0, 1)
            square(G_OUT1, C_OUT1, XA, [(att_tiles, 2 * j + 2) for j in range(4)])
            mlp(G_MLP1, C_MLP1, XB, XA, 32, 4, 32)
            after_norm(G_GATE1, C_GATE1, XB, 40, 5)
            stats(6)

        @block.scalar
        def _(act):
            def copy(out, in_, scale=1.0):
                return act.activation(out, in_, ACT.Copy, scale=scale)

            def split(m, it=0):
                if m < CHUNKS:
                    act.wait_ge(raw_landed[m % NRAW], it * (16 * 8 // NRAW) + 16 * (m // NRAW + 1))
                    if counts(m - NSPL + 1, it):
                        act.wait_ge(chunk_used, it * 8 + (m - NSPL + 1))
                    copy(spl[:, m % NSPL, :, 0, :], raw[:, m % NRAW, :, :]).then_inc(hi_ready, 1)

            def period(m, it, k=4):
                for q in range(k):
                    split(m + NSPL + q, it)

            def split_rg(j):
                m = C_RG + j
                act.wait_ge(raw_landed[m % NRAW], 16 * (m // NRAW + 1))
                copy(wrg[:, j, :, 0, :], raw[:, m % NRAW, :, :]).then_inc(hi_ready, 1)

            def take_cross(g, gi, ready):
                if counts(g, gi):
                    act.wait_ge(sum_ready, gi + g)
                act.wait_ge(*ready)
                b = 2 * (g % 2)
                copy(cross[:, :, :], ps[:, b:b + 2, 256:512]).then_inc(cross_copied, 1)

            def group_done(m, it):
                return chunk_used, it * 8 + (m + 4)

            def norm(n, columns=False):
                act.wait_ge(stat_ready, n + 1)
                r = act.activation(rB[:, :], Z[:, 0, 0:256], ACT.Sqrt, bias=epsb[:, :])
                if columns:
                    r = act.activation(rC[:, :], Z[:, 0, 256:258], ACT.Sqrt, bias=epsb[:, :])
                r.then_inc(root_ready, 1)

            def squares(t0):
                act.activation(tv[:, :, :], h[:, bass.ds(t0, 2), :], ACT.Square).then_inc(sq_ready, 1)

            def res_his(t0, n, X):
                for j in range(2):
                    r = act.activation(X[:, bass.ds(t0 + j, 1), 0, :], h[:, bass.ds(t0 + j, 1), :], ACT.Identity,
                                       scale=gain(n, t0 + j))
                r.then_inc(res_hi, 1)

            def residual(hidx, t0, n, X):
                act.wait_ge(res_ready, hidx + 1)
                squares(t0)
                if X is not None:
                    res_his(t0, n, X)
                else:
                    act.wait_ge(sq_ready, hidx - 47)
                    for j in range(2):
                        hj = h[:, bass.ds(t0 + j, 1), :]
                        r = act.activation(hj, hj, ACT.Identity, scale=gain(n, t0 + j))
                    r.then_inc(out_scaled, 1)

            def up(g, gi, m, it, u, t0, hid, norm_n=None):
                period(m, it)
                take_cross(g, gi, group_done(m, it))
                if norm_n is not None:
                    norm(norm_n)
                act.wait_ge(up_relu, u + 1)
                act.activation(tv[:, :, :], tv[:, :, :], ACT.Square).then_inc(up_sq, 1)
                act.wait_ge(up_sq, u + 1)
                copy(hid[:, bass.ds(t0, 2), 0, :], tv[:, :, :]).then_inc(up_hi, 1)

            def down(g, gi, m, it):
                period(m, it)
                take_cross(g, gi, group_done(m, it))

            def gate(g, gi, m, it, k, hidx, t0, n, X, norm_n=None):
                period(m, it)
                take_cross(g, gi, group_done(m, it))
                if norm_n is not None:
                    norm(norm_n)
                act.wait_ge(gate_scaled, k + 1)
                act.activation(tv[:, :, :], tv[:, :, :], ACT.Sigmoid).then_inc(gate_sig, 1)
                residual(hidx, t0, n, X)

            def out_groups(g, m, hidx, n, X):
                with act.Fori(0, 4) as i:
                    for s in range(2):
                        period(m + 4 * s, i)
                        take_cross(g + s, i * 2, group_done(m + 4 * s, i))
                        residual(i * 2 + (hidx + s), i * 4 + 2 * s, n, X)

            def mlp(g, m, u, hidx, norm_in, hid, n, X):
                for s in range(2):
                    up(g + s, 0, m + 4 * s, 0, u + s, 2 * s, hid, norm_in if s == 0 else None)
                with act.Fori(1, 4) as i:
                    for s in range(2):
                        up(g + s, i * 2, m + 4 * s, i, i * 2 + (u + s), i * 4 + 2 * s, hid)
                with act.Fori(0, 4) as i:
                    for s in range(2):
                        down(g + 8 + s, i * 2, m + 32 + 4 * s, i)
                with act.Fori(1, 3) as f:
                    with act.Fori(0, 4) as i:
                        for s in range(2):
                            up(g + s, f * 16 + i * 2, m + 4 * s, f * 8 + i, f * 8 + i * 2 + (u + s),
                               i * 4 + 2 * s, hid)
                    with act.Fori(0, 4) as i:
                        for s in range(2):
                            down(g + 8 + s, f * 16 + i * 2, m + 32 + 4 * s, f * 8 + i)
                g, m, u, hidx = g + 48, m + 192, u + 24, hidx + 24
                with act.Fori(0, 4) as i:
                    for s in range(2):
                        up(g + s, i * 2, m + 4 * s, i, i * 2 + (u + s), i * 4 + 2 * s, hid)
                out_groups(g + 8, m + 32, hidx, n, X)

            def gates(g, m, k, hidx, norm_in, n, X):
                for s in range(2):
                    gate(g + s, 0, m + 4 * s, 0, k + s, hidx + s, 2 * s, n, X, norm_in if s == 0 else None)
                with act.Fori(1, 3) as i:
                    for s in range(2):
                        gate(g + s, i * 2, m + 4 * s, i, i * 2 + (k + s), i * 2 + (hidx + s), i * 4 + 2 * s, n, X)
                for s in range(2):
                    gate(g + 6 + s, 0, m + 24 + 4 * s, 0, k + 6 + s, hidx + 6 + s, 12 + 2 * s, n, X)

            act.wait_ge(consts_ready, 2)
            act.wait_ge(par_landed, 16)
            for f in range(8):
                act.wait_ge(x_landed[f // 2], 16)
                res_his(2 * f, 0, XA)
                if f % 2 == 0:
                    split(f // 2)
            act.activation(small[:, 0, :], params[:, LAMBDA:LAMBDA + 8], ACT.Abs).then_inc(lam_abs, 1)
            act.wait_ge(lam_abs, 1)
            act.activation(small[:, 1, :], small[:, 0, :], ACT.Exp, scale=-1.0).then_inc(lam_exp, 1)
            for f in range(8):
                if f >= 1:
                    act.wait_ge(sq_folded, 2 * f)
                squares(2 * f)
                if f % 2 == 1:
                    split(4 + f // 2)

            def round_x(c):
                act.wait_ge(xr_step, c * 9 + 9)
                copy(XB[:, bass.ds(c * 2 + 8, 2), 0, :], pp[:, bass.ds(c * 2, 2), :]).then_inc(xr_hi, 1)

            def gelu_gate(c):
                act.wait_ge(gr_scaled, c + 1)
                act.activation(pp[:, bass.ds(c * 2 + 8, 2), :], tv[:, :, :], ACT.Gelu_apprx_tanh).then_inc(gr_ready, 1)

            def head_cross(pair, j, sums):
                act.wait_ge(rg_done, pair * 2 + (j + 1))
                act.wait_ge(*sums)
                copy(cross[:, :, :], (Z, O)[j][:, :, 256:512]).then_inc(rg_cross, 1)

            def head_sigmoids(pair):
                act.wait_ge(rg_sum, pair * 2 + 2)
                for j in range(2):
                    for a, bias in enumerate((RG_BA, RG_BX)):
                        o = rg[:, bass.ds(pair * 2 + j, 1), a, :]
                        r = act.activation(o, o, ACT.Sigmoid, bias=par_col(pair * 2 + (bias + j)))
                r.then_inc(rg_act, 1)

            def rec_pair(c):
                m = C_REC + NSPL
                split(m, c)
                if not isinstance(c, int):
                    head_sigmoids(c - 2)
                for q in range(1, 4):
                    split(m + q, c)
                take_cross(G_REC, c * 2, group_done(C_REC, c))
                for q in range(4, 6):
                    split(m + q, c)
                round_x(c)
                head_cross(c - 1, 0, (sum_ready, c * 2 + 1))
                for q in range(6, 8):
                    split(m + q, c)
                act.wait_ge(rg_sum, c * 2 - 1)
                take_cross(G_REC + 1, c * 2, group_done(C_REC + 4, c))
                gelu_gate(c)
                head_cross(c - 1, 1, (sum_ready, c * 2 + 2))

            for j in range(2):
                split_rg(j)
            for m in (10, 11):
                split(m)
            take_cross(G_REC, 0, (chunk_used, 4))
            norm(0)
            round_x(0)
            for m in range(12, 18):
                split(m)
            take_cross(G_REC + 1, 0, (chunk_used, 8))
            gelu_gate(0)
            rec_pair(1)
            with act.Fori(2, 4) as c:
                rec_pair(c)
            head_sigmoids(2)
            head_cross(3, 0, (rg_sum, 6))
            head_cross(3, 1, (rg_sum, 7))
            head_sigmoids(3)

            def rg_exp():
                act.wait_ge(rg_act, 4)
                act.wait_ge(lam_chain, LAM_STEPS)
                for t in range(8):
                    r = act.activation(dec[:, t, :], rg[:, t, 0, :], ACT.Exp, scale=nlamc[:, t:t + 1])
                r.then_inc(rg_act, 1)

            def rg_tanh():
                for t in range(8):
                    r = act.activation(mlt[:, t, :], rg[:, t, 0, :], ACT.Tanh, scale=lamc[:, t:t + 1])
                r.then_inc(rg_act, 1)

            def glu_gate(c):
                act.wait_ge(glu_scaled, c + 1)
                act.activation(tv[:, :, :], tv[:, :, :], ACT.Sigmoid).then_inc(glu_sig, 1)

            rg_exp()
            split(C_GLU + NSPL)
            rg_tanh()
            split(C_GLU + NSPL + 1)
            split(C_GLU + NSPL + 2)
            split(C_GLU + NSPL + 3)
            take_cross(G_GLU, 0, group_done(C_GLU, 0))
            act.wait_ge(rg_vec, 3)
            act.activation(mlt[:, :, :], mlt[:, :, :], ACT.Sqrt).then_inc(rg_act, 1)
            period(C_GLU + 4, 0)
            take_cross(G_GLU + 1, 0, group_done(C_GLU + 4, 0))
            glu_gate(0)
            act.wait_ge(rg_vec, 6)
            copy(XB[:, 8:16, 0, :], pp[:, 0:8, :]).then_inc(rg_act, 1)

            def tap_matrices(pair, count, tap, n):
                if tap == 0 and (not isinstance(pair, int) or pair > 0):
                    act.wait_ge(dg_used, count)
                for k in range(tap, tap + n):
                    if k >= NDG:
                        act.wait_ge(dg_used, count + (k + 1 - NDG))
                    act.activation(dg[:, k % NDG, :], ident[:, :], ACT.Copy,
                                   scale=par_col((pair * 2 + 1) * CA + (CONV_A_W + k))).then_inc(dg_ready, 1)

            def glu_pair(c):
                for q in range(8):
                    tap_matrices(c - 1, c * CA_PE - CA_PE, 3 * q, 3)
                    split(C_GLU + NSPL + q, c)
                    if q % 4 == 3:
                        take_cross(G_GLU + q // 4, c * 2, group_done(C_GLU + q - 3, c))
                glu_gate(c)

            glu_pair(1)
            with act.Fori(2, 4) as c:
                glu_pair(c)

            def ple_cross(g, m, layer, units):
                for u in units:
                    take_cross(g + u, 0, (ple_done, 7 * layer + u + 1) if u < 7 else (chunk_used, m + 5))

            for s in range(NG):
                if s < 4:
                    tap_matrices(3, 3 * CA_PE, 6 * s, 6)
                period(C_OUTB + 2 * s, 0, 2)
                take_cross(G_OUTB + s, 0, (chunk_used, C_OUTB + 2 * s + 2))
                if s == 5:
                    act.wait_ge(ln_vec, 1)
                    act.activation(dec[:, :, :], y[:, :, :], ACT.Square).then_inc(ln_act, 1)
            act.wait_ge(ln_stat, 2)
            act.activation(nacc[:, :], Z[:, 0, 0:256], ACT.Sqrt, bias=epsb[:, :]).then_inc(ln_act, 1)
            ple_cross(G_PLE0, C_PLE0, 0, range(3))
            for k in range(2):
                act.wait_ge(ln_vec, 3 + k)
                for t in range(4 * k, 4 * k + 4):
                    r = act.activation(y[:, t, :], y[:, t, :], ACT.Silu, scale=par_col(LN_G + t), bias=par_col(LN_B + t))
                    if t == 4 * k + 1:
                        ple_cross(G_PLE0, C_PLE0, 0, (3 + 2 * k,))
                r.then_inc(ln_act, 1)
                act.wait_ge(ln_act, 3 + 2 * k)
                copy(XB[:, 4 * k:4 * k + 4, 0, :], y[:, 4 * k:4 * k + 4, :]).then_inc(ln_act, 1)
                ple_cross(G_PLE0, C_PLE0, 0, (4 + 2 * k,))
            ple_cross(G_PLE0, C_PLE0, 0, (7,))
            period(C_PLE0, 0, 5)

            with act.Fori(0, 2) as i:
                for s in range(4):
                    m = C_OUTA + 2 * s
                    take_cross(G_OUTA + s, i * 4, (chunk_used, i * 8 + (m + 2)))
                    split(m + NSPL, i)
                    act.wait_ge(res_ready, i * 4 + (H_OUTA + s + 1))
                    squares(i * 8 + 2 * s)
                    split(m + NSPL + 1, i)
                    res_his(i * 8 + 2 * s, 1, XA)
            mlp(G_MLP0, C_MLP0, 0, H_MLP0, 1, XB, 2, XA)
            gates(G_GATE0, C_GATE0, 0, H_GATE0, 2, 3, XB)

            def soft_exp(pr, i):
                act.wait_ge(z_ready, i * 2 + (pr + 1))
                act.activation(te[:, :, :], Z[:, :, 0:384], ACT.Abs).then_inc(z_abs, 1)
                act.wait_ge(z_abs, i * 2 + (pr + 1))
                act.activation(te[:, :, :], te[:, :, :], ACT.Exp, scale=-1.0).then_inc(z_exp, 1)
                act.wait_ge(z_exp, i * 2 + (pr + 1))
                act.activation(te[:, :, :], te[:, :, :], ACT.Ln, bias=1.0).then_inc(z_log, 1)

            def soft_round(pr, i):
                act.wait_ge(soft_ready, i * 2 + (pr + 1))
                copy(ws[:, :, 0, :], tl[:, :, :]).then_inc(soft_hi, 1)

            def weights_exp(pr, i):
                act.wait_ge(logw_cut, i * 2 + (pr + 1))
                act.activation(tl[:, :, :], te[:, :, :], ACT.Exp).then_inc(w_exp, 1)

            def weights_round(pr, i):
                act.wait_ge(w_ready, i * 2 + (pr + 1))
                copy(ws[:, :, 0, :], tl[:, :, :]).then_inc(w_hi, 1)

            def out_round(pr, i):
                act.wait_ge(o_ready, i * 2 + (pr + 1))
                copy(XA[:, bass.ds(i * 4 + 2 * pr, 2), 0, :], O[:, :, 0:256]).then_inc(o_hi, 1)

            def qkv(part, s, i, first=False):
                g, m = G_QKV + 3 * s + part, C_QKV + 12 * s + 4 * part
                steps = ((soft_exp, soft_round, None, None), (None, None, weights_exp, weights_round),
                         (None, None, None, out_round))[part]
                for q in range(4):
                    if steps[q] is not None and not first:
                        steps[q](s - 1, i)
                    split(m + NSPL + q, i * 3)
                take_cross(g, i * 6, group_done(m, i * 3))
                if first and part == 0:
                    norm(3, columns=True)
                act.wait_ge(qk_scaled, i * 6 + (3 * s + part + 1))
                out = vv[s][:, :, 0, :] if part == 2 else qk[s][:, part, :, 0, :]
                copy(out, tv[:, :, :]).then_inc(qk_hi, 1)

            for s in range(2):
                for part in range(3):
                    qkv(part, s, 0, first=(s == 0))
            with act.Fori(1, 4) as i:
                for s in range(2):
                    for part in range(3):
                        qkv(part, s, i)
            soft_exp(7, 0)
            ple_cross(G_PLE1, C_PLE1, 1, range(2))
            soft_round(7, 0)
            ple_cross(G_PLE1, C_PLE1, 1, range(2, 4))
            weights_exp(7, 0)
            ple_cross(G_PLE1, C_PLE1, 1, range(4, 6))
            weights_round(7, 0)
            ple_cross(G_PLE1, C_PLE1, 1, range(6, 8))
            period(C_PLE1, 0, 5)
            out_round(7, 0)

            out_groups(G_OUT1, C_OUT1, H_OUT1, 4, XB)
            mlp(G_MLP1, C_MLP1, 32, H_MLP1, 4, XA, 5, XB)
            gates(G_GATE1, C_GATE1, 8, H_GATE1, 5, 6, None)
            norm(6)

        @block.vector
        def _(dve):
            def split(m, it=0):
                if m < CHUNKS:
                    dve.wait_ge(hi_ready, it * 8 + (m + 1))
                    s = spl[:, m % NSPL, :, :, :]
                    dve.tensor_tensor(s[:, :, 1, :], raw[:, m % NRAW, :, :], s[:, :, 0, :].bitcast(F32),
                                      ALU.subtract).then_inc(lo_ready, 1)

            def split_rg(j):
                m = C_RG + j
                dve.wait_ge(hi_ready, m + 1)
                s = wrg[:, j, :, :, :]
                dve.tensor_tensor(s[:, :, 1, :], raw[:, m % NRAW, :, :], s[:, :, 0, :].bitcast(F32),
                                  ALU.subtract).then_inc(lo_ready, 1)

            def period(m, it, k=4):
                for q in range(k):
                    split(m + NSPL + q, it)

            def lo_of(X, t0, n, v):
                return dve.tensor_tensor(X[:, bass.ds(t0, n), 1, :], v, X[:, bass.ds(t0, n), 0, :].bitcast(F32),
                                         ALU.subtract)

            def take_sum(g, gi, out=None):
                b = 2 * (g % 2)
                dve.wait_ge(cross_copied, gi + (g + 1))
                dve.tensor_tensor(tv[:, :, :] if out is None else out, cross[:, :, :], ps[:, b:b + 2, 0:256],
                                  ALU.add).then_inc(sum_ready, 1)

            def scaled(g, gi, out, done):
                dve.wait_ge(sum_ready, gi + (g + 1))
                dve.tensor_tensor(out, tv[:, :, :], bcast(rB[:, :], 2), ALU.mult).then_inc(done, 1)

            def norm(n, columns=False):
                dve.wait_ge(root_ready, n + 1)
                r = dve.reciprocal(rB[:, :], rB[:, :])
                if columns:
                    r = dve.reciprocal(rC[:, :], rC[:, :])
                r.then_inc(rstd_ready, 1)
                dve.wait_ge(rstd_ready, n + 1)

            def clear(n):
                if n >= 1:
                    dve.wait_ge(stat_ready, n)
                dve.memset(nacc[:, :], 0.0).then_inc(nacc_clear, 1)
                dve.wait_ge(nacc_clear, n + 1)

            def fold(f):
                dve.wait_ge(sq_ready, f + 1)
                dve.tensor_tensor(tv[:, 0, :], tv[:, 0, :], tv[:, 1, :], ALU.add).then_inc(sq_folded, 1)
                dve.wait_ge(sq_folded, f * 2 + 1)
                dve.tensor_tensor(nacc[:, :], nacc[:, :], tv[:, 0, :], ALU.add).then_inc(sq_folded, 1)
                dve.wait_ge(sq_folded, f * 2 + 2)

            def res_los(f, t0, n, X):
                dve.wait_ge(res_hi, f + 1)
                for j in range(2):
                    r = dve.scalar_tensor_tensor(
                        out=X[:, bass.ds(t0 + j, 1), 1, :], in0=h[:, bass.ds(t0 + j, 1), :], scalar=gain(n, t0 + j),
                        in1=X[:, bass.ds(t0 + j, 1), 0, :].bitcast(F32), op0=ALU.mult, op1=ALU.subtract)
                r.then_inc(res_tiles, 1)

            def add_h(hidx, t0, first=False):
                if not first:
                    dve.wait_ge(res_ready, hidx - 7)
                ht = h[:, bass.ds(t0, 2), :]
                dve.tensor_tensor(ht, ht, tv[:, :, :], ALU.add).then_inc(res_ready, 1)
                dve.wait_ge(res_ready, hidx + 1)

            def residual(f, t0, n, X):
                fold(f)
                if X is not None:
                    res_los(f, t0, n, X)

            def up(g, gi, m, it, u, t0, hid, norm_n=None):
                period(m, it)
                take_sum(g, gi)
                if norm_n is not None:
                    norm(norm_n)
                dve.wait_ge(sum_ready, gi + (g + 1))
                dve.scalar_tensor_tensor(out=tv[:, :, :], in0=tv[:, :, :], scalar=0.0, in1=bcast(rB[:, :], 2),
                                         op0=ALU.max, op1=ALU.mult).then_inc(up_relu, 1)
                dve.wait_ge(up_hi, u + 1)
                lo_of(hid, t0, 2, tv[:, :, :]).then_inc(up_tiles, 1)
                dve.wait_ge(up_tiles, u + 1)

            def down(g, gi, m, it, hidx, t0):
                period(m, it)
                take_sum(g, gi)
                dve.wait_ge(sum_ready, gi + (g + 1))
                add_h(hidx, t0)

            def gate(g, gi, m, it, k, f, hidx, t0, n, X, norm_n=None):
                period(m, it)
                take_sum(g, gi)
                if norm_n is not None:
                    norm(norm_n)
                    clear(n)
                scaled(g, gi, tv[:, :, :], gate_scaled)
                dve.wait_ge(gate_sig, k + 1)
                dve.tensor_tensor(tv[:, :, :], tv[:, :, :], pp[:, bass.ds(t0, 2), :], ALU.mult).then_inc(gate_mul, 1)
                dve.wait_ge(gate_mul, k + 1)
                add_h(hidx, t0)
                residual(f, t0, n, X)

            def out_groups(g, m, hidx, f, n, X):
                clear(n)
                with dve.Fori(0, 4) as i:
                    for s in range(2):
                        down(g + s, i * 2, m + 4 * s, i, i * 2 + (hidx + s), i * 4 + 2 * s)
                        residual(i * 2 + (f + s), i * 4 + 2 * s, n, X)

            def mlp(g, m, u, hidx, norm_in, hid, f_out, n, X):
                for s in range(2):
                    up(g + s, 0, m + 4 * s, 0, u + s, 2 * s, hid, norm_in if s == 0 else None)
                with dve.Fori(1, 4) as i:
                    for s in range(2):
                        up(g + s, i * 2, m + 4 * s, i, i * 2 + (u + s), i * 4 + 2 * s, hid)
                with dve.Fori(0, 4) as i:
                    for s in range(2):
                        down(g + 8 + s, i * 2, m + 32 + 4 * s, i, i * 2 + (hidx + s), i * 4 + 2 * s)
                with dve.Fori(1, 3) as f:
                    with dve.Fori(0, 4) as i:
                        for s in range(2):
                            up(g + s, f * 16 + i * 2, m + 4 * s, f * 8 + i, f * 8 + i * 2 + (u + s),
                               i * 4 + 2 * s, hid)
                    with dve.Fori(0, 4) as i:
                        for s in range(2):
                            down(g + 8 + s, f * 16 + i * 2, m + 32 + 4 * s, f * 8 + i,
                                 f * 8 + i * 2 + (hidx + s), i * 4 + 2 * s)
                g, m, u, hidx = g + 48, m + 192, u + 24, hidx + 24
                with dve.Fori(0, 4) as i:
                    for s in range(2):
                        up(g + s, i * 2, m + 4 * s, i, i * 2 + (u + s), i * 4 + 2 * s, hid)
                out_groups(g + 8, m + 32, hidx, f_out, n, X)

            def gates(g, m, k, f, hidx, norm_in, n, X):
                for s in range(2):
                    gate(g + s, 0, m + 4 * s, 0, k + s, f + s, hidx + s, 2 * s, n, X, norm_in if s == 0 else None)
                with dve.Fori(1, 3) as i:
                    for s in range(2):
                        gate(g + s, i * 2, m + 4 * s, i, i * 2 + (k + s), i * 2 + (f + s), i * 2 + (hidx + s),
                             i * 4 + 2 * s, n, X)
                for s in range(2):
                    gate(g + 6 + s, 0, m + 24 + 4 * s, 0, k + 6 + s, f + 6 + s, hidx + 6 + s, 12 + 2 * s, n, X)

            lam = params[:, LAMBDA:LAMBDA + 8]
            poly, e_, s2, s1 = (small[:, j, :] for j in range(4))
            steps = [0]

            def link(ins):
                steps[0] += 1
                ins.then_inc(lam_chain, 1)
                dve.wait_ge(lam_chain, steps[0])

            dve.wait_ge(par_landed, 16)
            dve.wait_ge(consts_ready, 2)
            dve.tensor_copy(ngtri[:, :], tl[:, 0, P:2 * P])
            dve.tensor_copy(ngone[:, :], tl[:, 0, 0:P])
            clear(0)
            for f in range(8):
                res_los(f, 2 * f, 0, XA)
                if f % 2 == 0:
                    split(f // 2)
            for f in range(8):
                fold(f)
                if f % 2 == 1:
                    split(4 + f // 2)
            dve.wait_ge(lam_exp, 1)
            link(dve.tensor_scalar(s2, e_, 2.0, None, ALU.add))
            link(dve.reciprocal(s2, s2))
            link(dve.tensor_tensor(s1, e_, s2, ALU.mult))
            link(dve.tensor_tensor(s2, s1, s1, ALU.mult))
            link(dve.tensor_scalar(poly, s2, 1.0 / 17, None, ALU.mult))
            for k in (15, 13, 11, 9, 7, 5, 3):
                link(dve.scalar_tensor_tensor(out=poly, in0=poly, scalar=1.0 / k, in1=s2, op0=ALU.add, op1=ALU.mult))
            link(dve.scalar_tensor_tensor(out=poly, in0=poly, scalar=1.0, in1=s1, op0=ALU.add, op1=ALU.mult))
            link(dve.tensor_scalar(s2, lam, 0.0, -1.0, ALU.min, ALU.mult))
            link(dve.scalar_tensor_tensor(out=s1, in0=poly, scalar=2.0, in1=s2, op0=ALU.mult, op1=ALU.add))
            link(dve.tensor_scalar(lamc[:, :], s1, 8.0, None, ALU.mult))
            link(dve.tensor_scalar(nlamc[:, :], s1, -8.0, None, ALU.mult))
            assert steps[0] == LAM_STEPS

            def short_conv(c):
                for n in range(2 * CB):
                    k, j = n // 2, n % 2
                    dve.wait_ge(xr_step, c * 9 + (1 if n < 2 else n))
                    t = c * 2 + j
                    x, w = xrp[:, j, k:k + T].unsqueeze(1), par_col(t * CB + (CONV_B_W + k))
                    o = pp[:, bass.ds(t, 1), :]
                    if k == 0:
                        r = dve.tensor_scalar(o, x, w, par_col(t + CONV_B_B), ALU.mult, ALU.add)
                    else:
                        r = dve.scalar_tensor_tensor(out=o, in0=x, scalar=w, in1=o, op0=ALU.mult, op1=ALU.add)
                    r.then_inc(xr_step, 1)

            def x_value(c):
                take_sum(G_REC, c * 2)
                if isinstance(c, int) and c == 0:
                    norm(0)
                scaled(G_REC, c * 2, xrp[:, :, PAD_B:PAD_B + T], xr_step)
                short_conv(c)

            def x_rest(c):
                dve.wait_ge(xr_hi, c + 1)
                lo_of(XB, c * 2 + 8, 2, pp[:, bass.ds(c * 2, 2), :]).then_inc(xr_tiles, 1)

            def gate_value(c):
                take_sum(G_REC + 1, c * 2)
                scaled(G_REC + 1, c * 2, tv[:, :, :], gr_scaled)

            def head_sum(pair, j):
                dve.wait_ge(rg_cross, pair * 2 + (j + 1))
                dve.tensor_tensor(rg[:, bass.ds(pair * 2 + j, 1), :, :], cross[:, :, :].unsqueeze(1),
                                  (Z, O)[j][:, :, 0:256].unsqueeze(1), ALU.add).then_inc(rg_sum, 1)

            def rec_pair(c):
                period(C_REC, c)
                dve.wait_ge(gr_ready, c)
                x_value(c)
                for q in range(4, 6):
                    split(C_REC + NSPL + q, c)
                x_rest(c)
                head_sum(c - 1, 0)
                for q in range(6, 8):
                    split(C_REC + NSPL + q, c)
                gate_value(c)
                head_sum(c - 1, 1)

            for j in range(2):
                split_rg(j)
            for m in (10, 11):
                split(m)
            x_value(0)
            x_rest(0)
            for m in range(12, 18):
                split(m)
            gate_value(0)
            with dve.Fori(1, 4) as c:
                rec_pair(c)
            head_sum(3, 0)
            head_sum(3, 1)

            def glu_value(c):
                take_sum(G_GLU, c * 2)
                scaled(G_GLU, c * 2, glu[:, bass.ds(c * 2, 2), PAD_A:], glu_val)
                dve.wait_ge(glu_val, c + 1)

            def glu_gate(c, meanwhile=None):
                take_sum(G_GLU + 1, c * 2)
                scaled(G_GLU + 1, c * 2, tv[:, :, :], glu_scaled)
                if meanwhile is not None:
                    meanwhile()
                dve.wait_ge(glu_sig, c + 1)
                gl = glu[:, bass.ds(c * 2, 2), PAD_A:]
                dve.tensor_tensor(gl, gl, tv[:, :, :], ALU.mult).then_inc(glu_ready, 1)
                dve.wait_ge(glu_ready, c + 1)

            r_, i_ = rg[:, :, 0, :], rg[:, :, 1, :]
            dve.wait_ge(gr_ready, 4)
            dve.wait_ge(rg_act, 4)
            dve.tensor_tensor(i_, i_, pp[:, 0:8, :], ALU.mult).then_inc(rg_vec, 1)
            split(C_GLU + NSPL)
            dve.wait_ge(rg_act, 6)
            dve.tensor_tensor(r_, dec[:, :, :], dec[:, :, :], ALU.mult).then_inc(rg_vec, 1)
            split(C_GLU + NSPL + 1)
            dve.wait_ge(rg_vec, 2)
            dve.scalar_tensor_tensor(out=mlt[:, :, :], in0=r_, scalar=1.0, in1=mlt[:, :, :],
                                     op0=ALU.add, op1=ALU.mult).then_inc(rg_vec, 1)
            split(C_GLU + NSPL + 2)
            split(C_GLU + NSPL + 3)
            glu_value(0)
            split(C_GLU + 4 + NSPL)
            dve.wait_ge(rg_act, 7)
            dve.tensor_tensor(i_, i_, mlt[:, :, :], ALU.mult).then_inc(rg_vec, 1)
            split(C_GLU + 4 + NSPL + 1)
            dve.wait_ge(rg_vec, 4)
            for t in range(8):
                r = dve.tensor_tensor_scan(rg[:, t, 0, :], dec[:, t, :], rg[:, t, 1, :], 0.0, ALU.mult, ALU.add)
            r.then_inc(rg_vec, 1)
            split(C_GLU + 4 + NSPL + 2)
            split(C_GLU + 4 + NSPL + 3)
            glu_gate(0)
            dve.wait_ge(rg_vec, 5)
            dve.tensor_tensor(pp[:, 0:8, :], r_, pp[:, 8:16, :], ALU.mult).then_inc(rg_vec, 1)
            dve.wait_ge(rg_act, 8)
            lo_of(XB, 8, 8, pp[:, 0:8, :]).then_inc(yb_tiles, 1)

            def conv(pair, base, q):
                first, y2t, second = y[:, bass.ds(pair * 2, 1), :], y2[:, :].unsqueeze(1), y[:, bass.ds(pair * 2 + 1, 1), :]

                def step(n):
                    return n + n // 4

                if q == 0:
                    dve.wait_ge(glu_ready, pair + 1)
                for n in range(4 * q, 4 * q + 4):
                    o = (first, y2t)[n % 2]
                    if n < CA:
                        x, w = glu[:, bass.ds(pair * 2, 1), n:n + T], par_col(pair * (2 * CA) + (CONV_A_W + n))
                    if n >= 2:
                        dve.wait_ge(conv_step, base + step(n - 2 if n < CA else n - 1) + 1)
                    if n == 0:
                        r = dve.tensor_scalar(o, x, w, par_col(pair * 2 + CONV_A_B), ALU.mult, ALU.add)
                    elif n == 1:
                        r = dve.tensor_scalar(o, x, w, None, ALU.mult)
                    elif n < CA:
                        r = dve.scalar_tensor_tensor(out=o, in0=x, scalar=w, in1=o, op0=ALU.mult, op1=ALU.add)
                    else:
                        r = dve.tensor_tensor(first, first, y2t, ALU.add)
                    r.then_inc(conv_step, 1)
                if q < 7:
                    k = CA_PE + q
                    x, w = glu[:, bass.ds(pair * 2 + 1, 1), k:k + T], par_col(pair * (2 * CA) + (CONV_A_W + CA + k))
                    if q == 0:
                        r = dve.tensor_scalar(second, x, w, par_col(pair * 2 + (1 + CONV_A_B)), ALU.mult, ALU.add)
                    else:
                        dve.wait_ge(conv_step, base + 5 * q)
                        r = dve.scalar_tensor_tensor(out=second, in0=x, scalar=w, in1=second, op0=ALU.mult, op1=ALU.add)
                    r.then_inc(conv_step, 1)
                else:
                    dve.wait_ge(conv_step, base + CSTEPS)

            def conv_end(pair):
                dve.wait_ge(dg_used, pair * CA_PE + CA_PE)
                second = y[:, bass.ds(pair * 2 + 1, 1), :]
                dve.tensor_tensor(second, second, O[:, 0:1, 0:256], ALU.add).then_inc(conv_taken, 1)

            with dve.Fori(1, 4) as c:
                for q in range(8):
                    conv(c - 1, c * CSTEPS - CSTEPS, q)
                    split(C_GLU + NSPL + q, c)
                    if q == 3:
                        glu_value(c)
                glu_gate(c, lambda: conv_end(c - 1))

            def ple_sums(g, units):
                for u in units:
                    take_sum(g + u, 0, pp[:, 2 * u:2 * u + 2, :])

            for s in range(NG):
                for q in range(2):
                    if s < 4:
                        conv(3, 3 * CSTEPS, 2 * s + q)
                    split(C_OUTB + 2 * s + q + NSPL)
                take_sum(G_OUTB + s, 0)
                dve.wait_ge(sum_ready, G_OUTB + s + 1)
                add_h(H_OUTB + s, 2 * s, first=True)
                if s == 3:
                    conv_end(3)
                    dve.wait_ge(conv_taken, 4)
                    dve.tensor_reduce(nacc[:, :], y[:, :, :].rearrange("p t n -> p n t"), AX_X,
                                      ALU.add).then_inc(ln_part, 1)
                elif s == 4:
                    dve.wait_ge(ln_stat, 1)
                    dve.tensor_tensor(y[:, :, :], y[:, :, :], bcast(Z[:, 0, 0:256], 8), ALU.subtract).then_inc(ln_vec, 1)
                elif s == 5:
                    dve.wait_ge(ln_act, 1)
                    dve.tensor_reduce(nacc[:, :], dec[:, :, :].rearrange("p t n -> p n t"), AX_X,
                                      ALU.add).then_inc(ln_part, 1)
            dve.wait_ge(ln_act, 2)
            dve.reciprocal(nacc[:, :], nacc[:, :]).then_inc(ln_vec, 1)
            dve.wait_ge(ln_vec, 2)
            for k in range(2):
                yk = y[:, 4 * k:4 * k + 4, :]
                dve.tensor_tensor(yk, yk, bcast(nacc[:, :], 4), ALU.mult).then_inc(ln_vec, 1)
            ple_sums(G_PLE0, range(4))
            for k in range(2):
                dve.wait_ge(ln_act, 4 + 2 * k)
                lo_of(XB, 4 * k, 4, y[:, 4 * k:4 * k + 4, :]).then_inc(ya_tiles, 1)
                ple_sums(G_PLE0, (4 + 2 * k, 5 + 2 * k))
            period(C_PLE0, 0, 5)
            dve.wait_ge(ln_vec, 4)
            clear(1)
            with dve.Fori(0, 2) as i:
                for s in range(4):
                    take_sum(G_OUTA + s, i * 4)
                    dve.wait_ge(sum_ready, i * 4 + (G_OUTA + s + 1))
                    add_h(i * 4 + (H_OUTA + s), i * 8 + 2 * s)
                    split(C_OUTA + 2 * s + NSPL, i)
                    fold(i * 4 + (8 + s))
                    split(C_OUTA + 2 * s + 1 + NSPL, i)
                    res_los(i * 4 + (8 + s), i * 8 + 2 * s, 1, XA)
            mlp(G_MLP0, C_MLP0, 0, H_MLP0, 1, XB, 16, 2, XA)
            gates(G_GATE0, C_GATE0, 0, 24, H_GATE0, 2, 3, XB)

            z = Z[:, :, 0:384]

            def keep_earlier_keys(done):
                d = tl[:, :, :].rearrange("p e (b n) -> p e b n", n=P)[:, :, 0:3:2, :]
                dve.tensor_tensor(d, d, mask[:, :].unsqueeze(1).unsqueeze(1).broadcast_to([P, 2, 2, P]),
                                  ALU.mult).then_inc(done, 1)

            def soft_sum(pr, i):
                dve.wait_ge(z_log, i * 2 + (pr + 1))
                dve.scalar_tensor_tensor(out=tl[:, :, :], in0=z, scalar=0.0, in1=te[:, :, :],
                                         op0=ALU.max, op1=ALU.add).then_inc(soft_raw, 1)
                dve.wait_ge(soft_raw, i * 2 + (pr + 1))
                keep_earlier_keys(soft_ready)

            def soft_rest(pr, i):
                dve.wait_ge(soft_hi, i * 2 + (pr + 1))
                dve.tensor_tensor(ws[:, :, 1, :], tl[:, :, :], ws[:, :, 0, :].bitcast(F32),
                                  ALU.subtract).then_inc(soft_split, 1)

            def weights_cut(pr, i):
                dve.wait_ge(logw_ready, i * 2 + (pr + 1))
                dve.tensor_scalar(te[:, :, :], z, 0.0, None, ALU.min).then_inc(logw_cut, 1)

            def weights_mask(pr, i):
                dve.wait_ge(w_exp, i * 2 + (pr + 1))
                keep_earlier_keys(w_ready)

            def weights_rest(pr, i):
                dve.wait_ge(w_hi, i * 2 + (pr + 1))
                dve.tensor_tensor(ws[:, :, 1, :], tl[:, :, :], ws[:, :, 0, :].bitcast(F32),
                                  ALU.subtract).then_inc(w_split, 1)

            def out_rest(pr, i):
                dve.wait_ge(o_hi, i * 2 + (pr + 1))
                lo_of(XA, i * 4 + 2 * pr, 2, O[:, :, 0:256]).then_inc(att_tiles, 1)

            def qkv(part, s, i, first=False):
                g, m = G_QKV + 3 * s + part, C_QKV + 12 * s + 4 * part
                steps = ((soft_sum, soft_rest, None, None), (None, None, weights_cut, weights_mask),
                         (None, None, None, out_rest))[part]
                for q in range(4):
                    if steps[q] is not None and not first:
                        steps[q](s - 1, i)
                    split(m + NSPL + q, i * 3)
                if part == 1 and not first:
                    weights_rest(s - 1, i)
                take_sum(g, i * 6)
                if first and part == 0:
                    norm(3, columns=True)
                dve.wait_ge(sum_ready, i * 6 + (g + 1))
                if part == 0:
                    dve.scalar_tensor_tensor(out=tv[:, :, :], in0=tv[:, :, :], scalar=float(DH) ** -0.5,
                                             in1=bcast(rB[:, :], 2), op0=ALU.mult, op1=ALU.mult).then_inc(qk_scaled, 1)
                elif part == 1:
                    dve.tensor_tensor(tv[:, :, :], tv[:, :, :], bcast(rB[:, :], 2), ALU.mult).then_inc(qk_scaled, 1)
                else:
                    for t in range(2):
                        r = dve.tensor_scalar(tv[:, t, :], tv[:, t, :], rC[:, t:t + 1], None, ALU.mult)
                    r.then_inc(qk_scaled, 1)
                dve.wait_ge(qk_hi, i * 6 + (3 * s + part + 1))
                X = vv[s] if part == 2 else qk[s][:, part, :, :, :]
                lo_of(X, 0, 2, tv[:, :, :]).then_inc(qk_split, 1)
                dve.wait_ge(qk_split, i * 6 + (3 * s + part + 1))

            for s in range(2):
                for part in range(3):
                    qkv(part, s, 0, first=(s == 0))
            with dve.Fori(1, 4) as i:
                for s in range(2):
                    for part in range(3):
                        qkv(part, s, i)
            ple_sums(G_PLE1, range(2))
            soft_sum(7, 0)
            soft_rest(7, 0)
            ple_sums(G_PLE1, range(2, 4))
            weights_cut(7, 0)
            ple_sums(G_PLE1, range(4, 6))
            weights_mask(7, 0)
            weights_rest(7, 0)
            ple_sums(G_PLE1, range(6, 8))
            period(C_PLE1, 0, 5)
            out_rest(7, 0)

            out_groups(G_OUT1, C_OUT1, H_OUT1, 32, 4, XB)
            mlp(G_MLP1, C_MLP1, 32, H_MLP1, 4, XA, 40, 5, XB)
            gates(G_GATE1, C_GATE1, 8, 48, H_GATE1, 5, 6, None)
            norm(6)
            dve.wait_ge(out_scaled, 8)
            for q in range(4):
                hq = h[:, 4 * q:4 * q + 4, :]
                dve.tensor_tensor(hq, hq, bcast(rB[:, :], 4), ALU.mult).then_inc(out_ready, 1)


def _columns(a, n):
    import numpy as np
    return np.asarray(a).reshape(-1, n, P).transpose(2, 0, 1).reshape(P, -1)


def kernel(x, p, norm_mix_g, norm_mlp_g, norm_ple_g, norm_f_g, w_in_rec, conv_a_w, conv_a_b, ln_a_g, ln_a_b,
           conv_b_w, conv_b_b, w_rg_a, b_rg_a, w_rg_x, b_rg_x, rg_lambda, w_out_rec, w_qkv, w_o_attn,
           w_mlp_up, w_mlp_down, w_ple_proj, w_ple_gate):
    import numpy as np
    import concourse.bacc as bacc
    from concourse.bass_utils import run_bass_kernel_spmd

    norms = [norm_mix_g[0], norm_mlp_g[0], norm_ple_g[0], norm_mix_g[1], norm_mlp_g[1], norm_ple_g[1], norm_f_g]
    taps_a = np.asarray(conv_a_w)[0].reshape(CA, 8, P).transpose(2, 1, 0).reshape(P, 8 * CA)
    taps_b = np.asarray(conv_b_w)[0].reshape(CB, 8, P).transpose(2, 1, 0).reshape(P, 8 * CB)
    par = np.concatenate([_columns(g, NT) for g in norms] + [taps_a] + [_columns(v, 8) for v in (conv_a_b, ln_a_g, ln_a_b)]
                         + [taps_b] + [_columns(v, 8) for v in (conv_b_b, b_rg_a, b_rg_x, rg_lambda)], axis=1)
    ins = {
        "xT": np.asarray(x)[0].T, "pT": np.asarray(p)[:, 0].transpose(0, 2, 1), "par": par,
        "w_in": w_in_rec, "w_rg_a": w_rg_a, "w_rg_x": w_rg_x, "w_out": w_out_rec, "w_qkv": w_qkv, "w_o": w_o_attn,
        "w_up": w_mlp_up, "w_down": w_mlp_down, "w_proj": w_ple_proj, "w_gate": w_ple_gate,
    }
    ins = {k: np.ascontiguousarray(v) for k, v in ins.items()}
    nc = bacc.Bacc("TRN2", target_bir_lowering=False, num_devices=1)
    aps = {k: nc.dram_tensor(f"in_{k}", v.shape, mybir.dt.from_np(v.dtype), kind="ExternalInput").ap()
           for k, v in ins.items()}
    out = nc.dram_tensor("outT", (D, T), F32, kind="ExternalOutput").ap()
    trunk(nc, outT=out, **aps)
    r = run_bass_kernel_spmd(nc, [{f"in_{k}": v for k, v in ins.items()}], core_ids=[0])
    return np.ascontiguousarray(r.results[0]["outT"].T)[None]
```

```python
from contextlib import ExitStack

import concourse.bass as bass
from concourse import mybir

P = 128
D = 2048
T = 256
DA = D // 2
DB = D // 2
CA = 31
CB = 4
DH = 128
NT = D // P
NG = D // T
NRAW = 4
NSPL = 8
EPS = 1e-6
PAD_A = CA - 1
PAD_B = CB - 1
XRP = PAD_B + T + 1

ALU = mybir.AluOpType
ACT = mybir.ActivationFunctionType
F32 = mybir.dt.float32
F32R = mybir.dt.float32r
AX_X = mybir.AxisListType.X

G_REC, C_REC = 0, 2
C_RG = 8
G_GLU, C_GLU = 8, 34
G_OUTB, C_OUTB = 16, 66
G_PLE0, C_PLE0 = 24, 82
G_OUTA, C_OUTA = 32, 87
G_MLP0, C_MLP0 = 40, 103
G_GATE0, C_GATE0 = 104, 359
G_QKV, C_QKV = 112, 391
G_PLE1, C_PLE1 = 136, 487
G_OUT1, C_OUT1 = 144, 492
G_MLP1, C_MLP1 = 152, 524
G_GATE1, C_GATE1 = 216, 780
CHUNKS = 812
H_OUTB, H_OUTA, H_MLP0, H_GATE0, H_OUT1, H_MLP1, H_GATE1 = 0, 8, 16, 48, 56, 64, 96
NDG = 14
CA_PE = 25
CA_VE = CA - CA_PE
CSTEPS = CA + 1 + CA_VE
LAM_STEPS = 17

GAIN = 0
CONV_A_W = GAIN + 7 * NT
CONV_A_B = CONV_A_W + 8 * CA
LN_G = CONV_A_B + 8
LN_B = LN_G + 8
CONV_B_W = LN_B + 8
CONV_B_B = CONV_B_W + 8 * CB
RG_BA = CONV_B_B + 8
RG_BX = RG_BA + 8
LAMBDA = RG_BX + 8
NPAR = LAMBDA + 8


def trunk(nc, xT, pT, par, w_in, w_rg_a, w_rg_x, w_out, w_qkv, w_o, w_up, w_down, w_proj, w_gate, outT):
    with ExitStack() as ctx:
        def sb(name, shape, dt=F32):
            return ctx.enter_context(nc.sbuf_tensor(name, shape, dt))

        def sem(name):
            return ctx.enter_context(nc.semaphore(name))

        raw = sb("raw", [P, NRAW, 4, 256])
        spl = sb("spl", [P, NSPL, 4, 2, 256], F32R)
        h = sb("h", [P, NT, T])
        cross = sb("cross", [P, 2, T])
        tv = sb("tv", [P, 2, T])
        nacc = sb("nacc", [P, T])
        rB = sb("rB", [P, T])
        rC = sb("rC", [P, 2])
        params = sb("params", [P, NPAR])
        lamc = sb("lamc", [P, 8])
        nlamc = sb("nlamc", [P, 8])
        small = sb("small", [P, 4, 8])
        onesD = sb("onesD", [P, P])
        onesA = sb("onesA", [P, P])
        epsb = sb("epsb", [P, 1])
        ngtri = sb("ngtri", [P, P], F32R)
        ngone = sb("ngone", [P, P], F32R)
        mask = sb("mask", [P, P])
        XA = sb("XA", [P, NT, 2, T], F32R)
        with nc.sbuf_tensor("glu", [P, 8, PAD_A + T], F32) as glu, \
                nc.sbuf_tensor("xrp", [P, 2, XRP], F32) as xrp, \
                nc.sbuf_tensor("rest", [P, 8 * 2 * T - 8 * (PAD_A + T) - 2 * XRP], F32), \
                nc.sbuf_tensor("rg", [P, 8, 2, T], F32) as rg:
            pass
        XB = sb("XB", [P, NT, 2, T], F32R)
        with nc.sbuf_tensor("qk0", [P, 2, 2, 2, T], F32R) as qk0, nc.sbuf_tensor("v0", [P, 2, 2, T], F32R) as v0, \
                nc.sbuf_tensor("te", [P, 2, 384], F32) as te:
            pass
        pp = sb("pp", [P, NT, T])
        with nc.sbuf_tensor("wrg", [P, 2, 4, 2, 256], F32R) as wrg:
            pass
        with nc.sbuf_tensor("mlt", [P, 8, T], F32) as mlt, nc.sbuf_tensor("dec", [P, 8, T], F32) as dec:
            pass
        with nc.sbuf_tensor("y", [P, 8, T], F32) as y, nc.sbuf_tensor("y2", [P, T], F32) as y2, \
                nc.sbuf_tensor("dg", [P, NDG, P], F32) as dg, nc.sbuf_tensor("ident", [P, P], F32) as ident:
            pass
        qk1 = sb("qk1", [P, 2, 2, 2, T], F32R)
        v1 = sb("v1", [P, 2, 2, T], F32R)
        tl = sb("tl", [P, 2, 384])
        ws = sb("ws", [P, 2, 2, 384], F32R)
        qk, vv = (qk0, qk1), (v0, v1)

        ps = ctx.enter_context(nc.psum_tensor("ps", [P, 4, 512], F32))
        Z = ctx.enter_context(nc.psum_tensor("Z", [P, 2, 512], F32))
        O = ctx.enter_context(nc.psum_tensor("O", [P, 2, 512], F32))

        raw_landed = [sem(f"raw_landed{i}") for i in range(NRAW)]
        hi_ready = sem("hi_ready")
        lo_ready = sem("lo_ready")
        chunk_used = sem("chunk_used")
        par_landed = sem("par_landed")
        x_landed = [sem(f"x_landed{i}") for i in range(4)]
        consts_ready = sem("consts_ready")
        cross_copied = sem("cross_copied")
        sum_ready = sem("sum_ready")
        res_ready = sem("res_ready")
        sq_ready = sem("sq_ready")
        res_hi = sem("res_hi")
        sq_folded = sem("sq_folded")
        res_tiles = sem("res_tiles")
        nacc_clear = sem("nacc_clear")
        stat_ready = sem("stat_ready")
        root_ready = sem("root_ready")
        rstd_ready = sem("rstd_ready")
        up_relu = sem("up_relu")
        up_sq = sem("up_sq")
        up_hi = sem("up_hi")
        up_tiles = sem("up_tiles")
        gate_scaled = sem("gate_scaled")
        gate_sig = sem("gate_sig")
        gate_mul = sem("gate_mul")
        glu_scaled = sem("glu_scaled")
        glu_sig = sem("glu_sig")
        glu_val = sem("glu_val")
        glu_ready = sem("glu_ready")
        conv_step = sem("conv_step")
        dg_ready = sem("dg_ready")
        dg_used = sem("dg_used")
        conv_taken = sem("conv_taken")
        xr_step = sem("xr_step")
        xr_hi = sem("xr_hi")
        xr_tiles = sem("xr_tiles")
        gr_scaled = sem("gr_scaled")
        gr_ready = sem("gr_ready")
        rg_done = sem("rg_done")
        rg_act = sem("rg_act")
        rg_vec = sem("rg_vec")
        ln_part = sem("ln_part")
        ln_stat = sem("ln_stat")
        ln_act = sem("ln_act")
        ln_vec = sem("ln_vec")
        qk_scaled = sem("qk_scaled")
        qk_hi = sem("qk_hi")
        qk_split = sem("qk_split")
        z_ready = sem("z_ready")
        z_abs = sem("z_abs")
        z_exp = sem("z_exp")
        z_log = sem("z_log")
        soft_raw = sem("soft_raw")
        soft_ready = sem("soft_ready")
        soft_hi = sem("soft_hi")
        soft_split = sem("soft_split")
        logw_ready = sem("logw_ready")
        logw_cut = sem("logw_cut")
        w_exp = sem("w_exp")
        w_ready = sem("w_ready")
        w_hi = sem("w_hi")
        w_split = sem("w_split")
        o_ready = sem("o_ready")
        o_hi = sem("o_hi")
        att_tiles = sem("att_tiles")
        out_scaled = sem("out_scaled")
        out_ready = sem("out_ready")
        stored = sem("stored")
        ple_done = sem("ple_done")
        yb_tiles = sem("yb_tiles")
        ya_tiles = sem("ya_tiles")
        lam_abs = sem("lam_abs")
        lam_exp = sem("lam_exp")
        lam_chain = sem("lam_chain")

        def counts(base, turns):
            return base > 0 or not isinstance(turns, int)

        def bcast(ap, n):
            return ap.unsqueeze(1).broadcast_to([P, n, ap.shape[-1]])

        def par_col(c):
            return params[:, bass.ds(c, 1)]

        def gain(n, t):
            return par_col(t + (GAIN + n * NT))

        block = ctx.enter_context(nc.Block())

        @block.sync
        def _(sp):
            def load(m, it, src):
                if counts(m - NRAW + 1, it):
                    sp.wait_ge(lo_ready, it * 8 + (m - NRAW + 1))
                sp.dma_start(raw[:, m % NRAW, :, :], src).then_inc(raw_landed[m % NRAW], 16)

            def load_group(m, it, w, col, row0=0, rows=(0, 4, 8, 12)):
                for j, r in enumerate(rows):
                    src = w[bass.ds(row0 + r * P, 4 * P), bass.ds(col, 256)]
                    load(m + j, it, src.rearrange("(t p) n -> p t n", p=P))

            def load_pair(m, w, cols):
                for j in range(4):
                    for s in range(2):
                        src = w[4 * j * P:(4 * j + 4) * P, cols[s]:cols[s] + 256]
                        load(m + 2 * j + s, 0, src.rearrange("(t p) n -> p t n", p=P))

            def load_ple(m, layer):
                load(m, 0, pT.rearrange("l (t p) n -> p (l t) n", p=P))
                for j in range(4):
                    src = w_proj[layer, :, 512 * j:512 * j + 512]
                    load(m + 1 + j, 0, src.rearrange("(t p) n -> p t n", p=P))

            def mlp(layer, m):
                def up(f, i):
                    for s in range(2):
                        load_group(m + 4 * s, f * 8 + i, w_up[layer], f * D + i * 512 + 256 * s)

                def down(f):
                    with sp.Fori(0, 4) as i:
                        for s in range(2):
                            load_group(m + 32 + 4 * s, f * 8 + i, w_down[layer], i * 512 + 256 * s, row0=f * D)

                load_pair(m, w_up[layer], (0, 256))
                with sp.Fori(1, 4) as i:
                    up(0, i)
                down(0)
                with sp.Fori(1, 4) as f:
                    with sp.Fori(0, 4) as i:
                        up(f, i)
                    down(f)

            def square(m, w):
                load_pair(m, w, (0, 256))
                with sp.Fori(1, 4) as i:
                    for s in range(2):
                        load_group(m + 4 * s, i, w, i * 512 + 256 * s)

            def half_square(m, w, row0):
                with sp.Fori(0, 2) as i:
                    for s in range(4):
                        load_group(m + 2 * s, i, w, i * 1024 + 256 * s, row0, (0, 4))

            def load_x(k):
                sp.dma_start(h[:, 4 * k:4 * k + 4, :], xT[4 * k * P:(4 * k + 4) * P, :].rearrange(
                    "(t p) n -> p t n", p=P)).then_inc(x_landed[k], 16)

            def load_first(k):
                for s in range(2):
                    col = 2 * DA + s * DB
                    src = w_in[0, k * 4 * P:(k + 1) * 4 * P, col:col + 256]
                    load(2 * k + s, 0, src.rearrange("(t p) n -> p t n", p=P))

            load_x(0)
            sp.dma_start(params[:, :], par).then_inc(par_landed, 16)
            load_first(0)
            load_x(1)
            load_first(1)
            load_x(2)
            load_x(3)
            load_first(2)
            load_first(3)
            for j, w in enumerate((w_rg_a, w_rg_x)):
                m = C_RG + j
                sp.wait_ge(lo_ready, m - NRAW + 1)
                dst = raw[:, m % NRAW, :, :].rearrange("p a (b n) -> p (a b) n", b=2)
                sp.dma_start(dst, w[0].rearrange("h i j -> i h j")).then_inc(raw_landed[m % NRAW], 16)
            with sp.Fori(1, 4) as i:
                load_group(C_REC, i, w_in[0], i * 256 + 2 * DA)
                load_group(C_REC + 4, i, w_in[0], i * 256 + 2 * DA + DB)
            with sp.Fori(0, 4) as i:
                load_group(C_GLU, i, w_in[0], i * 256)
                load_group(C_GLU + 4, i, w_in[0], i * 256 + DA)
            half_square(C_OUTB, w_out[0], DA)
            load_ple(C_PLE0, 0)
            half_square(C_OUTA, w_out[0], 0)
            mlp(0, C_MLP0)
            square(C_GATE0, w_gate[0])
            def load_qkv(s, part, i):
                load_group(C_QKV + 12 * s + 4 * part, i * 3, w_qkv[0], i * 512 + (part * D + 256 * s))

            load_pair(C_QKV, w_qkv[0], (0, D))
            load_qkv(0, 2, 0)
            for part in range(3):
                load_qkv(1, part, 0)
            with sp.Fori(1, 4) as i:
                for s in range(2):
                    for part in range(3):
                        load_qkv(s, part, i)
            load_ple(C_PLE1, 1)
            square(C_OUT1, w_o[0])
            mlp(1, C_MLP1)
            square(C_GATE1, w_gate[1])
            for q in range(4):
                sp.wait_ge(out_ready, q + 1)
                sp.dma_start(outT[4 * q * P:(4 * q + 4) * P, :].rearrange("(t p) n -> p t n", p=P),
                             h[:, 4 * q:4 * q + 4, :]).then_inc(stored, 16)
            sp.wait_ge(stored, 64)

        @block.gpsimd
        def _(pool):
            pool.memset(onesD[:, :], 1.0 / D)
            pool.memset(onesA[:, :], 1.0 / DA)
            pool.memset(epsb[:, :], EPS)
            pool.memset(y2[:, 0:P], 1.0)
            pool.memset(glu[:, :, 0:PAD_A], 0.0)
            pool.memset(xrp[:, :, 0:PAD_B], 0.0)
            pool.memset(tl[:, 0, 0:P], -1.0)
            pool.memset(tl[:, 1, 0:P], 1.0).then_inc(consts_ready, 1)
            pool.wait_ge(consts_ready, 1)
            pool.affine_select(out=tl[:, 0, P:2 * P], in_=tl[:, 0, 0:P], compare_op=ALU.is_ge, fill=0.0, base=0,
                               pattern=[[-1, P]], channel_multiplier=1)
            pool.affine_select(out=ident[:, :], in_=y2[:, 0:P], compare_op=ALU.is_equal, fill=0.0, base=0,
                               pattern=[[-1, P]], channel_multiplier=1)
            pool.affine_select(out=mask[:, :], in_=tl[:, 1, 0:P], compare_op=ALU.is_gt, fill=0.0, base=0,
                               pattern=[[1, P]], channel_multiplier=-1).then_inc(consts_ready, 1)

        @block.tensor
        def _(pe):
            def chunk(b, m, it, x, kt0, first, last, tokens_out=False, releases=1):
                pe.wait_ge(lo_ready, it * 8 + (m + 1))
                w = spl[:, m % NSPL, :, :, :]
                for q in range(4):
                    kt, start, stop = kt0 + q, first and q == 0, last and q == 3
                    for o in range(2):
                        c = slice(o * P, (o + 1) * P)
                        if tokens_out:
                            pe.matmul(ps[:, b + o, :], x[:, kt, 0, c], w[:, q, :, :], start=start, stop=False)
                            mm = pe.matmul(ps[:, b + o, 0:256], x[:, kt, 1, c], w[:, q, 0, :], start=False, stop=stop)
                        else:
                            pe.matmul(ps[:, b + o, :], w[:, q, 0, c], x[:, kt, :, :], start=start, stop=False)
                            mm = pe.matmul(ps[:, b + o, 0:256], w[:, q, 1, c], x[:, kt, 0, :], start=False, stop=stop)
                mm.then_inc(chunk_used, releases)

            def gemm(g, gi, m, it, x, tiles=None, rows=(0, 4, 8, 12), tokens_out=False, mid=None):
                if counts(g - 1, gi):
                    pe.wait_ge(sum_ready, gi + (g - 1))
                for j, row in enumerate(rows):
                    if mid is not None and j == len(rows) // 2:
                        mid()
                    if tiles is not None:
                        pe.wait_ge(*tiles[j])
                    chunk(2 * (g % 2), m + j, it, x, row, j == 0, j == len(rows) - 1, tokens_out)

            def first_pair(g, m, x, tiles, stat=None, releases=1, mid=None):
                for j in range(4):
                    if j == 2 and mid is not None:
                        mid()
                    pe.wait_ge(*tiles[j])
                    for s in range(2):
                        if j == 0 and g + s > 1:
                            pe.wait_ge(sum_ready, g + s - 1)
                        if j == 3 and s == 1 and stat is not None:
                            stat()
                        chunk(2 * s, m + 2 * j + s, 0, x, 4 * j, j == 0, j == 3,
                              releases=releases if j == 3 and s == 1 else 1)

            def stats(n, columns=False):
                pe.wait_ge(sq_folded, 16 * (n + 1))
                if n > 0:
                    pe.wait_ge(rstd_ready, n)
                mm = pe.matmul(Z[:, 0, 0:256], onesD[:, :], nacc[:, :], start=True, stop=True)
                if columns:
                    for t in range(2):
                        mm = pe.matmul(Z[:, 0, 256 + t:257 + t], nacc[:, t * P:(t + 1) * P], onesD[:, 0:1],
                                       start=False, stop=True, skip_group_check=True)
                mm.then_inc(stat_ready, 1)

            def after_res(f):
                return [(res_tiles, f + 2 * j + 2) for j in range(4)]

            def ple(g, m, layer, units):
                for u in units:
                    c, b = m + 1 + u // 2, 2 * (u % 2)
                    pe.wait_ge(sum_ready, g + u - 1)
                    pe.wait_ge(lo_ready, c + 1)
                    for k in range(2):
                        x = spl[:, m % NSPL, 2 * layer + k, :, :]
                        for o in range(2):
                            w = spl[:, c % NSPL, 2 * k + u % 2, :, o * P:(o + 1) * P]
                            pe.matmul(ps[:, b + o, :], w[:, 0, :], x, start=(k == 0), stop=False)
                            mm = pe.matmul(ps[:, b + o, 0:256], w[:, 1, :], x[:, 0, :], start=False, stop=(k == 1))
                    if u < 7:
                        mm.then_inc(ple_done, 1)
                    else:
                        mm.then_inc(chunk_used, 5)

            def scores(pr, i, s):
                pe.wait_ge(qk_split, i * 6 + (3 * pr + 2))
                if counts(pr, i):
                    pe.wait_ge(logw_cut, i * 2 + pr)
                q, k = qk[s][:, 0, :, :, :], qk[s][:, 1, :, :, :]
                for e in range(2):
                    for kt, cols, qs in ((0, slice(0, 256), slice(0, 256)), (1, slice(256, 384), slice(P, 256))):
                        kc = slice(kt * P, (kt + 1) * P)
                        for n, (kh, qh) in enumerate(((0, 0), (0, 1), (1, 0))):
                            mm = pe.matmul(Z[:, e, cols], k[:, e, kh, kc], q[:, e, qh, qs],
                                           start=(n == 0 and kt == 0), stop=False, skip_group_check=True)
                mm.then_inc(z_ready, 1)

            def suffix_sums(pr, i):
                pe.wait_ge(soft_split, i * 2 + (pr + 1))
                for e in range(2):
                    for hl in range(2):
                        pe.matmul(Z[:, e, 0:384], ngtri[:, :], ws[:, e, hl, 0:384],
                                  start=False, stop=False, skip_group_check=True)
                        mm = pe.matmul(Z[:, e, P:256], ngone[:, :], ws[:, e, hl, 256:384],
                                       start=False, stop=(hl == 1), skip_group_check=True)
                mm.then_inc(logw_ready, 1)

            def values(pr, i, s):
                v = vv[s]
                pe.wait_ge(qk_split, i * 6 + (3 * pr + 3))
                pe.wait_ge(w_split, i * 2 + (pr + 1))
                if counts(pr, i):
                    pe.wait_ge(att_tiles, i * 2 + pr)
                for e in range(2):
                    hc = slice(e * P, (e + 1) * P)
                    for kt, cols, wc in ((0, slice(0, 256), slice(0, 256)), (1, slice(P, 256), slice(256, 384))):
                        for n, (vh, wh) in enumerate(((0, 0), (0, 1), (1, 0))):
                            mm = pe.matmul(O[:, e, cols], v[:, kt, vh, hc], ws[:, e, wh, wc],
                                           start=(n == 0 and kt == 0), stop=(n == 2 and kt == 1),
                                           skip_group_check=True)
                mm.then_inc(o_ready, 1)

            def mlp(g, m, x, hid, f_in, norm, u):
                first_pair(g, m, x, after_res(f_in), lambda: stats(norm))
                with pe.Fori(1, 4) as i:
                    for s in range(2):
                        gemm(g + s, i * 2, m + 4 * s, i, x)
                with pe.Fori(0, 4) as i:
                    for s in range(2):
                        gemm(g + 8 + s, i * 2, m + 32 + 4 * s, i, hid,
                             [(up_tiles, u + 2 * j + 2) for j in range(4)])
                with pe.Fori(1, 4) as f:
                    with pe.Fori(0, 4) as i:
                        for s in range(2):
                            gemm(g + s, f * 16 + i * 2, m + 4 * s, f * 8 + i, x)
                    with pe.Fori(0, 4) as i:
                        for s in range(2):
                            gemm(g + 8 + s, f * 16 + i * 2, m + 32 + 4 * s, f * 8 + i, hid,
                                 [(up_tiles, f * 8 + (u + 2 * j + 2)) for j in range(4)])

            def square(g, m, x, tiles, mid):
                first_pair(g, m, x, tiles, mid=mid)
                with pe.Fori(1, 4) as i:
                    for s in range(2):
                        gemm(g + s, i * 2, m + 4 * s, i, x, tiles)

            def after_norm(g, m, x, f_in, norm):
                first_pair(g, m, x, after_res(f_in), lambda: stats(norm))
                with pe.Fori(1, 4) as i:
                    for s in range(2):
                        gemm(g + s, i * 2, m + 4 * s, i, x)

            pe.wait_ge(consts_ready, 1)
            first_pair(G_REC, 0, XA, after_res(0), lambda: stats(0), releases=3)

            def rg_head(pair, j):
                if j == 0:
                    pe.wait_ge(xr_tiles, pair + 1)
                if pair >= 2:
                    pe.wait_ge(rg_act, pair - 1)
                B, x = (Z, O)[pair % 2][:, j, :], XB[:, 8 + 2 * pair + j, :, :]
                for a in range(2):
                    w = wrg[:, a, pair, :, j * P:(j + 1) * P]
                    for n, (wh, xh) in enumerate(((0, 0), (0, 1), (1, 0))):
                        mm = pe.matmul(B[:, a * T:(a + 1) * T], w[:, wh, :], x[:, xh, :], start=(a == 0 and n == 0),
                                       stop=(a == 1 and n == 2), skip_group_check=True)
                mm.then_inc(rg_done, 1)

            pe.wait_ge(lo_ready, C_RG + 2)
            for i in range(1, 4):
                for s in range(2):
                    gemm(G_REC + 2 * i + s, 0, C_REC + 8 * i + 4 * s, 0, XA)
                    rg_head(i - 1, s)
            rg_head(3, 0)
            rg_head(3, 1)

            def conv(pair, count, part, parts):
                if part == 0:
                    pe.wait_ge(glu_ready, pair + 1)
                for k in range(part * CA_PE // parts, (part + 1) * CA_PE // parts):
                    pe.wait_ge(dg_ready, count + (k + 1))
                    pe.matmul(O[:, 0, 0:256], dg[:, k % NDG, :], glu[:, bass.ds(pair * 2 + 1, 1), k:k + T],
                              start=(k == 0), stop=(k == CA_PE - 1), skip_group_check=True).then_inc(dg_used, 1)

            gemm(G_GLU, 0, C_GLU, 0, XA)
            pe.wait_ge(rg_act, 4)
            gemm(G_GLU + 1, 0, C_GLU + 4, 0, XA)
            with pe.Fori(1, 4) as c:
                for s in range(2):
                    def taps(part):
                        conv(c - 1, c * CA_PE - CA_PE, part, 3)

                    gemm(G_GLU + s, c * 2, C_GLU + 4 * s, c, XA, mid=None if s == 0 else lambda: taps(1))
                    taps(2 * s)
            def ln_mean(n):
                pe.wait_ge(ln_part, n)
                pe.matmul(Z[:, 0, 0:256], onesA[:, :], nacc[:, :], start=True, stop=True).then_inc(ln_stat, 1)

            for s in range(NG):
                gemm(G_OUTB + s, 0, C_OUTB + 2 * s, 0, XB, [(yb_tiles, 1)] * 2, (8, 12),
                     mid={5: lambda: ln_mean(1), 7: lambda: ln_mean(2)}.get(s))
                if s < 4:
                    conv(3, 3 * CA_PE, s, 4)
            ple(G_PLE0, C_PLE0, 0, range(8))
            with pe.Fori(0, 2) as i:
                for s in range(4):
                    gemm(G_OUTA + s, i * 4, C_OUTA + 2 * s, i, XB, [(ya_tiles, 1), (ya_tiles, 2)], (0, 4))
            mlp(G_MLP0, C_MLP0, XA, XB, 8, 1, 0)
            after_norm(G_GATE0, C_GATE0, XA, 16, 2)

            def pair(s, i, first):
                g, m = G_QKV + 3 * s, C_QKV + 12 * s
                if first:
                    first_pair(g, m, XB, after_res(24), lambda: stats(3, columns=True))
                else:
                    gemm(g, i * 6, m, i * 3, XB)
                    gemm(g + 1, i * 6, m + 4, i * 3, XB, mid=lambda: suffix_sums(s - 1, i))
                gemm(g + 2, i * 6, m + 8, i * 3, XB, tokens_out=True,
                     mid=None if first else lambda: values(s - 1, i, (s - 1) % 2))
                scores(s, i, s)

            pair(0, 0, True)
            pair(1, 0, False)
            with pe.Fori(1, 4) as i:
                pair(0, i, False)
                pair(1, i, False)
            ple(G_PLE1, C_PLE1, 1, range(8))
            suffix_sums(7, 0)
            square(G_OUT1, C_OUT1, XA, [(att_tiles, 2 * j + 2) for j in range(4)], lambda: values(7, 0, 1))
            mlp(G_MLP1, C_MLP1, XB, XA, 32, 4, 32)
            after_norm(G_GATE1, C_GATE1, XB, 40, 5)
            stats(6)

        @block.scalar
        def _(act):
            def copy(out, in_, scale=1.0):
                return act.activation(out, in_, ACT.Copy, scale=scale)

            def split(m, it=0):
                if m < CHUNKS:
                    act.wait_ge(raw_landed[m % NRAW], it * (16 * 8 // NRAW) + 16 * (m // NRAW + 1))
                    if counts(m - NSPL + 1, it):
                        act.wait_ge(chunk_used, it * 8 + (m - NSPL + 1))
                    copy(spl[:, m % NSPL, :, 0, :], raw[:, m % NRAW, :, :]).then_inc(hi_ready, 1)

            def period(m, it, k=4):
                for q in range(k):
                    split(m + NSPL + q, it)

            def split_rg(j):
                m = C_RG + j
                act.wait_ge(raw_landed[m % NRAW], 16 * (m // NRAW + 1))
                copy(wrg[:, j, :, 0, :], raw[:, m % NRAW, :, :]).then_inc(hi_ready, 1)

            def take_cross(g, gi, ready):
                if counts(g, gi):
                    act.wait_ge(sum_ready, gi + g)
                act.wait_ge(*ready)
                b = 2 * (g % 2)
                copy(cross[:, :, :], ps[:, b:b + 2, 256:512]).then_inc(cross_copied, 1)

            def group_done(m, it):
                return chunk_used, it * 8 + (m + 4)

            def group(g, gi, m, it, first=False, later=0, steps={}):
                if not first:
                    period(m, it, 4 - later)
                    take_cross(g, gi, group_done(m, it))
                else:
                    s, m = g % 2, m - 4 * (g % 2)
                    for q in range(7 * s, 7 + s):
                        if q in steps:
                            steps[q]()
                        split(m + NSPL + q)
                    take_cross(g, 0, (chunk_used, m + 7 + s))

            def norm(n, columns=False):
                act.wait_ge(stat_ready, n + 1)
                r = act.activation(rB[:, :], Z[:, 0, 0:256], ACT.Sqrt, bias=epsb[:, :])
                if columns:
                    r = act.activation(rC[:, :], Z[:, 0, 256:258], ACT.Sqrt, bias=epsb[:, :])
                r.then_inc(root_ready, 1)

            def squares(t0):
                act.activation(tv[:, :, :], h[:, bass.ds(t0, 2), :], ACT.Square).then_inc(sq_ready, 1)

            def res_his(t0, n, X):
                for j in range(2):
                    r = act.activation(X[:, bass.ds(t0 + j, 1), 0, :], h[:, bass.ds(t0 + j, 1), :], ACT.Identity,
                                       scale=gain(n, t0 + j))
                r.then_inc(res_hi, 1)

            def residual(hidx, t0, n, X):
                act.wait_ge(res_ready, hidx + 1)
                squares(t0)
                if X is not None:
                    res_his(t0, n, X)
                else:
                    act.wait_ge(sq_ready, hidx - 47)
                    for j in range(2):
                        hj = h[:, bass.ds(t0 + j, 1), :]
                        r = act.activation(hj, hj, ACT.Identity, scale=gain(n, t0 + j))
                    r.then_inc(out_scaled, 1)

            def up(g, gi, m, it, u, t0, hid, norm_n=None, first=False):
                group(g, gi, m, it, first)
                if norm_n is not None:
                    norm(norm_n)
                act.wait_ge(up_relu, u + 1)
                act.activation(tv[:, :, :], tv[:, :, :], ACT.Square).then_inc(up_sq, 1)
                act.wait_ge(up_sq, u + 1)
                copy(hid[:, bass.ds(t0, 2), 0, :], tv[:, :, :]).then_inc(up_hi, 1)

            def gate(g, gi, m, it, k, hidx, t0, n, X, norm_n=None, first=False):
                group(g, gi, m, it, first, 2)
                if norm_n is not None:
                    norm(norm_n)
                if not first:
                    split(m + 2 + NSPL, it)
                act.wait_ge(gate_scaled, k + 1)
                act.activation(tv[:, :, :], tv[:, :, :], ACT.Sigmoid).then_inc(gate_sig, 1)
                if not first:
                    split(m + 3 + NSPL, it)
                residual(hidx, t0, n, X)

            def out_groups(g, m, hidx, n, X, first=None):
                if first:
                    for s in range(2):
                        group(g + s, 0, m + 4 * s, 0, True, steps=first)
                        residual(hidx + s, 2 * s, n, X)
                with act.Fori(1 if first else 0, 4) as i:
                    for s in range(2):
                        group(g + s, i * 2, m + 4 * s, i, later=1)
                        split(m + 4 * s + 3 + NSPL, i)
                        residual(i * 2 + (hidx + s), i * 4 + 2 * s, n, X)

            def mlp(g, m, u, hidx, norm_in, hid, n, X):
                for s in range(2):
                    up(g + s, 0, m + 4 * s, 0, u + s, 2 * s, hid, norm_in if s == 0 else None, True)
                with act.Fori(1, 4) as i:
                    for s in range(2):
                        up(g + s, i * 2, m + 4 * s, i, i * 2 + (u + s), i * 4 + 2 * s, hid)
                with act.Fori(0, 4) as i:
                    for s in range(2):
                        group(g + 8 + s, i * 2, m + 32 + 4 * s, i)
                with act.Fori(1, 3) as f:
                    with act.Fori(0, 4) as i:
                        for s in range(2):
                            up(g + s, f * 16 + i * 2, m + 4 * s, f * 8 + i, f * 8 + i * 2 + (u + s),
                               i * 4 + 2 * s, hid)
                    with act.Fori(0, 4) as i:
                        for s in range(2):
                            group(g + 8 + s, f * 16 + i * 2, m + 32 + 4 * s, f * 8 + i)
                g, m, u, hidx = g + 48, m + 192, u + 24, hidx + 24
                with act.Fori(0, 4) as i:
                    for s in range(2):
                        up(g + s, i * 2, m + 4 * s, i, i * 2 + (u + s), i * 4 + 2 * s, hid)
                out_groups(g + 8, m + 32, hidx, n, X)

            def gates(g, m, k, hidx, norm_in, n, X):
                for s in range(2):
                    gate(g + s, 0, m + 4 * s, 0, k + s, hidx + s, 2 * s, n, X, norm_in if s == 0 else None, True)
                with act.Fori(1, 3) as i:
                    for s in range(2):
                        gate(g + s, i * 2, m + 4 * s, i, i * 2 + (k + s), i * 2 + (hidx + s), i * 4 + 2 * s, n, X)
                for s in range(2):
                    gate(g + 6 + s, 0, m + 24 + 4 * s, 0, k + 6 + s, hidx + 6 + s, 12 + 2 * s, n, X)

            act.wait_ge(consts_ready, 2)
            act.wait_ge(par_landed, 16)
            def square_x(f):
                if f >= 1:
                    act.wait_ge(sq_folded, 2 * f)
                squares(2 * f)

            for k in range(4):
                act.wait_ge(x_landed[k], 16)
                for f in (2 * k, 2 * k + 1):
                    res_his(2 * f, 0, XA)
                split(2 * k)
                if k >= 2:
                    square_x(k - 1)
                split(2 * k + 1)
                if k == 1:
                    square_x(0)
            act.activation(small[:, 0, :], params[:, LAMBDA:LAMBDA + 8], ACT.Abs).then_inc(lam_abs, 1)
            act.wait_ge(lam_abs, 1)
            act.activation(small[:, 1, :], small[:, 0, :], ACT.Exp, scale=-1.0).then_inc(lam_exp, 1)
            for f in range(3, 8):
                square_x(f)
                if f < 5:
                    split_rg(f - 3)
                elif f < 7:
                    split(5 + f)

            def round_x(c):
                act.wait_ge(xr_step, c * 9 + 9)
                copy(XB[:, bass.ds(c * 2 + 8, 2), 0, :], pp[:, bass.ds(c * 2, 2), :]).then_inc(xr_hi, 1)

            def gelu_gate(c):
                act.wait_ge(gr_scaled, c + 1)
                act.activation(pp[:, bass.ds(c * 2 + 8, 2), :], tv[:, :, :], ACT.Gelu_apprx_tanh).then_inc(gr_ready, 1)

            def head_sigmoids(pair):
                act.wait_ge(rg_done, pair * 2 + 2)
                for j in range(2):
                    for a, bias in enumerate((RG_BA, RG_BX)):
                        r = act.activation(rg[:, 2 * pair + j, a, :], (Z, O)[pair % 2][:, j, a * T:(a + 1) * T],
                                           ACT.Sigmoid, bias=par_col(2 * pair + bias + j))
                r.then_inc(rg_act, 1)

            def rec_pair(c):
                m = C_REC + NSPL + 8 * c
                for q in range(4):
                    split(m + q)
                take_cross(G_REC + 2 * c, 0, group_done(C_REC + 8 * c, 0))
                for q in range(4, 6):
                    split(m + q)
                if c >= 2:
                    head_sigmoids(c - 2)
                round_x(c)
                for q in range(6, 8):
                    split(m + q)
                take_cross(G_REC + 2 * c + 1, 0, group_done(C_REC + 8 * c + 4, 0))
                gelu_gate(c)

            for m in range(12, 15):
                split(m)
            take_cross(G_REC, 0, (chunk_used, 7))
            norm(0)
            split(15)
            take_cross(G_REC + 1, 0, (chunk_used, 8))
            round_x(0)
            gelu_gate(0)
            for m in range(16, 18):
                split(m)
            for c in range(1, 4):
                rec_pair(c)
            head_sigmoids(2)
            head_sigmoids(3)

            def rg_exp():
                act.wait_ge(rg_act, 4)
                act.wait_ge(lam_chain, LAM_STEPS)
                for t in range(8):
                    r = act.activation(dec[:, t, :], rg[:, t, 0, :], ACT.Exp, scale=nlamc[:, t:t + 1])
                r.then_inc(rg_act, 1)

            def rg_tanh():
                for t in range(8):
                    r = act.activation(mlt[:, t, :], rg[:, t, 0, :], ACT.Tanh, scale=lamc[:, t:t + 1])
                r.then_inc(rg_act, 1)

            def glu_gate(c):
                act.wait_ge(glu_scaled, c + 1)
                act.activation(tv[:, :, :], tv[:, :, :], ACT.Sigmoid).then_inc(glu_sig, 1)

            rg_exp()
            split(C_GLU + NSPL)
            rg_tanh()
            split(C_GLU + NSPL + 1)
            split(C_GLU + NSPL + 2)
            split(C_GLU + NSPL + 3)
            take_cross(G_GLU, 0, group_done(C_GLU, 0))
            act.wait_ge(rg_vec, 3)
            act.activation(mlt[:, :, :], mlt[:, :, :], ACT.Sqrt).then_inc(rg_act, 1)
            period(C_GLU + 4, 0)
            take_cross(G_GLU + 1, 0, group_done(C_GLU + 4, 0))
            glu_gate(0)

            def tap_matrices(pair, count, part, parts):
                if part == 0 and (not isinstance(pair, int) or pair > 0):
                    act.wait_ge(dg_used, count)
                for k in range(part * CA_PE // parts, (part + 1) * CA_PE // parts):
                    if k >= NDG:
                        act.wait_ge(dg_used, count + (k + 1 - NDG))
                    act.activation(dg[:, k % NDG, :], ident[:, :], ACT.Copy,
                                   scale=par_col((pair * 2 + 1) * CA + (CONV_A_W + k))).then_inc(dg_ready, 1)

            def glu_pair(c):
                for q in range(8):
                    tap_matrices(c - 1, c * CA_PE - CA_PE, q, 8)
                    split(C_GLU + NSPL + q, c)
                    if isinstance(c, int) and q == 4:
                        act.wait_ge(rg_vec, 6)
                        copy(XB[:, 8:16, 0, :], pp[:, 0:8, :]).then_inc(rg_act, 1)
                    if q % 4 == 3:
                        take_cross(G_GLU + q // 4, c * 2, group_done(C_GLU + q - 3, c))
                glu_gate(c)

            act.wait_ge(rg_vec, 5)
            glu_pair(1)
            with act.Fori(2, 4) as c:
                glu_pair(c)

            def ple_cross(g, m, layer, units):
                for u in units:
                    take_cross(g + u, 0, (ple_done, 7 * layer + u + 1) if u < 7 else (chunk_used, m + 5))

            for s in range(NG):
                if s < 4:
                    tap_matrices(3, 3 * CA_PE, s, 4)
                period(C_OUTB + 2 * s, 0, 2)
                if s == 7:
                    act.wait_ge(ln_stat, 2)
                    act.activation(nacc[:, :], Z[:, 0, 0:256], ACT.Sqrt, bias=epsb[:, :]).then_inc(ln_act, 1)
                take_cross(G_OUTB + s, 0, (chunk_used, C_OUTB + 2 * s + 2))
                if s == 5:
                    act.wait_ge(ln_vec, 1)
                    act.activation(dec[:, :, :], y[:, :, :], ACT.Square).then_inc(ln_act, 1)
            ple_cross(G_PLE0, C_PLE0, 0, (0,))
            for k in range(2):
                act.wait_ge(ln_vec, 3 + k)
                for t in range(4 * k, 4 * k + 4):
                    r = act.activation(y[:, t, :], y[:, t, :], ACT.Silu, scale=par_col(LN_G + t), bias=par_col(LN_B + t))
                    if t == 4 * k + 1:
                        ple_cross(G_PLE0, C_PLE0, 0, (1 + 3 * k,))
                r.then_inc(ln_act, 1)
                ple_cross(G_PLE0, C_PLE0, 0, (2 + 3 * k,))
                act.wait_ge(ln_act, 3 + 2 * k)
                copy(XB[:, 4 * k:4 * k + 4, 0, :], y[:, 4 * k:4 * k + 4, :]).then_inc(ln_act, 1)
                ple_cross(G_PLE0, C_PLE0, 0, (3 + 3 * k,))
            ple_cross(G_PLE0, C_PLE0, 0, (7,))
            period(C_PLE0, 0, 5)

            with act.Fori(0, 2) as i:
                for s in range(4):
                    m = C_OUTA + 2 * s
                    take_cross(G_OUTA + s, i * 4, (chunk_used, i * 8 + (m + 2)))
                    period(m, i, 2)
                    residual(i * 4 + (H_OUTA + s), i * 8 + 2 * s, 1, XA)
            mlp(G_MLP0, C_MLP0, 0, H_MLP0, 1, XB, 2, XA)
            gates(G_GATE0, C_GATE0, 0, H_GATE0, 2, 3, XB)

            def soft_abs(pr, i):
                act.wait_ge(z_ready, i * 2 + (pr + 1))
                act.activation(te[:, :, :], Z[:, :, 0:384], ACT.Abs).then_inc(z_abs, 1)

            def soft_exp(pr, i):
                act.wait_ge(z_abs, i * 2 + (pr + 1))
                act.activation(te[:, :, :], te[:, :, :], ACT.Exp, scale=-1.0).then_inc(z_exp, 1)
                act.wait_ge(z_exp, i * 2 + (pr + 1))
                act.activation(te[:, :, :], te[:, :, :], ACT.Ln, bias=1.0).then_inc(z_log, 1)

            def soft_round(pr, i):
                act.wait_ge(soft_ready, i * 2 + (pr + 1))
                copy(ws[:, :, 0, :], tl[:, :, :]).then_inc(soft_hi, 1)

            def weights_exp(pr, i):
                act.wait_ge(logw_cut, i * 2 + (pr + 1))
                act.activation(tl[:, :, :], tl[:, :, :], ACT.Exp).then_inc(w_exp, 1)

            def weights_round(pr, i):
                act.wait_ge(w_ready, i * 2 + (pr + 1))
                copy(ws[:, :, 0, :], tl[:, :, :]).then_inc(w_hi, 1)

            def out_round(pr, i):
                act.wait_ge(o_ready, i * 2 + (pr + 1))
                copy(XA[:, bass.ds(i * 4 + 2 * pr, 2), 0, :], O[:, :, 0:256]).then_inc(o_hi, 1)

            def qkv(part, s, i, first=False):
                g, m = G_QKV + 3 * s + part, C_QKV + 12 * s + 4 * part
                steps = ((soft_exp, soft_round, None, None), (None, None, weights_exp, weights_round),
                         (None, None, None, out_round))[part]
                if first and part < 2:
                    group(g, 0, m, 0, True)
                else:
                    for q in range(4):
                        if part == 0 and q == 0:
                            soft_abs(s - 1, i)
                        if steps[q] is not None and not first:
                            steps[q](s - 1, i)
                        split(m + NSPL + q, i * 3)
                if not (first and part < 2):
                    take_cross(g, i * 6, group_done(m, i * 3))
                if first and part == 0:
                    norm(3, columns=True)
                act.wait_ge(qk_scaled, i * 6 + (3 * s + part + 1))
                out = vv[s][:, :, 0, :] if part == 2 else qk[s][:, part, :, 0, :]
                copy(out, tv[:, :, :]).then_inc(qk_hi, 1)

            for s in range(2):
                for part in range(3):
                    qkv(part, s, 0, first=(s == 0))
            with act.Fori(1, 4) as i:
                for s in range(2):
                    for part in range(3):
                        qkv(part, s, i)
            ple_cross(G_PLE1, C_PLE1, 1, (0,))
            soft_abs(7, 0)
            ple_cross(G_PLE1, C_PLE1, 1, (1,))
            soft_exp(7, 0)
            ple_cross(G_PLE1, C_PLE1, 1, range(2, 4))
            soft_round(7, 0)
            ple_cross(G_PLE1, C_PLE1, 1, range(4, 8))
            weights_exp(7, 0)
            period(C_PLE1, 0, 2)
            weights_round(7, 0)
            period(C_PLE1 + 2, 0, 3)

            out_groups(G_OUT1, C_OUT1, H_OUT1, 4, XB, {
                4: lambda: out_round(7, 0)})
            mlp(G_MLP1, C_MLP1, 32, H_MLP1, 4, XA, 5, XB)
            gates(G_GATE1, C_GATE1, 8, H_GATE1, 5, 6, None)
            norm(6)

        @block.vector
        def _(dve):
            def split(m, it=0):
                if m < CHUNKS:
                    dve.wait_ge(hi_ready, it * 8 + (m + 1))
                    s = spl[:, m % NSPL, :, :, :]
                    dve.tensor_tensor(s[:, :, 1, :], raw[:, m % NRAW, :, :], s[:, :, 0, :].bitcast(F32),
                                      ALU.subtract).then_inc(lo_ready, 1)

            def split_rg(j):
                m = C_RG + j
                dve.wait_ge(hi_ready, m + 1)
                s = wrg[:, j, :, :, :]
                dve.tensor_tensor(s[:, :, 1, :], raw[:, m % NRAW, :, :], s[:, :, 0, :].bitcast(F32),
                                  ALU.subtract).then_inc(lo_ready, 1)

            def period(m, it, k=4):
                for q in range(k):
                    split(m + NSPL + q, it)

            def group(g, gi, m, it, first=False, later=0, steps={}):
                if not first:
                    period(m, it, 4 - later)
                else:
                    s = g % 2
                    for q in range(7 * s, 7 + s):
                        if q in steps:
                            steps[q]()
                        split(m - 4 * s + NSPL + q)
                take_sum(g, gi)

            def lo_of(X, t0, n, v):
                return dve.tensor_tensor(X[:, bass.ds(t0, n), 1, :], v, X[:, bass.ds(t0, n), 0, :].bitcast(F32),
                                         ALU.subtract)

            def take_sum(g, gi, out=None):
                b = 2 * (g % 2)
                dve.wait_ge(cross_copied, gi + (g + 1))
                dve.tensor_tensor(tv[:, :, :] if out is None else out, cross[:, :, :], ps[:, b:b + 2, 0:256],
                                  ALU.add).then_inc(sum_ready, 1)

            def scaled(g, gi, out, done):
                dve.wait_ge(sum_ready, gi + (g + 1))
                dve.tensor_tensor(out, tv[:, :, :], bcast(rB[:, :], 2), ALU.mult).then_inc(done, 1)

            def norm(n, columns=False):
                dve.wait_ge(root_ready, n + 1)
                r = dve.reciprocal(rB[:, :], rB[:, :])
                if columns:
                    r = dve.reciprocal(rC[:, :], rC[:, :])
                r.then_inc(rstd_ready, 1)
                dve.wait_ge(rstd_ready, n + 1)

            def clear(n):
                if n >= 1:
                    dve.wait_ge(stat_ready, n)
                dve.memset(nacc[:, :], 0.0).then_inc(nacc_clear, 1)
                dve.wait_ge(nacc_clear, n + 1)

            def fold(f):
                dve.wait_ge(sq_ready, f + 1)
                dve.tensor_tensor(tv[:, 0, :], tv[:, 0, :], tv[:, 1, :], ALU.add).then_inc(sq_folded, 1)
                dve.wait_ge(sq_folded, f * 2 + 1)
                dve.tensor_tensor(nacc[:, :], nacc[:, :], tv[:, 0, :], ALU.add).then_inc(sq_folded, 1)
                dve.wait_ge(sq_folded, f * 2 + 2)

            def res_los(f, t0, n, X):
                dve.wait_ge(res_hi, f + 1)
                for j in range(2):
                    r = dve.scalar_tensor_tensor(
                        out=X[:, bass.ds(t0 + j, 1), 1, :], in0=h[:, bass.ds(t0 + j, 1), :], scalar=gain(n, t0 + j),
                        in1=X[:, bass.ds(t0 + j, 1), 0, :].bitcast(F32), op0=ALU.mult, op1=ALU.subtract)
                r.then_inc(res_tiles, 1)

            def add_h(hidx, t0, first=False):
                if not first:
                    dve.wait_ge(res_ready, hidx - 7)
                ht = h[:, bass.ds(t0, 2), :]
                dve.tensor_tensor(ht, ht, tv[:, :, :], ALU.add).then_inc(res_ready, 1)
                dve.wait_ge(res_ready, hidx + 1)

            def residual(f, t0, n, X):
                fold(f)
                if X is not None:
                    res_los(f, t0, n, X)

            def up(g, gi, m, it, u, t0, hid, norm_n=None, first=False):
                group(g, gi, m, it, first)
                if norm_n is not None:
                    norm(norm_n)
                dve.wait_ge(sum_ready, gi + (g + 1))
                dve.scalar_tensor_tensor(out=tv[:, :, :], in0=tv[:, :, :], scalar=0.0, in1=bcast(rB[:, :], 2),
                                         op0=ALU.max, op1=ALU.mult).then_inc(up_relu, 1)
                dve.wait_ge(up_hi, u + 1)
                lo_of(hid, t0, 2, tv[:, :, :]).then_inc(up_tiles, 1)
                dve.wait_ge(up_tiles, u + 1)

            def down(g, gi, m, it, hidx, t0, first=False, later=0, steps={}):
                group(g, gi, m, it, first, later, steps)
                dve.wait_ge(sum_ready, gi + (g + 1))
                add_h(hidx, t0)

            def gate(g, gi, m, it, k, f, hidx, t0, n, X, norm_n=None, first=False):
                group(g, gi, m, it, first, 2)
                if norm_n is not None:
                    norm(norm_n)
                    clear(n)
                scaled(g, gi, tv[:, :, :], gate_scaled)
                if not first:
                    split(m + 2 + NSPL, it)
                dve.wait_ge(gate_sig, k + 1)
                dve.tensor_tensor(tv[:, :, :], tv[:, :, :], pp[:, bass.ds(t0, 2), :], ALU.mult).then_inc(gate_mul, 1)
                dve.wait_ge(gate_mul, k + 1)
                add_h(hidx, t0)
                if not first:
                    split(m + 3 + NSPL, it)
                residual(f, t0, n, X)

            def out_groups(g, m, hidx, f, n, X, first=None):
                clear(n)
                if first:
                    for s in range(2):
                        down(g + s, 0, m + 4 * s, 0, hidx + s, 2 * s, True, steps=first)
                        residual(f + s, 2 * s, n, X)
                with dve.Fori(1 if first else 0, 4) as i:
                    for s in range(2):
                        down(g + s, i * 2, m + 4 * s, i, i * 2 + (hidx + s), i * 4 + 2 * s, later=1)
                        split(m + 4 * s + 3 + NSPL, i)
                        residual(i * 2 + (f + s), i * 4 + 2 * s, n, X)

            def mlp(g, m, u, hidx, norm_in, hid, f_out, n, X):
                for s in range(2):
                    up(g + s, 0, m + 4 * s, 0, u + s, 2 * s, hid, norm_in if s == 0 else None, True)
                with dve.Fori(1, 4) as i:
                    for s in range(2):
                        up(g + s, i * 2, m + 4 * s, i, i * 2 + (u + s), i * 4 + 2 * s, hid)
                with dve.Fori(0, 4) as i:
                    for s in range(2):
                        down(g + 8 + s, i * 2, m + 32 + 4 * s, i, i * 2 + (hidx + s), i * 4 + 2 * s)
                with dve.Fori(1, 3) as f:
                    with dve.Fori(0, 4) as i:
                        for s in range(2):
                            up(g + s, f * 16 + i * 2, m + 4 * s, f * 8 + i, f * 8 + i * 2 + (u + s),
                               i * 4 + 2 * s, hid)
                    with dve.Fori(0, 4) as i:
                        for s in range(2):
                            down(g + 8 + s, f * 16 + i * 2, m + 32 + 4 * s, f * 8 + i,
                                 f * 8 + i * 2 + (hidx + s), i * 4 + 2 * s)
                g, m, u, hidx = g + 48, m + 192, u + 24, hidx + 24
                with dve.Fori(0, 4) as i:
                    for s in range(2):
                        up(g + s, i * 2, m + 4 * s, i, i * 2 + (u + s), i * 4 + 2 * s, hid)
                out_groups(g + 8, m + 32, hidx, f_out, n, X)

            def gates(g, m, k, f, hidx, norm_in, n, X):
                for s in range(2):
                    gate(g + s, 0, m + 4 * s, 0, k + s, f + s, hidx + s, 2 * s, n, X, norm_in if s == 0 else None, True)
                with dve.Fori(1, 3) as i:
                    for s in range(2):
                        gate(g + s, i * 2, m + 4 * s, i, i * 2 + (k + s), i * 2 + (f + s), i * 2 + (hidx + s),
                             i * 4 + 2 * s, n, X)
                for s in range(2):
                    gate(g + 6 + s, 0, m + 24 + 4 * s, 0, k + 6 + s, f + 6 + s, hidx + 6 + s, 12 + 2 * s, n, X)

            lam = params[:, LAMBDA:LAMBDA + 8]
            poly, e_, s2, s1 = (small[:, j, :] for j in range(4))
            steps = [0]

            def link(ins):
                steps[0] += 1
                ins.then_inc(lam_chain, 1)
                dve.wait_ge(lam_chain, steps[0])

            dve.wait_ge(par_landed, 16)
            dve.wait_ge(consts_ready, 2)
            dve.tensor_copy(ngtri[:, :], tl[:, 0, P:2 * P])
            dve.tensor_copy(ngone[:, :], tl[:, 0, 0:P])
            clear(0)
            for k in range(4):
                for f in (2 * k, 2 * k + 1):
                    res_los(f, 2 * f, 0, XA)
                split(2 * k)
                if k >= 2:
                    fold(k - 1)
                split(2 * k + 1)
                if k == 1:
                    fold(0)
            for f in range(3, 8):
                fold(f)
                if f < 5:
                    split_rg(f - 3)
                elif f < 7:
                    split(5 + f)

            def short_conv(c):
                for n in range(2 * CB):
                    k, j = n // 2, n % 2
                    dve.wait_ge(xr_step, c * 9 + (1 if n < 2 else n))
                    t = c * 2 + j
                    x, w = xrp[:, j, k:k + T].unsqueeze(1), par_col(t * CB + (CONV_B_W + k))
                    o = pp[:, bass.ds(t, 1), :]
                    if k == 0:
                        r = dve.tensor_scalar(o, x, w, par_col(t + CONV_B_B), ALU.mult, ALU.add)
                    else:
                        r = dve.scalar_tensor_tensor(out=o, in0=x, scalar=w, in1=o, op0=ALU.mult, op1=ALU.add)
                    r.then_inc(xr_step, 1)

            def x_value(c):
                take_sum(G_REC, c * 2)
                if isinstance(c, int) and c == 0:
                    norm(0)
                scaled(G_REC, c * 2, xrp[:, :, PAD_B:PAD_B + T], xr_step)
                short_conv(c)

            def x_rest(c):
                dve.wait_ge(xr_hi, c + 1)
                lo_of(XB, c * 2 + 8, 2, pp[:, bass.ds(c * 2, 2), :]).then_inc(xr_tiles, 1)

            def gate_value(c):
                take_sum(G_REC + 1, c * 2)
                scaled(G_REC + 1, c * 2, tv[:, :, :], gr_scaled)

            def rec_pair(c):
                period(C_REC, c)
                dve.wait_ge(gr_ready, c)
                x_value(c)
                for q in range(4, 6):
                    split(C_REC + NSPL + q, c)
                x_rest(c)
                for q in range(6, 8):
                    split(C_REC + NSPL + q, c)
                gate_value(c)

            for m in range(12, 15):
                split(m)
            x_value(0)
            split(15)
            gate_value(0)
            x_rest(0)
            for m in range(16, 18):
                split(m)
            dve.wait_ge(lam_exp, 1)
            link(dve.tensor_scalar(s2, e_, 2.0, None, ALU.add))
            link(dve.reciprocal(s2, s2))
            link(dve.tensor_tensor(s1, e_, s2, ALU.mult))
            link(dve.tensor_tensor(s2, s1, s1, ALU.mult))
            link(dve.tensor_scalar(poly, s2, 1.0 / 17, None, ALU.mult))
            for k in (15, 13, 11, 9, 7, 5, 3):
                link(dve.scalar_tensor_tensor(out=poly, in0=poly, scalar=1.0 / k, in1=s2, op0=ALU.add, op1=ALU.mult))
            link(dve.scalar_tensor_tensor(out=poly, in0=poly, scalar=1.0, in1=s1, op0=ALU.add, op1=ALU.mult))
            link(dve.tensor_scalar(s2, lam, 0.0, -1.0, ALU.min, ALU.mult))
            link(dve.scalar_tensor_tensor(out=s1, in0=poly, scalar=2.0, in1=s2, op0=ALU.mult, op1=ALU.add))
            link(dve.tensor_scalar(lamc[:, :], s1, 8.0, None, ALU.mult))
            link(dve.tensor_scalar(nlamc[:, :], s1, -8.0, None, ALU.mult))
            assert steps[0] == LAM_STEPS
            with dve.Fori(1, 4) as c:
                rec_pair(c)

            def glu_value(c):
                take_sum(G_GLU, c * 2)
                scaled(G_GLU, c * 2, glu[:, bass.ds(c * 2, 2), PAD_A:], glu_val)
                dve.wait_ge(glu_val, c + 1)

            def glu_gate(c, meanwhile=None):
                take_sum(G_GLU + 1, c * 2)
                scaled(G_GLU + 1, c * 2, tv[:, :, :], glu_scaled)
                if meanwhile is not None:
                    meanwhile()
                dve.wait_ge(glu_sig, c + 1)
                gl = glu[:, bass.ds(c * 2, 2), PAD_A:]
                dve.tensor_tensor(gl, gl, tv[:, :, :], ALU.mult).then_inc(glu_ready, 1)
                dve.wait_ge(glu_ready, c + 1)

            r_, i_ = rg[:, :, 0, :], rg[:, :, 1, :]
            dve.wait_ge(gr_ready, 4)
            dve.wait_ge(rg_act, 4)
            dve.tensor_tensor(i_, i_, pp[:, 0:8, :], ALU.mult).then_inc(rg_vec, 1)
            split(C_GLU + NSPL)
            dve.wait_ge(rg_act, 6)
            dve.tensor_tensor(r_, dec[:, :, :], dec[:, :, :], ALU.mult).then_inc(rg_vec, 1)
            split(C_GLU + NSPL + 1)
            dve.wait_ge(rg_vec, 2)
            dve.scalar_tensor_tensor(out=mlt[:, :, :], in0=r_, scalar=1.0, in1=mlt[:, :, :],
                                     op0=ALU.add, op1=ALU.mult).then_inc(rg_vec, 1)
            split(C_GLU + NSPL + 2)
            split(C_GLU + NSPL + 3)
            glu_value(0)
            split(C_GLU + 4 + NSPL)
            dve.wait_ge(rg_act, 7)
            dve.tensor_tensor(i_, i_, mlt[:, :, :], ALU.mult).then_inc(rg_vec, 1)
            split(C_GLU + 4 + NSPL + 1)
            dve.wait_ge(rg_vec, 4)
            for t in range(8):
                r = dve.tensor_tensor_scan(rg[:, t, 0, :], dec[:, t, :], rg[:, t, 1, :], 0.0, ALU.mult, ALU.add)
            r.then_inc(rg_vec, 1)
            split(C_GLU + 4 + NSPL + 2)
            split(C_GLU + 4 + NSPL + 3)
            glu_gate(0)

            def conv(pair, base, q):
                first, y2t, second = y[:, bass.ds(pair * 2, 1), :], y2[:, :].unsqueeze(1), y[:, bass.ds(pair * 2 + 1, 1), :]

                def step(n):
                    return n + min(n // 4, CA_VE)

                if q == 0:
                    dve.wait_ge(glu_ready, pair + 1)
                for n in range(4 * q, 4 * q + 4):
                    o = (first, y2t)[n % 2]
                    if n < CA:
                        x, w = glu[:, bass.ds(pair * 2, 1), n:n + T], par_col(pair * (2 * CA) + (CONV_A_W + n))
                    if n >= 2:
                        dve.wait_ge(conv_step, base + step(n - 2 if n < CA else n - 1) + 1)
                    if n == 0:
                        r = dve.tensor_scalar(o, x, w, par_col(pair * 2 + CONV_A_B), ALU.mult, ALU.add)
                    elif n == 1:
                        r = dve.tensor_scalar(o, x, w, None, ALU.mult)
                    elif n < CA:
                        r = dve.scalar_tensor_tensor(out=o, in0=x, scalar=w, in1=o, op0=ALU.mult, op1=ALU.add)
                    else:
                        r = dve.tensor_tensor(first, first, y2t, ALU.add)
                    r.then_inc(conv_step, 1)
                if q < CA_VE:
                    k = CA_PE + q
                    x, w = glu[:, bass.ds(pair * 2 + 1, 1), k:k + T], par_col(pair * (2 * CA) + (CONV_A_W + CA + k))
                    if q == 0:
                        r = dve.tensor_scalar(second, x, w, par_col(pair * 2 + (1 + CONV_A_B)), ALU.mult, ALU.add)
                    else:
                        dve.wait_ge(conv_step, base + 5 * q)
                        r = dve.scalar_tensor_tensor(out=second, in0=x, scalar=w, in1=second, op0=ALU.mult, op1=ALU.add)
                    r.then_inc(conv_step, 1)
                if q == 7:
                    dve.wait_ge(conv_step, base + CSTEPS)

            def conv_end(pair):
                dve.wait_ge(dg_used, pair * CA_PE + CA_PE)
                second = y[:, bass.ds(pair * 2 + 1, 1), :]
                dve.tensor_tensor(second, second, O[:, 0:1, 0:256], ALU.add).then_inc(conv_taken, 1)

            def glu_pair(c):
                for q in range(8):
                    conv(c - 1, c * CSTEPS - CSTEPS, q)
                    split(C_GLU + NSPL + q, c)
                    if q == 3:
                        glu_value(c)
                    if isinstance(c, int) and q == 2:
                        dve.wait_ge(rg_vec, 5)
                        dve.tensor_tensor(pp[:, 0:8, :], r_, pp[:, 8:16, :], ALU.mult).then_inc(rg_vec, 1)
                    if isinstance(c, int) and q == 6:
                        dve.wait_ge(rg_act, 8)
                        lo_of(XB, 8, 8, pp[:, 0:8, :]).then_inc(yb_tiles, 1)
                glu_gate(c, lambda: conv_end(c - 1))

            glu_pair(1)
            with dve.Fori(2, 4) as c:
                glu_pair(c)

            def ple_sums(g, units):
                for u in units:
                    take_sum(g + u, 0, pp[:, 2 * u:2 * u + 2, :])

            for s in range(NG):
                for q in range(2):
                    if s < 4:
                        conv(3, 3 * CSTEPS, 2 * s + q)
                    split(C_OUTB + 2 * s + q + NSPL)
                    if s == 7 and q == 1:
                        dve.wait_ge(ln_act, 2)
                        dve.reciprocal(nacc[:, :], nacc[:, :]).then_inc(ln_vec, 1)
                take_sum(G_OUTB + s, 0)
                dve.wait_ge(sum_ready, G_OUTB + s + 1)
                add_h(H_OUTB + s, 2 * s, first=True)
                if s == 3:
                    conv_end(3)
                    dve.wait_ge(conv_taken, 4)
                    dve.tensor_reduce(nacc[:, :], y[:, :, :].rearrange("p t n -> p n t"), AX_X,
                                      ALU.add).then_inc(ln_part, 1)
                elif s == 4:
                    dve.wait_ge(ln_stat, 1)
                    dve.tensor_tensor(y[:, :, :], y[:, :, :], bcast(Z[:, 0, 0:256], 8), ALU.subtract).then_inc(ln_vec, 1)
                elif s == 5:
                    dve.wait_ge(ln_act, 1)
                    dve.tensor_reduce(nacc[:, :], dec[:, :, :].rearrange("p t n -> p n t"), AX_X,
                                      ALU.add).then_inc(ln_part, 1)
            dve.wait_ge(ln_vec, 2)
            for k in range(2):
                yk = y[:, 4 * k:4 * k + 4, :]
                dve.tensor_tensor(yk, yk, bcast(nacc[:, :], 4), ALU.mult).then_inc(ln_vec, 1)
                ple_sums(G_PLE0, (k,))
            ple_sums(G_PLE0, (2,))
            for k in range(2):
                dve.wait_ge(ln_act, 4 + 2 * k)
                lo_of(XB, 4 * k, 4, y[:, 4 * k:4 * k + 4, :]).then_inc(ya_tiles, 1)
                ple_sums(G_PLE0, range(3, 6) if k == 0 else range(6, 8))
            period(C_PLE0, 0, 5)
            dve.wait_ge(ln_vec, 4)
            clear(1)
            with dve.Fori(0, 2) as i:
                for s in range(4):
                    take_sum(G_OUTA + s, i * 4)
                    split(C_OUTA + 2 * s + NSPL, i)
                    dve.wait_ge(sum_ready, i * 4 + (G_OUTA + s + 1))
                    add_h(i * 4 + (H_OUTA + s), i * 8 + 2 * s)
                    split(C_OUTA + 2 * s + 1 + NSPL, i)
                    residual(i * 4 + (8 + s), i * 8 + 2 * s, 1, XA)
            mlp(G_MLP0, C_MLP0, 0, H_MLP0, 1, XB, 16, 2, XA)
            gates(G_GATE0, C_GATE0, 0, 24, H_GATE0, 2, 3, XB)

            z = Z[:, :, 0:384]

            def keep_earlier_keys(done):
                d = tl[:, :, :].rearrange("p e (b n) -> p e b n", n=P)[:, :, 0:3:2, :]
                dve.tensor_tensor(d, d, mask[:, :].unsqueeze(1).unsqueeze(1).broadcast_to([P, 2, 2, P]),
                                  ALU.mult).then_inc(done, 1)

            def soft_sum(pr, i):
                dve.wait_ge(z_log, i * 2 + (pr + 1))
                dve.scalar_tensor_tensor(out=tl[:, :, :], in0=z, scalar=0.0, in1=te[:, :, :],
                                         op0=ALU.max, op1=ALU.add).then_inc(soft_raw, 1)
                dve.wait_ge(soft_raw, i * 2 + (pr + 1))
                keep_earlier_keys(soft_ready)

            def soft_rest(pr, i):
                dve.wait_ge(soft_hi, i * 2 + (pr + 1))
                dve.tensor_tensor(ws[:, :, 1, :], tl[:, :, :], ws[:, :, 0, :].bitcast(F32),
                                  ALU.subtract).then_inc(soft_split, 1)

            def weights_cut(pr, i):
                dve.wait_ge(logw_ready, i * 2 + (pr + 1))
                dve.tensor_scalar(tl[:, :, :], z, 0.0, None, ALU.min).then_inc(logw_cut, 1)

            def weights_mask(pr, i):
                dve.wait_ge(w_exp, i * 2 + (pr + 1))
                keep_earlier_keys(w_ready)

            def weights_rest(pr, i):
                dve.wait_ge(w_hi, i * 2 + (pr + 1))
                dve.tensor_tensor(ws[:, :, 1, :], tl[:, :, :], ws[:, :, 0, :].bitcast(F32),
                                  ALU.subtract).then_inc(w_split, 1)

            def out_rest(pr, i):
                dve.wait_ge(o_hi, i * 2 + (pr + 1))
                lo_of(XA, i * 4 + 2 * pr, 2, O[:, :, 0:256]).then_inc(att_tiles, 1)

            def qkv(part, s, i, first=False):
                g, m = G_QKV + 3 * s + part, C_QKV + 12 * s + 4 * part
                steps = ((soft_sum, soft_rest, None, None), (None, None, weights_cut, weights_mask),
                         (None, None, None, out_rest))[part]
                if first and part < 2:
                    group(g, 0, m, 0, True)
                else:
                    for q in range(4):
                        if steps[q] is not None and not first:
                            steps[q](s - 1, i)
                        split(m + NSPL + q, i * 3)
                    if part == 1:
                        weights_rest(s - 1, i)
                    take_sum(g, i * 6)
                if first and part == 0:
                    norm(3, columns=True)
                dve.wait_ge(sum_ready, i * 6 + (g + 1))
                if part == 0:
                    dve.scalar_tensor_tensor(out=tv[:, :, :], in0=tv[:, :, :], scalar=float(DH) ** -0.5,
                                             in1=bcast(rB[:, :], 2), op0=ALU.mult, op1=ALU.mult).then_inc(qk_scaled, 1)
                elif part == 1:
                    dve.tensor_tensor(tv[:, :, :], tv[:, :, :], bcast(rB[:, :], 2), ALU.mult).then_inc(qk_scaled, 1)
                else:
                    for t in range(2):
                        r = dve.tensor_scalar(tv[:, t, :], tv[:, t, :], rC[:, t:t + 1], None, ALU.mult)
                    r.then_inc(qk_scaled, 1)
                dve.wait_ge(qk_hi, i * 6 + (3 * s + part + 1))
                X = vv[s] if part == 2 else qk[s][:, part, :, :, :]
                lo_of(X, 0, 2, tv[:, :, :]).then_inc(qk_split, 1)
                dve.wait_ge(qk_split, i * 6 + (3 * s + part + 1))

            for s in range(2):
                for part in range(3):
                    qkv(part, s, 0, first=(s == 0))
            with dve.Fori(1, 4) as i:
                for s in range(2):
                    for part in range(3):
                        qkv(part, s, i)
            ple_sums(G_PLE1, range(2))
            soft_sum(7, 0)
            ple_sums(G_PLE1, range(2, 4))
            soft_rest(7, 0)
            ple_sums(G_PLE1, range(4, 8))
            weights_cut(7, 0)
            weights_mask(7, 0)
            period(C_PLE1, 0, 2)
            weights_rest(7, 0)
            period(C_PLE1 + 2, 0, 3)

            out_groups(G_OUT1, C_OUT1, H_OUT1, 32, 4, XB, {
                4: lambda: out_rest(7, 0)})
            mlp(G_MLP1, C_MLP1, 32, H_MLP1, 4, XA, 40, 5, XB)
            gates(G_GATE1, C_GATE1, 8, 48, H_GATE1, 5, 6, None)
            norm(6)
            dve.wait_ge(out_scaled, 8)
            for q in range(4):
                hq = h[:, 4 * q:4 * q + 4, :]
                dve.tensor_tensor(hq, hq, bcast(rB[:, :], 4), ALU.mult).then_inc(out_ready, 1)


def _columns(a, n):
    import numpy as np
    return np.asarray(a).reshape(-1, n, P).transpose(2, 0, 1).reshape(P, -1)


def kernel(x, p, norm_mix_g, norm_mlp_g, norm_ple_g, norm_f_g, w_in_rec, conv_a_w, conv_a_b, ln_a_g, ln_a_b,
           conv_b_w, conv_b_b, w_rg_a, b_rg_a, w_rg_x, b_rg_x, rg_lambda, w_out_rec, w_qkv, w_o_attn,
           w_mlp_up, w_mlp_down, w_ple_proj, w_ple_gate):
    import numpy as np
    import concourse.bacc as bacc
    from concourse.bass_utils import run_bass_kernel_spmd

    norms = [norm_mix_g[0], norm_mlp_g[0], norm_ple_g[0], norm_mix_g[1], norm_mlp_g[1], norm_ple_g[1], norm_f_g]
    taps_a = np.asarray(conv_a_w)[0].reshape(CA, 8, P).transpose(2, 1, 0).reshape(P, 8 * CA)
    taps_b = np.asarray(conv_b_w)[0].reshape(CB, 8, P).transpose(2, 1, 0).reshape(P, 8 * CB)
    par = np.concatenate([_columns(g, NT) for g in norms] + [taps_a] + [_columns(v, 8) for v in (conv_a_b, ln_a_g, ln_a_b)]
                         + [taps_b] + [_columns(v, 8) for v in (conv_b_b, b_rg_a, b_rg_x, rg_lambda)], axis=1)
    ins = {
        "xT": np.asarray(x)[0].T, "pT": np.asarray(p)[:, 0].transpose(0, 2, 1), "par": par,
        "w_in": w_in_rec, "w_rg_a": w_rg_a, "w_rg_x": w_rg_x, "w_out": w_out_rec, "w_qkv": w_qkv, "w_o": w_o_attn,
        "w_up": w_mlp_up, "w_down": w_mlp_down, "w_proj": w_ple_proj, "w_gate": w_ple_gate,
    }
    ins = {k: np.ascontiguousarray(v) for k, v in ins.items()}
    nc = bacc.Bacc("TRN2", target_bir_lowering=False, num_devices=1)
    aps = {k: nc.dram_tensor(f"in_{k}", v.shape, mybir.dt.from_np(v.dtype), kind="ExternalInput").ap()
           for k, v in ins.items()}
    out = nc.dram_tensor("outT", (D, T), F32, kind="ExternalOutput").ap()
    trunk(nc, outT=out, **aps)
    r = run_bass_kernel_spmd(nc, [{f"in_{k}": v for k, v in ins.items()}], core_ids=[0])
    return np.ascontiguousarray(r.results[0]["outT"].T)[None]
```
